# Optimizing a Trainium2 kernel written in Bass

```python
import math
import jax
import jax.numpy as jnp
from jax import lax
import numpy as np

D_MODEL = 1024
BATCH = 1
SEQ = 256
DEPTH = 2

N_EVEN = (DEPTH + 1) // 2
N_ODD = DEPTH // 2
NORM_EPS = 1e-5

SSD_HEADS = 16
SSD_HEAD_DIM = 64
SSD_INNER = SSD_HEADS * SSD_HEAD_DIM
SSD_GROUPS = 2
SSD_STATE = 128
SSD_CONV = 4
SSD_CHUNK = 128
SSD_CONV_DIM = SSD_INNER + 2 * SSD_GROUPS * SSD_STATE
DT_MIN = 1e-3
DT_MAX = 1e-1

MOBA_HEADS = 8
MOBA_HEAD_DIM = 128
MOBA_INNER = MOBA_HEADS * MOBA_HEAD_DIM
MOBA_BLOCK = 256
MOBA_TOPK = 3
MOBA_QCHUNK = 32

Z_END = SSD_INNER
XBC_END = Z_END + SSD_CONV_DIM
DT_END = XBC_END + SSD_HEADS
Q_END = DT_END + MOBA_INNER
K_END = Q_END + MOBA_INNER
V_END = K_END + MOBA_INNER
EVEN_IN = V_END + MOBA_INNER
EVEN_MIX = SSD_INNER + MOBA_INNER

DIL_HEADS = 16
DIL_HEAD_DIM = 128
DIL_INNER = DIL_HEADS * DIL_HEAD_DIM
DIL_PATTERNS = ((128, 1), (512, 4), (2048, 16))
DIL_QBLOCK = 128
ODD_IN = 4 * DIL_INNER

kernel_name = 'hybrid_ssd_moba_dilated'

def rmsnorm(x, g):
    xf = x.astype(jnp.float32)
    y = xf * lax.rsqrt(jnp.mean(xf * xf, axis=-1, keepdims=True) + NORM_EPS)
    return (y * g.astype(jnp.float32)).astype(x.dtype)

def causal_dwconv(u, w, b):
    c = u.shape[-1]
    y = lax.conv_general_dilated(u, w[:, None, :].astype(u.dtype), window_strides=(1,),
                                 padding=[(w.shape[0] - 1, 0)],
                                 dimension_numbers=('NWC', 'WIO', 'NWC'),
                                 feature_group_count=c)
    return y + b.astype(u.dtype)

def ssd_chunked(x, dt, a, bmat, cmat, d_skip):
    f32 = jnp.float32
    bsz, s, h, p = x.shape
    g, n = bmat.shape[2], bmat.shape[3]
    l = SSD_CHUNK
    nc = s // l
    xf = x.astype(f32)
    dtf = dt.astype(f32)
    bh = jnp.repeat(bmat.astype(f32), h // g, axis=2).reshape(bsz, nc, l, h, n)
    ch = jnp.repeat(cmat.astype(f32), h // g, axis=2).reshape(bsz, nc, l, h, n)
    xc = (xf * dtf[..., None]).reshape(bsz, nc, l, h, p)
    ac = (dtf * a.astype(f32)).reshape(bsz, nc, l, h).transpose(0, 3, 1, 2)
    a_cum = jnp.cumsum(ac, axis=-1)
    seg = a_cum[..., :, None] - a_cum[..., None, :]
    causal = jnp.tril(jnp.ones((l, l), dtype=bool))
    lmat = jnp.exp(jnp.where(causal, seg, -jnp.inf))
    scores = jnp.einsum('bclhn,bcshn->bhcls', ch, bh)
    y_diag = jnp.einsum('bhcls,bcshp->bclhp', scores * lmat, xc)
    decay_states = jnp.exp(a_cum[..., -1:] - a_cum)
    states = jnp.einsum('bclhn,bhcl,bclhp->bchpn', bh, decay_states, xc)
    chunk_decay = jnp.exp(a_cum[..., -1])

    def step(carry, inp):
        st, dec = inp
        return carry * dec[..., None, None] + st, carry

    init = jnp.zeros((bsz, h, p, n), f32)
    _, prev = lax.scan(step, init, (states.transpose(1, 0, 2, 3, 4), chunk_decay.transpose(2, 0, 1)))
    prev = prev.transpose(1, 0, 2, 3, 4)
    y_off = jnp.einsum('bclhn,bchpn,bhcl->bclhp', ch, prev, jnp.exp(a_cum))
    y = (y_diag + y_off).reshape(bsz, s, h, p) + xf * d_skip.astype(f32)[:, None]
    return y.astype(x.dtype)

def gated_group_rmsnorm(y, z, g):
    bsz, s, _ = y.shape
    u = (y * jax.nn.silu(z)).astype(jnp.float32).reshape(bsz, s, SSD_GROUPS, -1)
    u = u * lax.rsqrt(jnp.mean(u * u, axis=-1, keepdims=True) + NORM_EPS)
    return (u.reshape(bsz, s, -1) * g.astype(jnp.float32)).astype(y.dtype)

def moba_attention(q, k, v):
    f32 = jnp.float32
    bsz, h, s, d = q.shape
    blk = MOBA_BLOCK
    nb = -(-s // blk)
    pad = nb * blk - s
    kb = jnp.pad(k, ((0, 0), (0, 0), (0, pad), (0, 0))).reshape(bsz, h, nb, blk, d)
    vb = jnp.pad(v, ((0, 0), (0, 0), (0, pad), (0, 0))).reshape(bsz, h, nb, blk, d)
    scale = d ** -0.5
    kmean = jnp.mean(kb.astype(f32), axis=3)
    gate = jnp.einsum('bhsd,bhnd->bhsn', q.astype(f32), kmean)
    qblk = jnp.arange(s) // blk
    past = jnp.arange(nb)[None, :] < qblk[:, None]
    gate = jnp.where(past, gate, -jnp.inf)
    k_sel = max(1, min(MOBA_TOPK, nb - 1))
    _, sel = lax.top_k(gate, k_sel)
    valid = sel < qblk[:, None]
    qc = MOBA_QCHUNK
    nq = s // qc
    qs = q.reshape(bsz, h, nq, qc, d).transpose(2, 0, 1, 3, 4)
    sels = sel.reshape(bsz, h, nq, qc, k_sel).transpose(2, 0, 1, 3, 4)
    valids = valid.reshape(bsz, h, nq, qc, k_sel).transpose(2, 0, 1, 3, 4)
    poss = jnp.arange(s, dtype=jnp.int32).reshape(nq, qc)
    bi = jnp.arange(bsz)[:, None, None, None]
    hi = jnp.arange(h)[None, :, None, None]
    nsel = k_sel * blk

    def one_chunk(args):
        qq, sc, vc, pos = args
        own = pos[0] // blk
        k_own = lax.dynamic_index_in_dim(kb, own, axis=2, keepdims=False)
        v_own = lax.dynamic_index_in_dim(vb, own, axis=2, keepdims=False)
        k_g = kb[bi, hi, sc]
        v_g = vb[bi, hi, sc]
        s_sel = jnp.einsum('bhqd,bhqjkd->bhqjk', qq, k_g).astype(f32) * scale
        s_sel = jnp.where(vc[..., None], s_sel, -jnp.inf)
        key_pos = own * blk + jnp.arange(blk)
        s_own = jnp.einsum('bhqd,bhkd->bhqk', qq, k_own).astype(f32) * scale
        s_own = jnp.where(key_pos[None, :] <= pos[:, None], s_own, -jnp.inf)
        logits = jnp.concatenate([s_sel.reshape(bsz, h, qc, nsel), s_own], axis=-1)
        pr = jax.nn.softmax(logits, axis=-1)
        p_sel = pr[..., :nsel].reshape(bsz, h, qc, k_sel, blk).astype(v.dtype)
        p_own = pr[..., nsel:].astype(v.dtype)
        return (jnp.einsum('bhqjk,bhqjkd->bhqd', p_sel, v_g)
                + jnp.einsum('bhqk,bhkd->bhqd', p_own, v_own))

    out = lax.map(one_chunk, (qs, sels, valids, poss))
    return out.transpose(1, 0, 3, 2, 4).reshape(bsz, s, h * d)

def dilated_attention(q, k, v):
    f32 = jnp.float32
    bsz, h, s, d = q.shape
    qb_len = DIL_QBLOCK
    scale = d ** -0.5
    outs, lses = [], []
    for window, r in DIL_PATTERNS:
        span = window // r
        L = -(-s // r)
        Lp = -(-L // qb_len) * qb_len
        nblk = Lp // qb_len

        def to_phase(t):
            t = jnp.pad(t, ((0, 0), (0, 0), (0, L * r - s), (0, 0)))
            t = t.reshape(bsz, h, L, r, d).transpose(0, 1, 3, 2, 4)
            t = jnp.pad(t, ((0, 0), (0, 0), (0, 0), (0, Lp - L), (0, 0)))
            return t.reshape(bsz, h, r, nblk, qb_len, d)

        def with_prev(t):
            prev = jnp.pad(t, ((0, 0), (0, 0), (0, 0), (1, 0), (0, 0), (0, 0)))[:, :, :, :-1]
            return jnp.concatenate([prev, t], axis=4)

        qp = to_phase(q)
        kw = with_prev(to_phase(k))
        vw = with_prev(to_phase(v))
        logits = jnp.einsum('bhrnqd,bhrnkd->bhrnqk', qp, kw).astype(f32) * scale
        qi = jnp.arange(qb_len)[:, None]
        kj = jnp.arange(2 * qb_len)[None, :]
        m = qi + qb_len - kj
        bidx = jnp.arange(nblk)[:, None, None]
        ok = (m >= 0) & (m <= span) & (bidx * qb_len + kj - qb_len >= 0)
        logits = jnp.where(ok, logits, -jnp.inf)
        lse = jax.nn.logsumexp(logits, axis=-1)
        pr = jnp.exp(logits - lse[..., None]).astype(v.dtype)
        o = jnp.einsum('bhrnqk,bhrnkd->bhrnqd', pr, vw)
        o = o.reshape(bsz, h, r, Lp, d)[:, :, :, :L].transpose(0, 1, 3, 2, 4)
        o = o.reshape(bsz, h, L * r, d)[:, :, :s]
        lse = lse.reshape(bsz, h, r, Lp)[..., :L].transpose(0, 1, 3, 2).reshape(bsz, h, L * r)[..., :s]
        outs.append(o)
        lses.append(lse)
    wts = jax.nn.softmax(jnp.stack(lses, axis=0), axis=0)
    out = jnp.einsum('pbhs,pbhsd->bhsd', wts, jnp.stack(outs, axis=0).astype(f32))
    return out.astype(q.dtype)

def even_mixer(hn, w_in, conv_w, conv_b, dt_bias, a_log, d_skip, ssd_norm, w_out):
    bsz, s, _ = hn.shape
    proj = hn @ w_in
    z, xbc, dt_raw, q, k, v, gate = jnp.split(proj, [Z_END, XBC_END, DT_END, Q_END, K_END, V_END], axis=-1)
    xbc = jax.nn.silu(causal_dwconv(xbc, conv_w, conv_b))
    xs, bm, cm = jnp.split(xbc, [SSD_INNER, SSD_INNER + SSD_GROUPS * SSD_STATE], axis=-1)
    xs = xs.reshape(bsz, s, SSD_HEADS, SSD_HEAD_DIM)
    bm = bm.reshape(bsz, s, SSD_GROUPS, SSD_STATE)
    cm = cm.reshape(bsz, s, SSD_GROUPS, SSD_STATE)
    dt = jax.nn.softplus((dt_raw + dt_bias).astype(jnp.float32))
    a = -jnp.exp(a_log.astype(jnp.float32))
    y = ssd_chunked(xs, dt, a, bm, cm, d_skip).reshape(bsz, s, SSD_INNER)
    y_ssd = gated_group_rmsnorm(y, z, ssd_norm)
    def heads(t):
        return t.reshape(bsz, s, MOBA_HEADS, MOBA_HEAD_DIM).transpose(0, 2, 1, 3)
    o = moba_attention(heads(q), heads(k), heads(v))
    y_moba = o * jax.nn.silu(gate)
    return jnp.concatenate([y_ssd, y_moba], axis=-1) @ w_out

def odd_mixer(hn, w_in, w_out):
    bsz, s, _ = hn.shape
    proj = hn @ w_in
    q, k, v, gate = jnp.split(proj, [DIL_INNER, 2 * DIL_INNER, 3 * DIL_INNER], axis=-1)
    def heads(t):
        return t.reshape(bsz, s, DIL_HEADS, DIL_HEAD_DIM).transpose(0, 2, 1, 3)
    o = dilated_attention(heads(q), heads(k), heads(v))
    o = o.transpose(0, 2, 1, 3).reshape(bsz, s, DIL_INNER)
    return (o * jax.nn.silu(gate)) @ w_out

def setup_inputs(seed: int = 0) -> dict:
    key = jax.random.key(seed)
    ks = jax.random.split(key, 16)
    f32 = jnp.float32

    def nrm(k, shape, scale):
        return jax.random.normal(k, shape, f32) * scale

    x = nrm(ks[0], (BATCH, SEQ, D_MODEL), 1.0)
    even_norm = 1.0 + nrm(ks[1], (N_EVEN, D_MODEL), 0.02)
    even_w_in = nrm(ks[2], (N_EVEN, D_MODEL, EVEN_IN), D_MODEL ** -0.5)
    ssd_conv_w = nrm(ks[3], (N_EVEN, SSD_CONV, SSD_CONV_DIM), SSD_CONV ** -0.5)
    ssd_conv_b = nrm(ks[4], (N_EVEN, SSD_CONV_DIM), 0.02)
    dt0 = jnp.exp(jax.random.uniform(ks[5], (N_EVEN, SSD_HEADS), f32, math.log(DT_MIN), math.log(DT_MAX)))
    ssd_dt_bias = dt0 + jnp.log(-jnp.expm1(-dt0))
    ssd_a_log = jnp.log(jax.random.uniform(ks[6], (N_EVEN, SSD_HEADS), f32, 1.0, 16.0))
    ssd_d = 1.0 + nrm(ks[7], (N_EVEN, SSD_HEADS), 0.02)
    ssd_norm = 1.0 + nrm(ks[8], (N_EVEN, SSD_INNER), 0.02)
    even_w_out = nrm(ks[9], (N_EVEN, EVEN_MIX, D_MODEL), EVEN_MIX ** -0.5)
    odd_norm = 1.0 + nrm(ks[10], (N_ODD, D_MODEL), 0.02)
    odd_w_in = nrm(ks[11], (N_ODD, D_MODEL, ODD_IN), D_MODEL ** -0.5)
    odd_w_out = nrm(ks[12], (N_ODD, DIL_INNER, D_MODEL), DIL_INNER ** -0.5)
    final_norm = 1.0 + nrm(ks[13], (D_MODEL,), 0.02)
    return {'x': x, 'even_norm': even_norm, 'even_w_in': even_w_in, 'ssd_conv_w': ssd_conv_w,
            'ssd_conv_b': ssd_conv_b, 'ssd_dt_bias': ssd_dt_bias, 'ssd_a_log': ssd_a_log,
            'ssd_d': ssd_d, 'ssd_norm': ssd_norm, 'even_w_out': even_w_out,
            'odd_norm': odd_norm, 'odd_w_in': odd_w_in, 'odd_w_out': odd_w_out,
            'final_norm': final_norm}

def reference(x, even_norm, even_w_in, ssd_conv_w, ssd_conv_b, ssd_dt_bias, ssd_a_log, ssd_d,
              ssd_norm, even_w_out, odd_norm, odd_w_in, odd_w_out, final_norm):
    for layer in range(DEPTH):
        i = layer // 2
        if layer % 2 == 0:
            hn = rmsnorm(x, even_norm[i])
            x = x + even_mixer(hn, even_w_in[i], ssd_conv_w[i], ssd_conv_b[i], ssd_dt_bias[i],
                               ssd_a_log[i], ssd_d[i], ssd_norm[i], even_w_out[i])
        else:
            hn = rmsnorm(x, odd_norm[i])
            x = x + odd_mixer(hn, odd_w_in[i], odd_w_out[i])
    return rmsnorm(x, final_norm)


_drawn_inputs = setup_inputs


def setup_inputs(seed=0):
    import zlib

    import numpy as np

    out = dict(_drawn_inputs(seed))
    spreads = {}
    factors = {'even_norm': 2.849,
     'ssd_conv_b': 3.601,
     'ssd_d': 24.595,
     'ssd_norm': 5.301,
     'odd_norm': 8.0,
     'final_norm': 7.501}
    for name, (base, spread) in spreads.items():
        noise = np.random.default_rng([zlib.crc32(name.encode()), seed]).standard_normal(out[name].shape)
        drawn = base * np.exp(spread * noise) if base else spread * noise
        out[name] = jnp.asarray(drawn.astype(out[name].dtype))
    for name, factor in factors.items():
        out[name] = (out[name] * factor).astype(out[name].dtype)
    return out
```

```python
from contextlib import ExitStack

import concourse.bass as bass
from concourse import mybir

P = 128
D_MODEL, SEQ = 1024, 256
KT = D_MODEL // P
NT = SEQ // P
SSD_HEADS, SSD_INNER, SSD_STATE, SSD_GROUPS, CONV = 16, 1024, 128, 2, 4
MOBA_HEADS, DIL_HEADS, HD = 8, 16, 128
IT0, IT1 = MOBA_HEADS // 2, DIL_HEADS // 2
CW = 256
CF = KT * CW
OUT_CHUNKS = 2048 // CW
X, Z, Q0, K0, V0, G0, PER0 = 0, 1, 2, 3, 4, 5, 6
Q1, K1, V1, G1, PER1 = 0, 1, 2, 3, 4
N_PRE = 2
N_OUT0 = N_PRE + PER0 * IT0
N_L1 = N_OUT0 + OUT_CHUNKS
N_OUT1 = N_L1 + PER1 * IT1
N_ALL = N_OUT1 + OUT_CHUNKS
RING0, RING1 = 3, 4
SLOTS1 = [3] + [(N_L1 - RING0 + j) % RING0 for j in range(RING0)]
USED1 = {s: len(range(s, N_L1, RING0)) if s < RING0 else 0 for s in range(RING1)}
OUT_ORDER0 = [8, 10, 12, 0, 2, 4, 6, 14]
ACC_BANKS = [2, 3, 0, 1]
HEADS_PER_IT = SSD_HEADS // IT0
CPAR = 2 * (CONV + 1) + 2
BLK = 3 * P
SCALE = float(HD) ** -0.5
EPS = 1e-5
BIG = 1e30

F32, F32R = mybir.dt.float32, mybir.dt.float32r
ALU, ACT = mybir.AluOpType, mybir.ActivationFunctionType

C_ID, C_TRI, C_ONE, C_TRI2, C_M0 = 0, P, 2 * P, 3 * P, 4 * P
C_M1 = C_M0 + BLK
C_INV = C_M1 + BLK
N_CONST = C_INV + 2
MARKS0, MARKS1 = 12, 2
P_CONV, P_EVEN = 0, (IT0 + 2) * CPAR
P_ODD, P_FINAL, P_SSD = P_EVEN + KT, P_EVEN + 2 * KT, P_EVEN + 3 * KT
P_DTB, P_ALOG = P_EVEN + 4 * KT, P_EVEN + 4 * KT + NT * SSD_HEADS
N_PAR = P_ALOG + NT * SSD_HEADS


class Chunk:

    def __init__(self, layer, i, j):
        if layer == 0 and isinstance(i, int) and N_PRE + PER0 * i + j >= N_L1:
            layer, j, i = 1, N_PRE + PER0 * i + j - N_L1, 0
        self.layer = layer
        if layer == 0:
            self.n = i * PER0 + (N_PRE + j)
            self.slot = (N_PRE + j) % RING0
            self.use = i * (PER0 // RING0) + (N_PRE + j) // RING0
            self.ring = RING0
        else:
            self.n = i * PER1 + (N_L1 + j)
            self.slot = SLOTS1[j % RING1]
            self.use = i + (USED1[self.slot] + j // RING1)
            self.ring = RING1
        self.landed = self.use * 16 + 16
        self.freed = self.n - (self.ring - 1)
        self.waits = not isinstance(self.n, int) or self.freed > 0
        self.exists = not isinstance(self.n, int) or self.n < N_ALL


class Chain:

    def __init__(self, eng, sem):
        self.eng, self.sem, self.base, self.k = eng, sem, 0, 0

    def restart(self, base):
        self.base, self.k = base, 0

    def mark(self, ins):
        ins.then_inc(self.sem, 1)
        self.k += 1
        return self.base + self.k

    def wait(self, mark):
        self.eng.wait_ge(self.sem, mark)


def build(nc, w_all, w_dt, x_in, par_in, con_in, out):
    with ExitStack() as ctx:
        def sb(name, shape, dt=F32):
            return ctx.enter_context(nc.sbuf_tensor(name, shape, dt))

        def sem(name):
            return ctx.enter_context(nc.semaphore(name))

        raw = sb("raw", [P, RING1, CF])
        w_hi = sb("w_hi", [P, RING1, CF], F32R)
        w_lo = sb("w_lo", [P, RING1, CF], F32R)
        xT = sb("xT", [P, KT, SEQ])
        work = sb("work", [P, KT * SEQ])
        sq = work[:].rearrange("p (k t) -> p k t", k=KT)
        m_t = work[:, 0:HEADS_PER_IT * BLK].rearrange("p (h c) -> p h c", h=HEADS_PER_IT)
        xdt = work[:, HEADS_PER_IT * BLK:KT * SEQ].rearrange("p (t c) -> p t c", t=NT)
        hn_hi = sb("hn_hi", [P, KT, SEQ], F32R)
        hn_lo = sb("hn_lo", [P, KT, SEQ], F32R)
        y_hi = sb("y_hi", [P, 2 * KT, SEQ], F32R)
        y_lo = sb("y_lo", [P, 2 * KT, SEQ], F32R)
        ssd_u = raw[:, RING1 - 1, :].rearrange("p (k t) -> p k t", k=KT)
        con = sb("con", [P, N_CONST])
        par = sb("par", [P, N_PAR])
        tri_r = sb("tri_r", [P, 2 * P], F32R)
        qT = sb("qT", [P, 2, SEQ])
        kT = sb("kT", [P, 2, SEQ])
        v_t = sb("v_t", [P, NT, 2 * HD])
        gate2 = sb("gate2", [P, 2 * SEQ])
        s_m = sb("s_m", [P, 2, BLK])
        neg_max = sb("neg_max", [P, 2, NT])
        pace = sb("pace", [P, 2])
        prob = sb("prob", [P, 2, BLK])
        p_sum = sb("p_sum", [P, 2, NT])
        p_inv = sb("p_inv", [P, 2, NT])
        pT = sb("pT", [P, 2, BLK])
        conv = sb("conv", [P, 2, SEQ])
        xs = sb("xs", [P, 2, SEQ])
        b_s = sb("b_s", [P, SSD_GROUPS, SEQ])
        c_s = sb("c_s", [P, SSD_GROUPS, SEQ])
        z2 = sb("z2", [P, 2 * SEQ])
        decay = sb("decay", [P, 2, BLK])
        g_m = sb("g_m", [P, IT0, BLK])
        wd = sb("wd", [P, KT * SSD_HEADS])
        wd_hi = sb("wd_hi", [P, KT, SSD_HEADS], F32R)
        wd_lo = sb("wd_lo", [P, KT, SSD_HEADS], F32R)
        NH = NT * SSD_HEADS
        sp = sb("sp", [P, 8, NH])
        dt = sb("dt", [P, NT, SSD_HEADS])
        a_exp = sb("a_exp", [P, NH])
        ac = sb("ac", [P, NH])
        ac_hl = sb("ac_hl", [P, 2, NH], F32R)
        cum_s = sb("cum_s", [P, NH])
        cblk = sb("cblk", [P, SSD_HEADS, 3])
        it_par = sb("it_par", [P, CPAR])
        it_c = sb("it_c", [P, HEADS_PER_IT, 3])
        it_dt = sb("it_dt", [P, NT, HEADS_PER_IT])
        it_ac = sb("it_ac", [P, 2 * NT, HEADS_PER_IT], F32R)
        eps_t = sb("eps_t", [P, 2])
        nv = sb("nv", [P, 5, 4])

        bank = [ctx.enter_context(nc.psum_tensor(f"bank{b}", [P, 512], F32)) for b in range(8)]
        CUM, O_PS, Y_PS, S_PS, T_PS = [bank[2], bank[3]], bank[4], bank[5], bank[6], bank[7]

        ident, tri, ones = con[:, C_ID:C_ID + P], con[:, C_TRI:C_TRI + P], con[:, C_ONE:C_ONE + P]
        causal3 = con[:, C_TRI:C_TRI + BLK]
        mask = [con[:, C_M0:C_M0 + BLK], con[:, C_M1:C_M1 + BLK]]

        g_flat = g_m[:].rearrange("p i c -> p (i c)")

        def w3(t, slot):
            return t[:, slot, :].rearrange("p (k c) -> p k c", k=KT)

        def w_out(t, slot):
            return t[:, slot, :].rearrange("p (r c) -> p r c", r=2)

        landed = [sem(f"landed{s}") for s in range(RING1)]
        x_in_a, x_in_b, con_in_s, par_in_s, wd_in = (
            sem("x_in_a"), sem("x_in_b"), sem("con_landed"), sem("par_landed"), sem("wd_landed"))
        hi_ready, lo_ready = sem("hi_ready"), sem("lo_ready")
        mm_done = sem("mm_done")
        act_evac, dve_evac = sem("act_evac"), sem("dve_evac")
        s_done, s_free = sem("s_done"), sem("s_free")
        exp_done, p_ready = sem("exp_done"), sem("p_ready")
        t_done, t_ready = sem("t_done"), sem("t_ready")
        o_done, yf_ready = sem("o_done"), sem("yf_ready")
        yhi_ready, y_ready = sem("yhi_ready"), sem("y_ready")
        tap_bias, conv_tanh, taps_halved = sem("tap_bias"), sem("conv_tanh"), sem("taps_halved")
        xs_ready, xt_done, xdt_ready = sem("xs_ready"), sem("xt_done"), sem("xdt_ready")
        tanh_z, tanh_g = sem("tanh_z"), sem("tanh_g")
        staged, cum_done, sub_done = sem("staged"), sem("cum_done"), sem("sub_done")
        dec_ready, m_ready, yd_done = sem("dec_ready"), sem("m_ready"), sem("yd_done")
        u_ready = sem("u_ready")
        bc_done, gm_ready = sem("bc_done"), sem("gm_ready")
        dt_mm, dt_abs, dt_exp, ac_ready, cs_done, a_ready, wd_hi_s, wd_ready = (
            sem("dt_mm"), sem("dt_abs"), sem("dt_exp"), sem("ac_ready"), sem("cs_done"),
            sem("a_ready"), sem("wd_hi_ready"), sem("wd_ready"))
        eps_ready = sem("eps_ready")
        sq_ready, ms_done, sd_ready, r_ready = sem("sq_ready"), sem("ms_done"), sem("sd_ready"), sem("r_ready")
        rb_done, scaled, hnhi_ready, hn_ready = sem("rb_done"), sem("scaled"), sem("hnhi_ready"), sem("hn_ready")
        acc_done, x_ready = sem("acc_done"), sem("x_ready")
        dve_chain, out_landed = sem("dve_chain"), sem("out_landed")

        block = ctx.enter_context(nc.Block())

        def cols(norm):
            return NT * SSD_GROUPS if norm == 1 else NT

        @block.sync
        def _(sync):
            def load(c):
                if c.waits:
                    sync.wait_ge(lo_ready, c.freed)
                sync.dma_start(raw[:, c.slot, :], w_all[:, bass.ds(c.n, 1), :]).then_inc(landed[c.slot], 16)

            half = KT // 2
            sync.dma_start(xT[:, 0:half, :], x_in[:, 0:half, :]).then_inc(x_in_a, 16)
            sync.dma_start(xT[:, half:KT, :], x_in[:, half:KT, :]).then_inc(x_in_b, 16)
            sync.dma_start(con[:], con_in).then_inc(con_in_s, 16)
            load(Chunk(0, 0, -2))
            sync.dma_start(par[:], par_in).then_inc(par_in_s, 16)
            sync.dma_start(wd[:], w_dt).then_inc(wd_in, 16)
            load(Chunk(0, 0, -1))
            for j in range(PER0):
                load(Chunk(0, 0, j))
            with sync.Fori(1, IT0) as i:
                for j in range(PER0):
                    load(Chunk(0, i, j))
            for j in range(OUT_CHUNKS):
                load(Chunk(0, IT0, j))
            with sync.Fori(0, IT1) as i:
                for j in range(PER1):
                    load(Chunk(1, i, j))
            for j in range(OUT_CHUNKS):
                load(Chunk(1, IT1, j))
            for b in range(4):
                sync.wait_ge(scaled, 3 * KT + 2 * b + 2)
                sync.dma_start(out[:, 2 * b:2 * b + 2, :], sq[:, 2 * b:2 * b + 2, :]).then_inc(out_landed, 16)
            sync.wait_ge(out_landed, 64)

        @block.tensor
        def _(pe):
            def three(ps, a_hi, a_lo, m_hi, m_lo, start, stop, **kw):
                pe.matmul(ps, a_hi, m_hi, start=start, stop=False, **kw)
                pe.matmul(ps, a_hi, m_lo, start=False, stop=False, **kw)
                return pe.matmul(ps, a_lo, m_hi, start=False, stop=stop, **kw)

            def project(c, tile, pb, fresh=False):
                cs = slice(tile * P, tile * P + P)
                hi, lo = w3(w_hi, c.slot), w3(w_lo, c.slot)
                for k in range(KT):
                    if fresh is not False:
                        pe.wait_ge(hn_ready, fresh + k + 1)
                    last = three(bank[pb][:, tile * SEQ:(tile + 1) * SEQ], hi[:, k, cs], lo[:, k, cs],
                                 hn_hi[:, k, :], hn_lo[:, k, :], k == 0, k == KT - 1)
                return last

            def project_v(c, t, pb):
                ts = slice(t * P, t * P + P)
                hi, lo = w3(w_hi, c.slot), w3(w_lo, c.slot)
                for k in range(KT):
                    last = three(bank[pb][:, t * CW:(t + 1) * CW], hn_hi[:, k, ts], hn_lo[:, k, ts],
                                 hi[:, k, :], lo[:, k, :], k == 0, k == KT - 1)
                return last

            def scores(h, count):
                if not (isinstance(count, int) and count == 0):
                    pe.wait_ge(s_free, count)
                pe.matmul(S_PS[:, 0:P], qT[:, h, 0:P], kT[:, h, 0:P], start=True, stop=True)
                pe.matmul(S_PS[:, P:BLK], qT[:, h, P:SEQ], kT[:, h, :], start=True,
                          stop=True).then_inc(s_done, 1)

            def flip(h, count):
                pe.wait_ge(p_ready, count + 1)
                if not (isinstance(count, int) and count == 0):
                    pe.wait_ge(t_ready, count)
                for b in range(3):
                    last = pe.transpose(T_PS[:, b * P:(b + 1) * P], prob[:, h, b * P:(b + 1) * P], ident)
                last.then_inc(t_done, 1)

            def attend(h, count):
                pe.wait_ge(t_ready, count + 1)
                hs = slice(h * HD, (h + 1) * HD)
                pe.matmul(O_PS[:, h * SEQ:(h + 1) * SEQ], v_t[:, 0, hs], pT[:, h, 0:SEQ],
                          start=True, stop=False)
                pe.matmul(O_PS[:, h * SEQ + P:(h + 1) * SEQ], v_t[:, 1, hs], pT[:, h, SEQ:BLK],
                          start=False, stop=True).then_inc(o_done, 1)

            def mean_squares(norm):
                n = cols(norm)
                group = KT * NT // n
                for order, piece in enumerate(ACC_BANKS if norm >= 2 else range(4)):
                    pe.wait_ge(sq_ready, 4 * norm + order + 1)
                    for k in (2 * piece, 2 * piece + 1):
                        for t in range(NT):
                            col = k // group * NT + t
                            last = pe.matmul(Y_PS[:, col:col + 1], sq[:, k, t * P:(t + 1) * P],
                                             con[:, C_INV + (norm == 1):C_INV + (norm == 1) + 1],
                                             start=order == 0 and k == 2 * piece and t == 0,
                                             stop=order == 3, skip_group_check=True)
                last.then_inc(ms_done, 1)

            def spread(norm):
                pe.wait_ge(r_ready, norm + 1)
                for c in range(cols(norm)):
                    last = pe.matmul(Y_PS[:, c * P:(c + 1) * P], nv[:, 3, c:c + 1].to_broadcast([P, P]), ident,
                                     start=True, stop=True)
                last.then_inc(rb_done, 1)

            def cum(h, i):
                n = i * HEADS_PER_IT + h
                if h == 0:
                    pe.wait_ge(staged, i + 1)
                if not (isinstance(n, int) and n < 2):
                    pe.wait_ge(sub_done, n - 1)
                ps = CUM[h % 2]
                for c, cs in ((0, slice(0, P)), (1, slice(P, BLK))):
                    for part in range(2):
                        last = pe.matmul(ps[:, cs], it_ac[:, part * NT + c, h:h + 1].to_broadcast([P, P]),
                                         tri_r[:, 0:cs.stop - cs.start], start=part == 0, stop=part == 1)
                last.then_inc(cum_done, 1)

            def x_to_tokens(i):
                pe.wait_ge(xs_ready, i + 3)
                if isinstance(i, int) and i == 0:
                    pe.wait_ge(gm_ready, 1)
                for t in range(NT):
                    for c in range(2):
                        last = pe.transpose(S_PS[:, t * CW + c * P:t * CW + (c + 1) * P],
                                            xs[:, c, t * P:(t + 1) * P], ident)
                last.then_inc(xt_done, 1)

            def ssd_out(h, i):
                pe.wait_ge(m_ready, i * HEADS_PER_IT + (h + 1))
                if h == 0:
                    pe.wait_ge(xdt_ready, i + 1)
                    if not (isinstance(i, int) and i == 0):
                        pe.wait_ge(u_ready, i)
                rows, c0 = slice(64 * (h % 2), 64 * (h % 2) + 64), (h // 2) * SEQ
                pe.matmul(Y_PS[rows, c0:c0 + SEQ], xdt[:, 0, h * 64:(h + 1) * 64], m_t[:, h, 0:SEQ],
                          start=True, stop=False)
                last = pe.matmul(Y_PS[rows, c0 + P:c0 + SEQ], xdt[:, 1, h * 64:(h + 1) * 64],
                                 m_t[:, h, SEQ:BLK], start=False, stop=True)
                if h == HEADS_PER_IT - 1:
                    last.then_inc(yd_done, 1)

            def bc_scores():
                pe.wait_ge(xs_ready, 2)
                for g, ps in ((0, S_PS), (1, T_PS)):
                    pe.matmul(ps[:, 0:SEQ], b_s[:, g, 0:P], c_s[:, g, :], start=True, stop=True)
                    last = pe.matmul(ps[:, SEQ:BLK], b_s[:, g, P:SEQ], c_s[:, g, P:SEQ], start=True, stop=True)
                last.then_inc(bc_done, 1)

            def layer0(i, first):
                heads = (i - 1) * 2
                c = [Chunk(0, i, j) for j in range(PER0)]
                pe.wait_ge(lo_ready, c[X].n + 1)
                if first:
                    pe.wait_ge(dve_evac, 1)
                else:
                    pe.wait_ge(act_evac, i * 3)
                project(c[X], 0, 0)
                if not first:
                    pe.wait_ge(act_evac, i * 3)
                    scores(0, heads)
                project(c[X], 1, 0).then_inc(mm_done, 1)
                if not first:
                    scores(1, heads + 1)
                pe.wait_ge(lo_ready, c[Z].n + 1)
                pe.wait_ge(dve_evac, i * 3 + 2)
                project(c[Z], 0, 1)
                if first:
                    cum_sums()
                    bc_scores()
                else:
                    flip(0, heads)
                    cum(0, i)
                project(c[Z], 1, 1).then_inc(mm_done, 1)
                if first:
                    cum(0, i)
                else:
                    flip(1, heads + 1)
                cum(1, i)
                pe.wait_ge(lo_ready, c[Q0].n + 1)
                pe.wait_ge(dve_evac, i * 3 + 3)
                project(c[Q0], 0, 0)
                if not first:
                    attend(0, heads)
                x_to_tokens(i)
                project(c[Q0], 1, 0).then_inc(mm_done, 1)
                if not first:
                    attend(1, heads + 1)
                cum(2, i)
                pe.wait_ge(lo_ready, c[K0].n + 1)
                pe.wait_ge(dve_evac, i * 3 + 4)
                project(c[K0], 0, 1)
                cum(3, i)
                project(c[K0], 1, 1).then_inc(mm_done, 1)
                pe.wait_ge(lo_ready, c[V0].n + 1)
                pe.wait_ge(act_evac, i * 3 + 1)
                project_v(c[V0], 0, 0)
                ssd_out(0, i)
                ssd_out(1, i)
                project_v(c[V0], 1, 0).then_inc(mm_done, 1)
                ssd_out(2, i)
                ssd_out(3, i)
                pe.wait_ge(lo_ready, c[G0].n + 1)
                pe.wait_ge(act_evac, i * 3 + 2)
                project(c[G0], 0, 1)
                project(c[G0], 1, 1).then_inc(mm_done, 1)

            def layer1(i, first):
                heads = (i - 1) * 2 + MOBA_HEADS
                c = [Chunk(1, i, j) for j in range(PER1)]
                act0 = i * 3 + 3 * IT0
                pe.wait_ge(lo_ready, c[Q1].n + 1)
                if not first:
                    pe.wait_ge(act_evac, act0)
                project(c[Q1], 0, 0, fresh=2 * KT if first else False)
                if not first:
                    scores(0, heads)
                project(c[Q1], 1, 0).then_inc(mm_done, 1)
                if not first:
                    scores(1, heads + 1)
                pe.wait_ge(lo_ready, c[K1].n + 1)
                if not first:
                    pe.wait_ge(dve_evac, i + (2 + 3 * IT0))
                project(c[K1], 0, 1)
                if not first:
                    flip(0, heads)
                project(c[K1], 1, 1).then_inc(mm_done, 1)
                if not first:
                    flip(1, heads + 1)
                pe.wait_ge(lo_ready, c[V1].n + 1)
                pe.wait_ge(act_evac, act0 + 1)
                project_v(c[V1], 0, 0)
                if not first:
                    attend(0, heads)
                project_v(c[V1], 1, 0).then_inc(mm_done, 1)
                if not first:
                    attend(1, heads + 1)
                pe.wait_ge(lo_ready, c[G1].n + 1)
                pe.wait_ge(act_evac, act0 + 2)
                project(c[G1], 0, 1)
                project(c[G1], 1, 1).then_inc(mm_done, 1)

            def project_out(j, tiles, c, hooks, y_need):
                pe.wait_ge(lo_ready, c.n + 1)
                pe.wait_ge(y_ready, y_need)
                hi, lo = w_out(w_hi, c.slot), w_out(w_lo, c.slot)
                for nb, b in enumerate(ACC_BANKS):
                    if j == 0 and b == 0:
                        pe.wait_ge(act_evac, 3 * IT0 + (3 * IT1 if c.layer else 0))
                    if j == 0 and b == 1:
                        pe.wait_ge(dve_evac, 2 + 3 * IT0 + (IT1 if c.layer else 0))
                    for d in range(2):
                        ds = slice((2 * b + d) * P, (2 * b + d + 1) * P)
                        for r in range(2):
                            last = three(bank[b][:, d * SEQ:(d + 1) * SEQ], hi[:, r, ds], lo[:, r, ds],
                                         y_hi[:, tiles + r, :], y_lo[:, tiles + r, :],
                                         j == 0 and d == 0 and r == 0, j == OUT_CHUNKS - 1 and r == 1,
                                         skip_group_check=True)
                    if nb == 3:
                        last.then_inc(mm_done, 1)
                    elif j == OUT_CHUNKS - 1:
                        last.then_inc(acc_done, 1)
                    if nb in hooks:
                        hooks[nb]()

            def cum_sums():
                pe.wait_ge(ac_ready, 1)
                pe.matmul(Y_PS[:, 64:64 + NH], tri, ac[:], start=True, stop=True)
                pe.matmul(Y_PS[:, 64 + NH:64 + NH + SSD_HEADS], ones, ac[:, 0:SSD_HEADS],
                          start=True, stop=True).then_inc(cs_done, 1)

            pe.wait_ge(con_in_s, 16)
            mean_squares(0)
            spread(0)
            pe.wait_ge(lo_ready, 1)
            project(Chunk(0, 0, -2), 0, 0, fresh=0)
            project(Chunk(0, 0, -2), 1, 0).then_inc(mm_done, 1)
            pe.wait_ge(wd_ready, 1)
            for t in range(NT):
                for k in range(KT):
                    ts = slice(t * P, (t + 1) * P)
                    last = three(Y_PS[:, t * SSD_HEADS:(t + 1) * SSD_HEADS], hn_hi[:, k, ts], hn_lo[:, k, ts],
                                 wd_hi[:, k, :], wd_lo[:, k, :], k == 0, k == KT - 1)
            last.then_inc(dt_mm, 1)
            pe.wait_ge(lo_ready, 2)
            project(Chunk(0, 0, -1), 0, 1)
            project(Chunk(0, 0, -1), 1, 1).then_inc(mm_done, 1)

            layer0(0, True)
            with pe.Fori(1, IT0) as i:
                layer0(i, False)

            h0 = MOBA_HEADS - 2
            pe.wait_ge(act_evac, 3 * IT0 - 1)
            pe.wait_ge(sub_done, SSD_HEADS)
            hooks = {0: {2: lambda: scores(0, h0), 3: lambda: (scores(1, h0 + 1), mean_squares(1))},
                     1: {1: lambda: flip(0, h0), 3: lambda: (flip(1, h0 + 1), spread(1))},
                     2: {1: lambda: attend(0, h0), 3: lambda: attend(1, h0 + 1)}}
            order = OUT_ORDER0
            for j in range(OUT_CHUNKS):
                if order[j] < KT:
                    pe.wait_ge(hn_ready, KT + order[j] + 2)
                    need = 3
                else:
                    need = order[j] // 2 - 3
                project_out(j, order[j], Chunk(0, IT0, j), hooks.get(j, {}), need)
            mean_squares(2)
            spread(2)

            layer1(0, True)
            with pe.Fori(1, IT1) as i:
                layer1(i, False)
            h1 = MOBA_HEADS + DIL_HEADS - 2
            pe.wait_ge(act_evac, 3 * IT0 + 3 * IT1 - 1)
            hooks = {0: {2: lambda: scores(0, h1), 3: lambda: scores(1, h1 + 1)},
                     1: {1: lambda: flip(0, h1), 3: lambda: flip(1, h1 + 1)},
                     2: {1: lambda: attend(0, h1), 3: lambda: attend(1, h1 + 1)}}
            for j in range(OUT_CHUNKS):
                project_out(j, 2 * j, Chunk(1, IT1, j), hooks.get(j, {}), IT0 + j + 1)
            mean_squares(3)
            spread(3)

        @block.scalar
        def _(act):
            def split_hi(c):
                if not c.exists:
                    return
                act.wait_ge(landed[c.slot], c.landed)
                if c.waits:
                    act.wait_ge(mm_done, c.freed)
                act.activation(w_hi[:, c.slot, :], raw[:, c.slot, :], ACT.Copy).then_inc(hi_ready, 1)

            def squares(src, piece, norm):
                act.activation(sq[:, 2 * piece:2 * piece + 2, :], src[:, 2 * piece:2 * piece + 2, :],
                               ACT.Square).then_inc(sq_ready, 1)

            def root(norm):
                act.wait_ge(ms_done, norm + 1)
                act.activation(nv[:, 0, 0:cols(norm)], Y_PS[:, 0:cols(norm)], ACT.Sqrt,
                               bias=eps_t[:, (norm == 1):(norm == 1) + 1]).then_inc(sd_ready, 1)

            def norm_hi(dst, base):
                for k in range(KT):
                    act.wait_ge(scaled, base + k + 1)
                    act.activation(dst[:, k, :], sq[:, k, :], ACT.Copy).then_inc(hnhi_ready, 1)

            def exps(h, count):
                act.wait_ge(s_free, count + 1)
                act.activation(prob[:, h, 0:P], s_m[:, h, 0:P], ACT.Exp, bias=neg_max[:, h, 0:1], scale=-1.0,
                               accum_out=p_sum[:, h, 0:1])
                act.activation(prob[:, h, P:BLK], s_m[:, h, P:BLK], ACT.Exp, bias=neg_max[:, h, 1:2], scale=-1.0,
                               accum_out=p_sum[:, h, 1:2]).then_inc(exp_done, 1)

            def take_t(h, count):
                act.wait_ge(t_done, count + 1)
                act.activation(pT[:, h, :], T_PS[:, 0:BLK], ACT.Copy).then_inc(t_ready, 1)

            def conv_start(c, pb, taps):
                act.wait_ge(mm_done, c.n + 1)
                for t in range(2):
                    o = (CONV + 1) * t
                    last = act.activation(conv[:, t, :], bank[pb][:, t * SEQ:(t + 1) * SEQ], ACT.Identity,
                                          bias=taps[:, o + CONV:o + CONV + 1], scale=taps[:, o + 3:o + 4])
                last.then_inc(tap_bias, 1)

            def conv_end(n, dst):
                act.wait_ge(dve_evac, n)
                act.activation(dst[:], conv[:], ACT.Tanh).then_inc(conv_tanh, 1)

            def dec(h, i):
                act.wait_ge(sub_done, i * HEADS_PER_IT + (h + 1))
                act.activation(decay[:, h % 2, :], decay[:, h % 2, :], ACT.Exp).then_inc(dec_ready, 1)

            def y_high(tile, count):
                act.wait_ge(yf_ready, count)
                act.activation(y_hi[:, tile, :], gate2[:].rearrange("p (a t) -> p a t", a=2),
                               ACT.Copy).then_inc(yhi_ready, 1)

            def take(dst, c, pb, scale=1.0):
                act.wait_ge(mm_done, c.n + 1)
                act.activation(dst, bank[pb][:], ACT.Copy, scale=scale).then_inc(act_evac, 1)

            def tanh_of(dst, c, pb, s):
                act.wait_ge(mm_done, c.n + 1)
                act.activation(dst, bank[pb][:], ACT.Tanh, scale=0.5).then_inc(s, 1)

            def flat(t):
                return t[:].rearrange("p a t -> p (a t)")

            def layer0(i, first):
                heads = (i - 1) * 2
                c = [Chunk(0, i, j) for j in range(PER0 + 2)]
                prev = Chunk(0, i, -1)
                if first:
                    act.wait_ge(xs_ready, 1)
                    conv_start(prev, 1, par[:, P_CONV + CPAR:P_CONV + 2 * CPAR])
                    split_hi(c[X + 2])
                    conv_end(2, c_s)
                else:
                    act.wait_ge(u_ready, i)
                    tanh_of(gate2[:], prev, 1, tanh_g)
                    split_hi(c[X + 2])
                    exps(0, heads)
                act.wait_ge(staged, i + 1)
                act.wait_ge(xs_ready, i + 2)
                conv_start(c[X], 0, it_par)
                if not first:
                    exps(1, heads + 1)
                    take_t(0, heads)
                conv_end(i * 3 + 3, xs)
                split_hi(c[Z + 2])
                dec(0, i)
                tanh_of(z2[:], c[Z], 1, tanh_z)
                if not first:
                    take_t(1, heads + 1)
                dec(1, i)
                split_hi(c[Q0 + 2])
                dec(2, i)
                if not first:
                    act.wait_ge(s_done, heads + 2)
                take(flat(qT), c[Q0], 0, -SCALE)
                if not first:
                    y_high(bass.ds(i * 2 + (KT - 2), 2), i)
                split_hi(c[K0 + 2])
                dec(3, i)
                take(flat(kT), c[K0], 1)
                split_hi(c[V0 + 2])
                if not first:
                    act.wait_ge(o_done, heads + 2)
                take(flat(v_t), c[V0], 0)
                split_hi(c[G0 + 2])

            def layer1(i, first):
                heads = (i - 1) * 2 + MOBA_HEADS
                c = [Chunk(1, i, j) for j in range(PER1 + 2)]
                prev = Chunk(1, i, -1)
                if not first:
                    act.wait_ge(y_ready, i + (IT0 - 1))
                    tanh_of(gate2[:], prev, 1, tanh_g)
                split_hi(c[Q1 + 2])
                if not first:
                    exps(0, heads)
                    act.wait_ge(s_done, heads + 2)
                take(flat(qT), c[Q1], 0, -SCALE)
                if not first:
                    exps(1, heads + 1)
                split_hi(c[K1 + 2])
                if not first:
                    take_t(0, heads)
                take(flat(kT), c[K1], 1)
                if not first:
                    take_t(1, heads + 1)
                split_hi(c[V1 + 2])
                if not first:
                    act.wait_ge(o_done, heads + 2)
                take(flat(v_t), c[V1], 0)
                split_hi(c[G1 + 2])
                if not first:
                    y_high(bass.ds(i * 2 - 2, 2), i + IT0)

            act.preload_act_table(ACT.Sqrt)
            act.wait_ge(x_in_a, 16)
            squares(xT, 0, 0)
            squares(xT, 1, 0)
            act.wait_ge(x_in_b, 16)
            squares(xT, 2, 0)
            squares(xT, 3, 0)
            split_hi(Chunk(0, 0, -2))
            act.wait_ge(eps_ready, 1)
            root(0)
            act.preload_act_table(ACT.Exp)
            act.wait_ge(con_in_s, 16)
            for t in range(2):
                last = act.activation(tri_r[:, t * P:(t + 1) * P], tri, ACT.Copy)
            act.wait_ge(wd_in, 16)
            act.activation(wd_hi[:], wd[:].rearrange("p (k h) -> p k h", k=KT), ACT.Copy).then_inc(wd_hi_s, 1)
            norm_hi(hn_hi, 0)
            act.wait_ge(par_in_s, 16)
            act.activation(a_exp[:], par[:, P_ALOG:P_ALOG + NH], ACT.Exp).then_inc(a_ready, 1)
            split_hi(Chunk(0, 0, -1))
            act.wait_ge(taps_halved, 1)
            conv_start(Chunk(0, 0, -2), 0, par[:, P_CONV:P_CONV + CPAR])
            act.wait_ge(dt_abs, 1)
            act.activation(sp[:, 2, :], sp[:, 1, :], ACT.Exp, scale=-1.0).then_inc(dt_exp, 1)
            conv_end(1, b_s)
            split_hi(Chunk(0, 0, 0))
            split_hi(Chunk(0, 0, 1))

            layer0(0, True)
            with act.Fori(1, IT0) as i:
                layer0(i, False)

            h0 = MOBA_HEADS - 2
            o = [Chunk(0, IT0, j) for j in range(-1, OUT_CHUNKS + 2)]
            act.wait_ge(u_ready, IT0)
            tanh_of(gate2[:], o[0], 1, tanh_g)
            for k in range(4):
                squares(ssd_u, k, 1)
            split_hi(o[3])
            exps(0, h0)
            exps(1, h0 + 1)
            root(1)
            split_hi(o[4])
            take_t(0, h0)
            take_t(1, h0 + 1)
            for k in range(4):
                act.wait_ge(scaled, KT + k + 1)
                act.activation(y_hi[:, k, :], sq[:, k, :], ACT.Copy).then_inc(hnhi_ready, 1)
            split_hi(o[5])
            for k in range(4, KT):
                act.wait_ge(scaled, KT + k + 1)
                act.activation(y_hi[:, k, :], sq[:, k, :], ACT.Copy).then_inc(hnhi_ready, 1)
            y_high(slice(2 * KT - 2, 2 * KT), IT0)
            split_hi(o[6])
            split_hi(o[7])
            split_hi(o[8])
            split_hi(o[9])
            split_hi(o[10])
            act.preload_act_table(ACT.Sqrt)
            for k, b in enumerate(ACC_BANKS):
                act.wait_ge(x_ready, k + 1)
                squares(xT, b, 2)
            root(2)
            act.preload_act_table(ACT.Exp)
            norm_hi(hn_hi, 2 * KT)
            layer1(0, True)
            with act.Fori(1, IT1) as i:
                layer1(i, False)
            h1 = MOBA_HEADS + DIL_HEADS - 2
            o = [Chunk(1, IT1, j) for j in range(-1, OUT_CHUNKS + 2)]
            act.wait_ge(y_ready, IT0 + IT1 - 1)
            tanh_of(gate2[:], o[0], 1, tanh_g)
            split_hi(o[3])
            exps(0, h1)
            exps(1, h1 + 1)
            split_hi(o[4])
            take_t(0, h1)
            take_t(1, h1 + 1)
            split_hi(o[5])
            y_high(slice(2 * KT - 2, 2 * KT), IT0 + IT1)
            for k in range(6, 9):
                split_hi(o[k])
            act.preload_act_table(ACT.Sqrt)
            for k, b in enumerate(ACC_BANKS):
                act.wait_ge(x_ready, 4 + k + 1)
                squares(xT, b, 3)
            root(3)

        @block.vector
        def _(dve):
            ch = Chain(dve, dve_chain)

            def split_lo(c):
                if not c.exists:
                    return
                dve.wait_ge(hi_ready, c.n + 1)
                dve.tensor_tensor(w_lo[:, c.slot, :], raw[:, c.slot, :], w_hi[:, c.slot, :].bitcast(F32),
                                  ALU.subtract).then_inc(lo_ready, 1)

            def inverse_root(norm):
                n = slice(0, cols(norm))
                dve.wait_ge(sd_ready, norm + 1)
                a = ch.mark(dve.tensor_scalar(nv[:, 1, n], Y_PS[:, n], 4 * EPS if norm == 1 else EPS, None, ALU.add))
                b = ch.mark(dve.reciprocal(nv[:, 2, n], nv[:, 0, n]))
                ch.wait(b)
                b = ch.mark(dve.tensor_tensor(nv[:, 4, n], nv[:, 2, n], nv[:, 2, n], ALU.mult))
                ch.wait(b)
                b = ch.mark(dve.tensor_tensor(nv[:, 4, n], nv[:, 4, n], nv[:, 1, n], ALU.mult))
                ch.wait(b)
                b = ch.mark(dve.tensor_scalar(nv[:, 4, n], nv[:, 4, n], -0.5, 1.5, ALU.mult, ALU.add))
                ch.wait(b)
                dve.tensor_tensor(nv[:, 3, n], nv[:, 2, n], nv[:, 4, n], ALU.mult).then_inc(r_ready, 1)

            def scale_tile(src, k, gains, norm):
                g = (k // 4) * SEQ if norm == 1 else 0
                dve.scalar_tensor_tensor(out=sq[:, k, :], in0=src[:, k, :], scalar=par[:, gains + k:gains + k + 1],
                                         in1=Y_PS[:, g:g + SEQ], op0=ALU.mult, op1=ALU.mult).then_inc(scaled, 1)

            def norm_lo(dst_hi, dst_lo, k, base):
                dve.wait_ge(hnhi_ready, base + k + 1)
                dve.tensor_tensor(dst_lo[:, k, :], sq[:, k, :], dst_hi[:, k, :].bitcast(F32),
                                  ALU.subtract).then_inc(hn_ready, 1)

            def apply_norm(src, gains, norm, dst_hi, dst_lo, base):
                dve.wait_ge(rb_done, norm + 1)
                for k in range(KT + 1):
                    if k < KT:
                        scale_tile(src, k, gains, norm)
                    if k:
                        norm_lo(dst_hi, dst_lo, k - 1, base)

            def soft_scores(h, count, layer):
                dve.wait_ge(s_done, count + 1)
                dve.memset(pace[:, h:h + 1], 0.0)
                for t, cs in ((0, slice(0, P)), (1, slice(P, BLK))):
                    last = dve.tensor_tensor_reduce(s_m[:, h, cs], S_PS[:, cs], mask[layer][:, cs], 1.0, BIG,
                                                    ALU.add, ALU.min, neg_max[:, h, t:t + 1])
                last.then_inc(s_free, 1)

            def normalise(h, count):
                dve.wait_ge(exp_done, count + 1)
                ch.wait(ch.mark(dve.reciprocal(p_inv[:, h, :], p_sum[:, h, :])))
                for t, cs in ((0, slice(0, P)), (1, slice(P, BLK))):
                    last = dve.tensor_scalar(prob[:, h, cs], prob[:, h, cs], p_inv[:, h, t:t + 1], None, ALU.mult)
                last.then_inc(p_ready, 1)

            def gate_of(c, count):
                dve.wait_ge(tanh_g, count)
                dve.scalar_tensor_tensor(out=gate2[:], in0=gate2[:], scalar=1.0, in1=bank[1][:], op0=ALU.add,
                                         op1=ALU.mult).then_inc(dve_evac, 1)

            def gated(heads):
                dve.wait_ge(o_done, heads + 2)
                dve.scalar_tensor_tensor(out=gate2[:], in0=O_PS[:], scalar=0.5, in1=gate2[:], op0=ALU.mult,
                                         op1=ALU.mult).then_inc(yf_ready, 1)

            def y_low(tile, count):
                dve.wait_ge(yhi_ready, count)
                dve.tensor_tensor(y_lo[:, tile, :], gate2[:].rearrange("p (a t) -> p a t", a=2),
                                  y_hi[:, tile, :].bitcast(F32), ALU.subtract).then_inc(y_ready, 1)

            def conv_taps(n, pb, taps):
                dve.wait_ge(tap_bias, n)
                marks = [None, None]
                for k in range(CONV - 1):
                    shift = CONV - 1 - k
                    for t in range(2):
                        o = (CONV + 1) * t
                        if k:
                            ch.wait(marks[t])
                        last = dve.scalar_tensor_tensor(
                            out=conv[:, t, shift:], in0=bank[pb][:, t * SEQ:(t + 1) * SEQ - shift],
                            scalar=taps[:, o + k:o + k + 1], in1=conv[:, t, shift:], op0=ALU.mult, op1=ALU.add)
                        if k < CONV - 2:
                            marks[t] = ch.mark(last)
                last.then_inc(dve_evac, 1)

            def conv_silu(n, dst):
                dve.wait_ge(conv_tanh, n)
                dve.scalar_tensor_tensor(out=dst, in0=dst, scalar=1.0, in1=conv[:], op0=ALU.add,
                                         op1=ALU.mult).then_inc(xs_ready, 1)

            def sub(h, i):
                if not (isinstance(i, int) and i * HEADS_PER_IT + h < 2):
                    dve.wait_ge(m_ready, i * HEADS_PER_IT + (h - 1))
                dve.wait_ge(cum_done, i * HEADS_PER_IT + (h + 1))
                three = CUM[h % 2][:, 0:BLK].rearrange("p (b l) -> p b l", b=3)
                ch.wait(ch.mark(dve.tensor_tensor(decay[:, h % 2, :].rearrange("p (b l) -> p b l", b=3), three,
                                                  it_c[:, h, :].unsqueeze(2).to_broadcast([P, 3, P]),
                                                  ALU.subtract)))
                dve.tensor_scalar(decay[:, h % 2, :], decay[:, h % 2, :], 0.0, None,
                                  ALU.min).then_inc(sub_done, 1)

            def weigh(h, i):
                dve.wait_ge(dec_ready, i * HEADS_PER_IT + (h + 1))
                dve.tensor_tensor(m_t[:, h, :], decay[:, h % 2, :], g_flat[:, bass.ds(i * BLK, BLK)],
                                  ALU.mult).then_inc(m_ready, 1)

            def stage(i):
                if not (isinstance(i, int) and i == 0):
                    dve.wait_ge(cum_done, i * HEADS_PER_IT)
                hs = bass.ds(i * HEADS_PER_IT, HEADS_PER_IT)
                dve.tensor_copy(it_par[:], par[:, bass.ds(i * CPAR + (P_CONV + 2 * CPAR), CPAR)])
                dve.tensor_copy(it_c[:], cblk[:, hs, :])
                dve.tensor_copy(it_dt[:], dt[:, :, hs])
                dve.tensor_copy(it_ac[:], ac_hl[:].bitcast(F32).rearrange("p a (c h) -> p (a c) h", c=NT)
                                [:, :, hs]).then_inc(staged, 1)
                dve.wait_ge(staged, i + 1)

            def layer0(i, first):
                heads = (i - 1) * 2
                c = [Chunk(0, i, j) for j in range(PER0 + 2)]
                if first:
                    conv_taps(2, 1, par[:, P_CONV + CPAR:])
                    split_lo(c[X + 2])
                    prepare_dt()
                    conv_silu(2, c_s[:])
                    prepare_cum()
                else:
                    gate_of(None, i)
                stage(i)
                if not first:
                    soft_scores(0, heads, 0)
                    split_lo(c[X + 2])
                    normalise(0, heads)
                    soft_scores(1, heads + 1, 0)
                if first:
                    prepare_gm()
                conv_taps(i + 3, 0, it_par)
                if not first:
                    normalise(1, heads + 1)
                sub(0, i)
                conv_silu(i + 3, xs[:])
                split_lo(c[Z + 2])
                sub(1, i)
                weigh(0, i)
                dve.wait_ge(tanh_z, i + 1)
                dve.scalar_tensor_tensor(out=z2[:], in0=z2[:], scalar=1.0, in1=bank[1][:], op0=ALU.add,
                                         op1=ALU.mult).then_inc(dve_evac, 1)
                dve.wait_ge(xt_done, i + 1)
                dve.tensor_tensor(xdt.rearrange("p t (h c) -> p (t h) c", h=HEADS_PER_IT),
                                  S_PS[:].rearrange("p (a c) -> p a c", c=64),
                                  it_dt[:].rearrange("p t h -> p (t h)").unsqueeze(2)
                                  .to_broadcast([P, NT * HEADS_PER_IT, 64]), ALU.mult).then_inc(xdt_ready, 1)
                weigh(1, i)
                sub(2, i)
                split_lo(c[Q0 + 2])
                if not first:
                    gated(heads)
                sub(3, i)
                weigh(2, i)
                split_lo(c[K0 + 2])
                weigh(3, i)
                if not first:
                    y_low(bass.ds(i * 2 + (KT - 2), 2), i)
                split_lo(c[V0 + 2])
                dve.wait_ge(yd_done, i + 1)
                for t in range(2):
                    m = ch.mark(dve.scalar_tensor_tensor(
                        out=xs[:, t, :], in0=xs[:, t, :], scalar=it_par[:, 2 * (CONV + 1) + t:2 * (CONV + 1) + t + 1],
                        in1=Y_PS[:, t * SEQ:(t + 1) * SEQ], op0=ALU.mult, op1=ALU.add))
                ch.wait(m)
                dve.tensor_tensor(ssd_u[:, bass.ds(i * 2, 2), :], xs[:], z2[:].rearrange("p (a t) -> p a t", a=2),
                                  ALU.mult).then_inc(u_ready, 1)
                split_lo(c[G0 + 2])

            def layer1(i, first):
                heads = (i - 1) * 2 + MOBA_HEADS
                c = [Chunk(1, i, j) for j in range(PER1 + 2)]
                if not first:
                    gate_of(None, i + IT0)
                    soft_scores(0, heads, 1)
                split_lo(c[Q1 + 2])
                if not first:
                    normalise(0, heads)
                    soft_scores(1, heads + 1, 1)
                    normalise(1, heads + 1)
                split_lo(c[K1 + 2])
                split_lo(c[V1 + 2])
                if not first:
                    gated(heads)
                split_lo(c[G1 + 2])
                if not first:
                    y_low(bass.ds(i * 2 - 2, 2), i + IT0)

            def prepare_dt():
                v, mag, e, s, z, zz, acc = (sp[:, k, :] for k in range(7))
                dve.wait_ge(dt_exp, 1)
                ch.wait(ch.mark(dve.tensor_scalar(s, e, 2.0, None, ALU.add)))
                ch.wait(ch.mark(dve.reciprocal(s, s)))
                ch.wait(ch.mark(dve.tensor_tensor(z, e, s, ALU.mult)))
                ch.wait(ch.mark(dve.tensor_tensor(zz, z, z, ALU.mult)))
                ch.wait(ch.mark(dve.tensor_scalar(acc, zz, 1.0 / 17, None, ALU.mult)))
                for odd in (15, 13, 11, 9, 7, 5, 3):
                    ch.wait(ch.mark(dve.scalar_tensor_tensor(out=acc, in0=acc, scalar=1.0 / odd, in1=zz,
                                                             op0=ALU.add, op1=ALU.mult)))
                ch.wait(ch.mark(dve.scalar_tensor_tensor(out=acc, in0=acc, scalar=1.0, in1=z,
                                                         op0=ALU.add, op1=ALU.mult)))
                ch.wait(ch.mark(dve.tensor_scalar(v, v, 0.0, None, ALU.max)))
                d = dt[:].rearrange("p t h -> p (t h)")
                ch.wait(ch.mark(dve.scalar_tensor_tensor(out=d, in0=acc, scalar=2.0, in1=v, op0=ALU.mult,
                                                         op1=ALU.add)))
                dve.wait_ge(a_ready, 1)
                ch.wait(ch.mark(dve.scalar_tensor_tensor(out=ac[:], in0=d, scalar=-1.0, in1=a_exp[:],
                                                         op0=ALU.mult, op1=ALU.mult)))
                ch.wait(ch.mark(dve.tensor_copy(ac_hl[:, 0, :], ac[:])))
                dve.tensor_tensor(ac_hl[:, 1, :], ac[:], ac_hl[:, 0, :].bitcast(F32),
                                  ALU.subtract).then_inc(ac_ready, 1)

            def prepare_cum():
                dve.wait_ge(cs_done, 1)
                H = SSD_HEADS
                ch.wait(ch.mark(dve.tensor_copy(cum_s[:], Y_PS[:, 64:64 + NH])))
                dve.tensor_copy(cblk[:, :, 0:1], cum_s[:, 0:H].unsqueeze(2))
                dve.tensor_tensor(cblk[:, :, 1:2], cum_s[:, 0:H].unsqueeze(2),
                                  Y_PS[:, 64 + NH:64 + NH + H].unsqueeze(2), ALU.subtract)
                ch.wait(ch.mark(dve.tensor_copy(cblk[:, :, 2:3], cum_s[:, H:2 * H].unsqueeze(2))))

            def prepare_gm():
                dve.wait_ge(bc_done, 1)
                for k in range(IT0):
                    ps = S_PS if k < IT0 // 2 else T_PS
                    last = dve.tensor_tensor(g_m[:, k, :], ps[:, 0:BLK], causal3, ALU.mult)
                last.then_inc(gm_ready, 1)
                dve.wait_ge(gm_ready, 1)

            def add_residual(layer):
                for k, b in enumerate(ACC_BANKS):
                    if k < 3:
                        dve.wait_ge(acc_done, 3 * layer + k + 1)
                    else:
                        dve.wait_ge(mm_done, (N_L1, N_ALL)[layer])
                    x2 = xT[:, 2 * b:2 * b + 2, :]
                    dve.tensor_tensor(x2, bank[b][:].rearrange("p (a t) -> p a t", a=2), x2,
                                      ALU.add).then_inc(x_ready, 1)
                dve.wait_ge(x_ready, 4 * layer + 4)

            dve.memset(eps_t[:, 0:1], EPS)
            dve.memset(eps_t[:, 1:2], 4 * EPS).then_inc(eps_ready, 1)
            dve.wait_ge(eps_ready, 1)
            split_lo(Chunk(0, 0, -2))
            inverse_root(0)
            dve.wait_ge(par_in_s, 16)
            apply_norm(xT, P_EVEN, 0, hn_hi, hn_lo, 0)
            dve.wait_ge(wd_hi_s, 1)
            dve.tensor_tensor(wd_lo[:], wd[:].rearrange("p (k h) -> p k h", k=KT), wd_hi[:].bitcast(F32),
                              ALU.subtract).then_inc(wd_ready, 1)
            cp = par[:, P_CONV:P_CONV + (IT0 + 2) * CPAR].rearrange("p (n c) -> p n c", c=CPAR)
            cp = cp[:, :, 0:2 * (CONV + 1)]
            dve.tensor_scalar(cp, cp, 0.5, None, ALU.mult).then_inc(taps_halved, 1)
            dve.wait_ge(taps_halved, 1)
            split_lo(Chunk(0, 0, -1))
            conv_taps(1, 0, par[:, P_CONV:])
            dve.wait_ge(dt_mm, 1)
            v, mag = sp[:, 0, :], sp[:, 1, :]
            ch.wait(ch.mark(dve.tensor_tensor(v, Y_PS[:, 0:NH], par[:, P_DTB:P_DTB + NH], ALU.add)))
            dve.scalar_tensor_tensor(out=mag, in0=v, scalar=-1.0, in1=v, op0=ALU.mult,
                                     op1=ALU.max).then_inc(dt_abs, 1)
            conv_silu(1, b_s[:])
            split_lo(Chunk(0, 0, 0))
            split_lo(Chunk(0, 0, 1))

            layer0(0, True)
            base = ch.base + ch.k
            with dve.Fori(1, IT0) as i:
                ch.restart(i * MARKS0 + (base - MARKS0))
                layer0(i, False)
                assert ch.k == MARKS0, ch.k
            ch.restart(base + (IT0 - 1) * MARKS0)

            h0 = MOBA_HEADS - 2
            o = [Chunk(0, IT0, j) for j in range(-1, OUT_CHUNKS + 2)]
            gate_of(None, IT0)
            split_lo(o[3])
            soft_scores(0, h0, 0)
            soft_scores(1, h0 + 1, 0)
            inverse_root(1)
            normalise(0, h0)
            normalise(1, h0 + 1)
            split_lo(o[4])
            dve.wait_ge(rb_done, 2)
            for k in range(5):
                if k < 4:
                    scale_tile(ssd_u, k, P_SSD, 1)
                if k:
                    norm_lo(y_hi, y_lo, k - 1, KT)
            for k in range(4, KT + 1):
                if k < KT:
                    scale_tile(ssd_u, k, P_SSD, 1)
                if k > 4:
                    norm_lo(y_hi, y_lo, k - 1, KT)
            split_lo(o[5])
            gated(h0)
            y_low(slice(2 * KT - 2, 2 * KT), IT0)
            for k in range(6, 11):
                split_lo(o[k])
            add_residual(0)
            inverse_root(2)
            apply_norm(xT, P_ODD, 2, hn_hi, hn_lo, 2 * KT)
            layer1(0, True)
            base = ch.base + ch.k
            with dve.Fori(1, IT1) as i:
                ch.restart(i * MARKS1 + (base - MARKS1))
                layer1(i, False)
                assert ch.k == MARKS1, ch.k
            ch.restart(base + (IT1 - 1) * MARKS1)
            h1 = MOBA_HEADS + DIL_HEADS - 2
            o = [Chunk(1, IT1, j) for j in range(-1, OUT_CHUNKS + 2)]
            gate_of(None, IT0 + IT1)
            split_lo(o[3])
            soft_scores(0, h1, 1)
            soft_scores(1, h1 + 1, 1)
            normalise(0, h1)
            normalise(1, h1 + 1)
            split_lo(o[4])
            split_lo(o[5])
            gated(h1)
            y_low(slice(2 * KT - 2, 2 * KT), IT0 + IT1)
            for k in range(6, 9):
                split_lo(o[k])
            add_residual(1)
            inverse_root(3)
            dve.wait_ge(rb_done, 4)
            for k in range(KT):
                scale_tile(xT, k, P_FINAL, 3)


def constants():
    import numpy as np
    con = np.zeros((P, N_CONST), np.float32)
    con[:, C_ID:C_ID + P] = np.eye(P)
    lower = np.triu(np.ones((P, P)))
    con[:, C_TRI:C_TRI + P] = con[:, C_TRI2:C_TRI2 + P] = lower
    con[:, C_ONE:C_ONE + P] = 1.0
    i, j = np.arange(SEQ)[:, None], np.arange(SEQ)[None, :]
    causal = (j <= i).astype(np.float64)
    count = sum(causal * ((i - j) % r == 0) * ((i - j) <= w) for w, r in ((128, 1), (512, 4), (2048, 16)))
    for at, times in ((C_M0, causal), (C_M1, count)):
        m = np.where(times > 0, -np.log(np.maximum(times, 1)), BIG)
        con[:, at:at + P] = m[0:P, 0:P]
        con[:, at + P:at + BLK] = m[P:SEQ, :]
    con[:, C_INV], con[:, C_INV + 1] = 1.0 / D_MODEL, SSD_GROUPS / SSD_INNER
    return con


def kernel(**inputs):
    import numpy as np
    import concourse.bacc as bacc
    from concourse.bass_utils import run_bass_kernel_spmd as run

    a = {k: np.asarray(v) for k, v in inputs.items()}
    w_in, w_out = a["even_w_in"][0], a["even_w_out"][0]
    v_in, v_out = a["odd_w_in"][0], a["odd_w_out"][0]

    def in_chunk(w, c0):
        return w[:, c0:c0 + CW].reshape(KT, P, CW).transpose(1, 0, 2).reshape(P, CF)

    def out_chunk(w, r0):
        return w[r0:r0 + CW].reshape(2, P, D_MODEL).transpose(1, 0, 2).reshape(P, CF)

    z0, x0 = 0, SSD_INNER
    b0 = x0 + SSD_INNER
    c0 = b0 + SSD_GROUPS * SSD_STATE
    dt0 = c0 + SSD_GROUPS * SSD_STATE
    q0 = dt0 + SSD_HEADS
    inner = MOBA_HEADS * HD
    w_all = np.empty((P, N_ALL, CF), np.float32)
    chunks = [in_chunk(w_in, b0), in_chunk(w_in, c0)]
    for i in range(IT0):
        chunks += [in_chunk(w_in, s + i * CW) for s in (x0, z0, q0, q0 + inner, q0 + 2 * inner, q0 + 3 * inner)]
    chunks += [out_chunk(w_out, t * P) for t in OUT_ORDER0]
    for i in range(IT1):
        chunks += [in_chunk(v_in, s * DIL_HEADS * HD + i * CW) for s in range(4)]
    chunks += [out_chunk(v_out, j * CW) for j in range(OUT_CHUNKS)]
    for n, chunk in enumerate(chunks):
        w_all[:, n] = chunk
    w_dt = np.ascontiguousarray(w_in[:, dt0:q0].reshape(KT, P, SSD_HEADS).transpose(1, 0, 2).reshape(P, -1))

    def by_tile(v):
        return v.reshape(-1, P).T

    par = np.zeros((P, N_PAR), np.float32)
    taps = np.concatenate([a["ssd_conv_w"][0], a["ssd_conv_b"][0][None]])
    skip = np.repeat(a["ssd_d"][0], SSD_INNER // SSD_HEADS)
    for n, ch0 in enumerate([SSD_INNER, SSD_INNER + CW] + [i * CW for i in range(IT0)]):
        at = P_CONV + n * CPAR
        par[:, at:at + 2 * (CONV + 1)] = taps[:, ch0:ch0 + CW].reshape(CONV + 1, 2, P).transpose(2, 1, 0).reshape(P, -1)
        if n >= 2:
            par[:, at + 2 * (CONV + 1):at + CPAR] = by_tile(skip[ch0:ch0 + CW])
    for at, v in ((P_EVEN, a["even_norm"][0]), (P_ODD, a["odd_norm"][0]), (P_FINAL, a["final_norm"]),
                  (P_SSD, a["ssd_norm"][0])):
        par[:, at:at + KT] = by_tile(v)
    par[:, P_DTB:P_DTB + NT * SSD_HEADS] = np.tile(a["ssd_dt_bias"][0], NT)
    par[:, P_ALOG:P_ALOG + NT * SSD_HEADS] = np.tile(a["ssd_a_log"][0], NT)
    x_in = np.ascontiguousarray(a["x"][0].T.reshape(KT, P, SEQ).transpose(1, 0, 2))

    nc = bacc.Bacc("TRN2", target_bir_lowering=False, num_devices=1)
    arrays = {"w_all": w_all, "w_dt": w_dt, "x_in": x_in, "par_in": par, "con_in": constants()}
    aps = [nc.dram_tensor(n, v.shape, F32, kind="ExternalInput").ap() for n, v in arrays.items()]
    out = nc.dram_tensor("out", (P, KT, SEQ), F32, kind="ExternalOutput").ap()
    build(nc, *aps, out)
    r = run(nc, [arrays], core_ids=[0])
    return r.results[0]["out"].transpose(1, 0, 2).reshape(D_MODEL, SEQ).T[None]
```

```python
from contextlib import ExitStack

import concourse.bass as bass
from concourse import mybir

P = 128
D_MODEL, SEQ = 1024, 256
KT = D_MODEL // P
NT = SEQ // P
SSD_HEADS, SSD_INNER, SSD_STATE, SSD_GROUPS, CONV = 16, 1024, 128, 2, 4
MOBA_HEADS, DIL_HEADS, HD = 8, 16, 128
IT0, IT1 = MOBA_HEADS // 2, DIL_HEADS // 2
CW = 256
CF = KT * CW
OUT_CHUNKS = 2048 // CW
X, Z, Q0, K0, V0, G0, PER0 = 0, 1, 2, 3, 4, 5, 6
Q1, K1, V1, G1, PER1 = 0, 1, 2, 3, 4
N_PRE = 2
N_OUT0 = N_PRE + PER0 * IT0
N_L1 = N_OUT0 + OUT_CHUNKS
N_OUT1 = N_L1 + PER1 * IT1
N_ALL = N_OUT1 + OUT_CHUNKS
RING0, RING1 = 3, 4
SLOTS1 = [3] + [(N_L1 - RING0 + j) % RING0 for j in range(RING0)]
USED1 = {s: len(range(s, N_L1, RING0)) if s < RING0 else 0 for s in range(RING1)}
OUT_ORDER0 = [8, 10, 12, 0, 2, 4, 6, 14]
ACC_BANKS = [2, 3, 0, 1]
HEADS_PER_IT = SSD_HEADS // IT0
CPAR = 2 * (CONV + 1) + 2
BLK = 3 * P
SCALE = float(HD) ** -0.5
EPS = 1e-5
BIG = 1e30

F32, F32R = mybir.dt.float32, mybir.dt.float32r
ALU, ACT = mybir.AluOpType, mybir.ActivationFunctionType

C_ID, C_TRI, C_ONE, C_TRI2, C_INV = 0, P, 2 * P, 3 * P, 4 * P
C_M0 = C_INV + 2
C_M1 = C_M0 + BLK
N_CONST = C_M1 + BLK
DT0 = 0
CS0 = DT0 + NT * SSD_HEADS
MARKS0, MARKS1 = 12, 2
P_CONV, P_EVEN = 0, (IT0 + 2) * CPAR
P_ODD, P_SSD = P_EVEN + KT, P_EVEN + 2 * KT
P_DTB, P_ALOG = P_EVEN + 3 * KT, P_EVEN + 3 * KT + NT * SSD_HEADS
N_PAR = P_ALOG + NT * SSD_HEADS


class Chunk:

    def __init__(self, layer, i, j):
        if layer == 0 and isinstance(i, int) and N_PRE + PER0 * i + j >= N_L1:
            layer, j, i = 1, N_PRE + PER0 * i + j - N_L1, 0
        self.layer = layer
        if layer == 0:
            self.n = i * PER0 + (N_PRE + j)
            self.slot = (N_PRE + j) % RING0
            self.use = i * (PER0 // RING0) + (N_PRE + j) // RING0
            self.ring = RING0
        else:
            self.n = i * PER1 + (N_L1 + j)
            self.slot = SLOTS1[j % RING1]
            self.use = i + (USED1[self.slot] + j // RING1)
            self.ring = RING1
        self.landed = self.use * 16 + 16
        self.freed = self.n - (self.ring - 1)
        self.waits = not isinstance(self.n, int) or self.freed > 0
        self.exists = not isinstance(self.n, int) or self.n < N_ALL


class Chain:

    def __init__(self, eng, sem):
        self.eng, self.sem, self.base, self.k = eng, sem, 0, 0

    def restart(self, base):
        self.base, self.k = base, 0

    def mark(self, ins):
        ins.then_inc(self.sem, 1)
        self.k += 1
        return self.base + self.k

    def wait(self, mark):
        self.eng.wait_ge(self.sem, mark)


def build(nc, w_all, w_dt, x_in, par_in, con_in, gains_dram, out):
    with ExitStack() as ctx:
        def sb(name, shape, dt=F32):
            return ctx.enter_context(nc.sbuf_tensor(name, shape, dt))

        def sem(name):
            return ctx.enter_context(nc.semaphore(name))

        raw = sb("raw", [P, RING1, CF])
        w_hi = sb("w_hi", [P, RING1, CF], F32R)
        w_lo = sb("w_lo", [P, RING1, CF], F32R)
        xT = sb("xT", [P, KT, SEQ])
        work = sb("work", [P, KT * SEQ])
        sq = work[:].rearrange("p (k t) -> p k t", k=KT)
        m_t = work[:, 0:HEADS_PER_IT * BLK].rearrange("p (h c) -> p h c", h=HEADS_PER_IT)
        xdt = work[:, HEADS_PER_IT * BLK:KT * SEQ].rearrange("p (t c) -> p t c", t=NT)
        hn_hi = sb("hn_hi", [P, KT, SEQ], F32R)
        hn_lo = sb("hn_lo", [P, KT, SEQ], F32R)
        y_hi = sb("y_hi", [P, 2 * KT, SEQ], F32R)
        y_lo = sb("y_lo", [P, 2 * KT, SEQ], F32R)
        xg_hi, xg_lo = y_hi, y_lo
        ssd_u = raw[:, RING1 - 1, :].rearrange("p (k t) -> p k t", k=KT)
        u_sq = sb("u_sq", [P, 2, SEQ])
        g_sum = sb("g_sum", [P, SSD_GROUPS * SEQ])
        con = sb("con", [P, N_CONST])
        par = sb("par", [P, N_PAR])
        tri_r = sb("tri_r", [P, 2 * P], F32R)
        qT = sb("qT", [P, 2, SEQ])
        kT = sb("kT", [P, 2, SEQ])
        v_t = sb("v_t", [P, NT, 2 * HD])
        gate2 = sb("gate2", [P, 2 * SEQ])
        rb = gate2[:, 0:SEQ]
        s_m = sb("s_m", [P, 2, BLK])
        neg_max = sb("neg_max", [P, 2, NT])
        pace = sb("pace", [P, 2])
        p_sum = sb("p_sum", [P, 2, NT])
        p_inv = sb("p_inv", [P, 2, NT])
        pT = sb("pT", [P, 2, BLK])
        conv = sb("conv", [P, 2, SEQ])
        xs = sb("xs", [P, 2, SEQ])
        b_s = sb("b_s", [P, SSD_GROUPS, SEQ])
        c_s = sb("c_s", [P, SSD_GROUPS, SEQ])
        z2 = sb("z2", [P, 2 * SEQ])
        decay = sb("decay", [P, 2, BLK])
        g_m = sb("g_m", [P, IT0, BLK])
        wd = sb("wd", [P, KT * SSD_HEADS])
        wd_hi = sb("wd_hi", [P, KT, SSD_HEADS], F32R)
        wd_lo = sb("wd_lo", [P, KT, SSD_HEADS], F32R)
        NH = NT * SSD_HEADS
        sp = sb("sp", [P, 8, NH])
        dt_rows = pT[0:SSD_HEADS, 0, 0:SEQ]
        dt = sb("dt", [P, NT, SSD_HEADS])
        a_exp = sb("a_exp", [P, NH])
        ac = sb("ac", [P, NH])
        ac_hl = sb("ac_hl", [P, 2, NH], F32R)
        cum_s = sb("cum_s", [P, NH])
        cblk = sb("cblk", [P, SSD_HEADS, 3])
        it_par = sb("it_par", [P, CPAR])
        it_c = sb("it_c", [P, HEADS_PER_IT, 3])
        it_dt = sb("it_dt", [P, NT, HEADS_PER_IT])
        it_ac = sb("it_ac", [P, 2 * NT, HEADS_PER_IT], F32R)
        eps_t = sb("eps_t", [P, 2])
        nv = sb("nv", [P, 5, 4])
        row_ms = sb("row_ms", [P, 4])

        bank = [ctx.enter_context(nc.psum_tensor(f"bank{b}", [P, 512], F32)) for b in range(8)]
        CUM, O_PS, Y_PS, S_PS, T_PS = [bank[2], bank[3]], bank[4], bank[5], bank[6], bank[7]

        D_PS = bank[3]
        ident, tri, ones = con[:, C_ID:C_ID + P], con[:, C_TRI:C_TRI + P], con[:, C_ONE:C_ONE + P]
        causal3 = con[:, C_TRI:C_TRI + BLK]
        mask = [con[:, C_M0:C_M0 + BLK], con[:, C_M1:C_M1 + BLK]]

        par0 = par[:, P_CONV + 2 * CPAR:]
        g_flat = g_m[:].rearrange("p i c -> p (i c)")
        sums = {0: sq[:, 0:1, :], 1: g_sum[:].rearrange("p (g t) -> p g t", g=SSD_GROUPS), 2: sq[:, 2 * ACC_BANKS[0]:2 * ACC_BANKS[0] + 1, :]}
        gains = work[:, 0:D_MODEL]
        squared = work[:, D_MODEL:2 * D_MODEL]
        x_out = xT[:].rearrange("p k t -> p (k t)")

        def w3(t, slot):
            return t[:, slot, :].rearrange("p (k c) -> p k c", k=KT)

        def w_out(t, slot):
            return t[:, slot, :].rearrange("p (r c) -> p r c", r=2)

        landed = [sem(f"landed{s}") for s in range(RING1)]
        x_in_a, x_in_b, par_in_s, wd_in = (
            sem("x_in_a"), sem("x_in_b"), sem("par_landed"), sem("wd_landed"))
        hi_ready, lo_ready = sem("hi_ready"), sem("lo_ready")
        mm_done = sem("mm_done")
        act_evac, dve_evac = sem("act_evac"), sem("dve_evac")
        s_done, s_free = sem("s_done"), sem("s_free")
        exp_done, p_ready = sem("exp_done"), sem("p_ready")
        t_done, t_ready = sem("t_done"), sem("t_ready")
        o_done, yf_ready = sem("o_done"), sem("yf_ready")
        yhi_ready, y_ready = sem("yhi_ready"), sem("y_ready")
        tap_bias, conv_tanh, taps_halved = sem("tap_bias"), sem("conv_tanh"), sem("taps_halved")
        xs_ready, xt_done, xdt_ready = sem("xs_ready"), sem("xt_done"), sem("xdt_ready")
        tanh_z, tanh_g = sem("tanh_z"), sem("tanh_g")
        staged, cum_done, sub_done = sem("staged"), sem("cum_done"), sem("sub_done")
        dec_ready, m_ready, yd_done = sem("dec_ready"), sem("m_ready"), sem("yd_done")
        u_ready = sem("u_ready")
        bc_done, gm_ready = sem("bc_done"), sem("gm_ready")
        dt_mm, dt_abs, dt_exp, ac_ready, cs_done, a_ready, wd_hi_s, wd_ready = (
            sem("dt_mm"), sem("dt_abs"), sem("dt_exp"), sem("ac_ready"), sem("cs_done"),
            sem("a_ready"), sem("wd_hi_ready"), sem("wd_ready"))
        eps_ready = sem("eps_ready")
        bank_sq, sums_ready = sem("bank_sq"), sem("sums_ready")
        ms_done, sd_ready, r_ready = sem("ms_done"), sem("sd_ready"), sem("r_ready")
        row_sq, ms_ready, out_ready = sem("row_sq"), sem("ms_ready"), sem("out_ready")
        first_half, hi_half, lo_half = sem("first_half"), sem("hi_half"), sem("lo_half")
        id_in, mask_in, gains_in = sem("id_landed"), sem("masks_landed"), sem("gains_landed")
        xghi_ready, xg_ready = sem("xghi_ready"), sem("xg_ready")
        rescaled = sem("rescaled")
        rec_ready, pool_chain = sem("rec_ready"), sem("pool_chain")
        dt_copied, dt_flipped, gm_copied = sem("dt_copied"), sem("dt_flipped"), sem("gm_copied")
        rb_done, scaled, hnhi_ready, hn_ready = sem("rb_done"), sem("scaled"), sem("hnhi_ready"), sem("hn_ready")
        acc_done, x_ready = sem("acc_done"), sem("x_ready")
        dve_chain, out_landed = sem("dve_chain"), sem("out_landed")

        block = ctx.enter_context(nc.Block())

        def cols(norm):
            return NT * SSD_GROUPS if norm == 1 else NT

        @block.sync
        def _(sync):
            def load(c):
                if c.waits:
                    sync.wait_ge(lo_ready, c.freed)
                sync.dma_start(raw[:, c.slot, :], w_all[:, bass.ds(c.n, 1), :]).then_inc(landed[c.slot], 16)

            half, first = KT // 2, Chunk(0, 0, -2)
            sync.dma_start(par[:], par_in).then_inc(par_in_s, 16)
            sync.dma_start(xT[:, 0:half, :], x_in[:, 0:half, :]).then_inc(x_in_a, 16)
            sync.dma_start(raw[:, first.slot, 0:CF // 2], w_all[:, first.n, 0:CF // 2]).then_inc(first_half, 16)
            sync.dma_start(xT[:, half:KT, :], x_in[:, half:KT, :]).then_inc(x_in_b, 16)
            sync.dma_start(raw[:, first.slot, CF // 2:], w_all[:, first.n, CF // 2:]).then_inc(
                landed[first.slot], 16)
            sync.dma_start(con[:, 0:C_M0], con_in[:, 0:C_M0]).then_inc(id_in, 16)
            sync.dma_start(wd[:], w_dt).then_inc(wd_in, 16)
            load(Chunk(0, 0, -1))
            load(Chunk(0, 0, 0))
            sync.dma_start(con[:, C_M0:], con_in[:, C_M0:]).then_inc(mask_in, 16)
            for j in range(1, PER0):
                load(Chunk(0, 0, j))
            with sync.Fori(1, IT0) as i:
                for j in range(PER0):
                    load(Chunk(0, i, j))
            for j in range(OUT_CHUNKS):
                load(Chunk(0, IT0, j))
            with sync.Fori(0, IT1) as i:
                for j in range(PER1):
                    load(Chunk(1, i, j))
            sync.wait_ge(hn_ready, 3 * KT)
            sync.dma_start(gains, gains_dram).then_inc(gains_in, 16)
            for j in range(OUT_CHUNKS):
                load(Chunk(1, IT1, j))
            for q in range(4):
                sync.wait_ge(out_ready, q + 1)
                sync.dma_start(out[(q // 2) * P:(q // 2 + 1) * P, (q % 2) * 512:(q % 2 + 1) * 512],
                               x_out[:, q * 512:(q + 1) * 512]).then_inc(out_landed, 16)
            sync.wait_ge(out_landed, 64)

        @block.tensor
        def _(pe):
            def three(ps, a_hi, a_lo, m_hi, m_lo, start, stop, **kw):
                pe.matmul(ps, a_hi, m_hi, start=start, stop=False, **kw)
                pe.matmul(ps, a_hi, m_lo, start=False, stop=False, **kw)
                return pe.matmul(ps, a_lo, m_hi, start=False, stop=stop, **kw)

            def project(c, tile, pb, raw_x=False, order=range(KT), before=lambda n: None):
                cs = slice(tile * P, tile * P + P)
                hi, lo = w3(w_hi, c.slot), w3(w_lo, c.slot)
                m_hi, m_lo = (xg_hi, xg_lo) if raw_x else (hn_hi, hn_lo)
                for n, k in enumerate(order):
                    before(n)
                    last = three(bank[pb][:, tile * SEQ:(tile + 1) * SEQ], hi[:, k, cs], lo[:, k, cs],
                                 m_hi[:, k, :], m_lo[:, k, :], n == 0, n == KT - 1)
                return last

            def project_v(c, t, pb, raw_x=False):
                ts = slice(t * P, t * P + P)
                hi, lo = w3(w_hi, c.slot), w3(w_lo, c.slot)
                m_hi, m_lo = (xg_hi, xg_lo) if raw_x else (hn_hi, hn_lo)
                for k in range(KT):
                    last = three(bank[pb][:, t * CW:(t + 1) * CW], m_hi[:, k, ts], m_lo[:, k, ts],
                                 hi[:, k, :], lo[:, k, :], k == 0, k == KT - 1)
                return last

            def scores(h, count):
                if not (isinstance(count, int) and count == 0):
                    pe.wait_ge(s_free, count)
                pe.matmul(S_PS[:, 0:P], qT[:, h, 0:P], kT[:, h, 0:P], start=True, stop=True)
                pe.matmul(S_PS[:, P:BLK], qT[:, h, P:SEQ], kT[:, h, :], start=True,
                          stop=True).then_inc(s_done, 1)

            def flip(h, count):
                pe.wait_ge(p_ready, count + 1)
                if not (isinstance(count, int) and count == 0):
                    pe.wait_ge(t_ready, count)
                for b in range(3):
                    last = pe.transpose(T_PS[:, b * P:(b + 1) * P], s_m[:, h, b * P:(b + 1) * P], ident)
                last.then_inc(t_done, 1)

            def attend(h, count):
                pe.wait_ge(t_ready, count + 1)
                hs = slice(h * HD, (h + 1) * HD)
                pe.matmul(O_PS[:, h * SEQ:(h + 1) * SEQ], v_t[:, 0, hs], pT[:, h, 0:SEQ],
                          start=True, stop=False)
                pe.matmul(O_PS[:, h * SEQ + P:(h + 1) * SEQ], v_t[:, 1, hs], pT[:, h, SEQ:BLK],
                          start=False, stop=True).then_inc(o_done, 1)

            def mean_squares(norm):
                pe.wait_ge(sums_ready, norm + 1)
                for col in range(cols(norm)):
                    g, t = col // NT, col % NT
                    last = pe.matmul(Y_PS[:, col:col + 1], sums[norm][:, g, t * P:(t + 1) * P],
                                     con[:, C_INV + (norm == 1):C_INV + (norm == 1) + 1], start=True, stop=True)
                last.then_inc(ms_done, 1)

            def spread(norm):
                pe.wait_ge(r_ready, norm + 1)
                for c in range(cols(norm)):
                    last = pe.matmul(Y_PS[:, c * P:(c + 1) * P], nv[:, 3, c:c + 1].to_broadcast([P, P]), ident,
                                     start=True, stop=True)
                last.then_inc(rb_done, 1)

            def cum(h, i):
                n = i * HEADS_PER_IT + h
                if h == 0:
                    pe.wait_ge(staged, i + 1)
                if not (isinstance(n, int) and n < 2):
                    pe.wait_ge(sub_done, n - 1)
                ps = CUM[h % 2]
                for c, cs in ((0, slice(0, P)), (1, slice(P, BLK))):
                    for part in range(2):
                        last = pe.matmul(ps[:, cs], it_ac[:, part * NT + c, h:h + 1].to_broadcast([P, P]),
                                         tri_r[:, 0:cs.stop - cs.start], start=part == 0, stop=part == 1)
                last.then_inc(cum_done, 1)

            def x_to_tokens(i):
                pe.wait_ge(xs_ready, i + 3)
                if isinstance(i, int) and i == 0:
                    pe.wait_ge(gm_ready, 1)
                for t in range(NT):
                    for c in range(2):
                        last = pe.transpose(S_PS[:, t * CW + c * P:t * CW + (c + 1) * P],
                                            xs[:, c, t * P:(t + 1) * P], ident)
                last.then_inc(xt_done, 1)

            def ssd_out(h, i):
                pe.wait_ge(m_ready, i * HEADS_PER_IT + (h + 1))
                if h == 0:
                    pe.wait_ge(xdt_ready, i + 1)
                    if not (isinstance(i, int) and i == 0):
                        pe.wait_ge(u_ready, i)
                rows, c0 = slice(64 * (h % 2), 64 * (h % 2) + 64), (h // 2) * SEQ
                pe.matmul(Y_PS[rows, c0:c0 + SEQ], xdt[:, 0, h * 64:(h + 1) * 64], m_t[:, h, 0:SEQ],
                          start=True, stop=False)
                last = pe.matmul(Y_PS[rows, c0 + P:c0 + SEQ], xdt[:, 1, h * 64:(h + 1) * 64],
                                 m_t[:, h, SEQ:BLK], start=False, stop=True)
                if h == HEADS_PER_IT - 1:
                    last.then_inc(yd_done, 1)

            def bc_scores():
                pe.wait_ge(xs_ready, 2)
                for g, ps in ((0, S_PS), (1, T_PS)):
                    pe.matmul(ps[:, 0:SEQ], b_s[:, g, 0:P], c_s[:, g, :], start=True, stop=True)
                    last = pe.matmul(ps[:, SEQ:BLK], b_s[:, g, P:SEQ], c_s[:, g, P:SEQ], start=True, stop=True)
                last.then_inc(bc_done, 1)

            def layer0(i, first):
                heads = (i - 1) * 2
                c = [Chunk(0, i, j) for j in range(PER0)]
                pe.wait_ge(lo_ready, c[X].n + 1)
                if first:
                    pe.wait_ge(dve_evac, 1)
                else:
                    pe.wait_ge(act_evac, i * 3)
                project(c[X], 0, 0, first)
                if not first:
                    scores(0, heads)
                project(c[X], 1, 0, first).then_inc(mm_done, 1)
                if not first:
                    scores(1, heads + 1)
                pe.wait_ge(lo_ready, c[Z].n + 1)
                pe.wait_ge(dve_evac, i * 3 + 2)
                project(c[Z], 0, 1, first)
                if not first:
                    flip(0, heads)
                    cum(0, i)
                project(c[Z], 1, 1, first).then_inc(mm_done, 1)
                if first:
                    cum_sums()
                    bc_scores()
                else:
                    flip(1, heads + 1)
                    cum(1, i)
                pe.wait_ge(lo_ready, c[Q0].n + 1)
                pe.wait_ge(dve_evac, i * 3 + 3)
                project(c[Q0], 0, 0, before=lambda k: pe.wait_ge(hn_ready, k + 1) if first else None)
                if first:
                    cum(0, i)
                    cum(1, i)
                else:
                    attend(0, heads)
                x_to_tokens(i)
                project(c[Q0], 1, 0).then_inc(mm_done, 1)
                if not first:
                    attend(1, heads + 1)
                cum(2, i)
                pe.wait_ge(lo_ready, c[K0].n + 1)
                pe.wait_ge(dve_evac, i * 3 + 4)
                project(c[K0], 0, 1)
                cum(3, i)
                project(c[K0], 1, 1).then_inc(mm_done, 1)
                pe.wait_ge(lo_ready, c[V0].n + 1)
                pe.wait_ge(act_evac, i * 3 + 1)
                project_v(c[V0], 0, 0)
                ssd_out(0, i)
                ssd_out(1, i)
                project_v(c[V0], 1, 0).then_inc(mm_done, 1)
                ssd_out(2, i)
                ssd_out(3, i)
                pe.wait_ge(lo_ready, c[G0].n + 1)
                pe.wait_ge(act_evac, i * 3 + 2)
                project(c[G0], 0, 1)
                project(c[G0], 1, 1).then_inc(mm_done, 1)

            def layer1(i, first):
                heads = (i - 1) * 2 + MOBA_HEADS
                c = [Chunk(1, i, j) for j in range(PER1)]
                act0 = i * 3 + 3 * IT0
                pe.wait_ge(lo_ready, c[Q1].n + 1)
                if first:
                    order = [2 * b + d for b in ACC_BANKS for d in range(2)]
                    pe.wait_ge(x_ready, 3)
                    project(c[Q1], 0, 0, True, order, lambda n: pe.wait_ge(xg_ready, KT + n + 1))
                    project(c[Q1], 1, 0, True).then_inc(mm_done, 1)
                    mean_squares(2)
                else:
                    pe.wait_ge(act_evac, act0)
                    project(c[Q1], 0, 0)
                    scores(0, heads)
                    project(c[Q1], 1, 0).then_inc(mm_done, 1)
                if not first:
                    scores(1, heads + 1)
                pe.wait_ge(lo_ready, c[K1].n + 1)
                if first:
                    pe.wait_ge(x_ready, 4)
                else:
                    pe.wait_ge(dve_evac, i + (2 + 3 * IT0))
                project(c[K1], 0, 1, first)
                if first:
                    spread(2)
                else:
                    flip(0, heads)
                project(c[K1], 1, 1, first).then_inc(mm_done, 1)
                if not first:
                    flip(1, heads + 1)
                pe.wait_ge(lo_ready, c[V1].n + 1)
                pe.wait_ge(act_evac, act0 + 1)
                project_v(c[V1], 0, 0, first)
                if not first:
                    attend(0, heads)
                project_v(c[V1], 1, 0, first).then_inc(mm_done, 1)
                if not first:
                    attend(1, heads + 1)
                pe.wait_ge(lo_ready, c[G1].n + 1)
                pe.wait_ge(act_evac, act0 + 2)
                project(c[G1], 0, 1, before=lambda k: pe.wait_ge(hn_ready, 2 * KT + k + 1) if first else None)
                project(c[G1], 1, 1).then_inc(mm_done, 1)

            def project_out(j, tiles, c, hooks, y_need):
                pe.wait_ge(lo_ready, c.n + 1)
                pe.wait_ge(y_ready, y_need)
                hi, lo = w_out(w_hi, c.slot), w_out(w_lo, c.slot)
                for nb, b in enumerate(ACC_BANKS):
                    if j == 0 and b == 0:
                        pe.wait_ge(act_evac, 3 * IT0)
                    if j == 0 and b == 1:
                        pe.wait_ge(dve_evac, 2 + 3 * IT0)
                    for d in range(2):
                        ds = slice((2 * b + d) * P, (2 * b + d + 1) * P)
                        for r in range(2):
                            last = three(bank[b][:, d * SEQ:(d + 1) * SEQ], hi[:, r, ds], lo[:, r, ds],
                                         y_hi[:, tiles + r, :], y_lo[:, tiles + r, :],
                                         j == 0 and d == 0 and r == 0, j == OUT_CHUNKS - 1 and r == 1,
                                         skip_group_check=True)
                    if nb == 3:
                        last.then_inc(mm_done, 1)
                    elif j == OUT_CHUNKS - 1:
                        last.then_inc(acc_done, 1)
                    if nb in hooks:
                        hooks[nb]()

            def project_final(j, c, hooks):
                if j == 0:
                    for q, b in enumerate(ACC_BANKS):
                        if b == 0:
                            pe.wait_ge(act_evac, 3 * IT0 + 3 * IT1)
                        if b == 1:
                            pe.wait_ge(dve_evac, 2 + 3 * IT0 + IT1)
                        t, k0 = q // 2, (q % 2) * (KT // 2)
                        for k in range(KT // 2):
                            last = pe.matmul(bank[b][:, k * P:(k + 1) * P], xT[:, k0 + k, t * P:(t + 1) * P],
                                             ident, start=k == 0, stop=False, skip_group_check=True)
                        if q in hooks:
                            hooks[q]()
                pe.wait_ge(lo_ready, c.n + 1)
                pe.wait_ge(y_ready, IT0 + j + 1)
                hi, lo = w_out(w_hi, c.slot), w_out(w_lo, c.slot)
                for q, b in enumerate(ACC_BANKS):
                    ts, ds = slice(q // 2 * P, (q // 2 + 1) * P), slice(q % 2 * 512, (q % 2 + 1) * 512)
                    for r in range(2):
                        last = three(bank[b][:], y_hi[:, 2 * j + r, ts], y_lo[:, 2 * j + r, ts],
                                     hi[:, r, ds], lo[:, r, ds], False, j == OUT_CHUNKS - 1 and r == 1,
                                     skip_group_check=True)
                    if q == 3:
                        last.then_inc(mm_done, 1)
                    elif j == OUT_CHUNKS - 1:
                        last.then_inc(acc_done, 1)
                    if j and q in hooks:
                        hooks[q]()

            def cum_sums():
                pe.wait_ge(ac_ready, 1)
                pe.matmul(D_PS[:, CS0:CS0 + NH], tri, ac[:], start=True, stop=True)
                pe.matmul(D_PS[:, CS0 + NH:CS0 + NH + SSD_HEADS], ones, ac[:, 0:SSD_HEADS],
                          start=True, stop=True).then_inc(cs_done, 1)

            def first_tiles(k):
                pe.wait_ge(xg_ready, k + 1)
                pe.wait_ge(*((lo_half, 1) if k < KT // 2 else (lo_ready, 1)))

            project(Chunk(0, 0, -2), 0, 0, True, before=first_tiles)
            project(Chunk(0, 0, -2), 1, 0, True).then_inc(mm_done, 1)
            pe.wait_ge(id_in, 16)
            mean_squares(0)
            pe.wait_ge(wd_ready, 1)
            for k in range(KT):
                last = three(D_PS[0:SSD_HEADS, 0:SEQ], wd_hi[:, k, :], wd_lo[:, k, :],
                             xg_hi[:, k, :], xg_lo[:, k, :], k == 0, k == KT - 1)
            last.then_inc(dt_mm, 1)
            spread(0)
            pe.wait_ge(lo_ready, 2)
            project(Chunk(0, 0, -1), 0, 1, True)
            pe.wait_ge(dt_copied, 1)
            for t in range(NT):
                last = pe.transpose(D_PS[:, DT0 + t * SSD_HEADS:DT0 + (t + 1) * SSD_HEADS],
                                    dt_rows[:, t * P:(t + 1) * P], ident[0:SSD_HEADS, 0:SSD_HEADS])
            last.then_inc(dt_flipped, 1)
            project(Chunk(0, 0, -1), 1, 1, True).then_inc(mm_done, 1)

            layer0(0, True)
            with pe.Fori(1, IT0) as i:
                layer0(i, False)

            h0 = MOBA_HEADS - 2
            pe.wait_ge(act_evac, 3 * IT0 - 1)
            pe.wait_ge(sub_done, SSD_HEADS)
            hooks = {0: {0: lambda: scores(0, h0), 1: lambda: mean_squares(1), 2: lambda: scores(1, h0 + 1)},
                     1: {1: lambda: flip(0, h0), 3: lambda: (flip(1, h0 + 1), spread(1))},
                     2: {1: lambda: attend(0, h0), 3: lambda: attend(1, h0 + 1)}}
            order = OUT_ORDER0
            for j in range(OUT_CHUNKS):
                if order[j] < KT:
                    pe.wait_ge(hn_ready, KT + order[j] + 2)
                    need = 3
                else:
                    need = order[j] // 2 - 3
                project_out(j, order[j], Chunk(0, IT0, j), hooks.get(j, {}), need)

            layer1(0, True)
            pe.wait_ge(rescaled, 6)
            with pe.Fori(1, IT1) as i:
                layer1(i, False)
            h1 = MOBA_HEADS + DIL_HEADS - 2
            pe.wait_ge(act_evac, 3 * IT0 + 3 * IT1 - 1)
            hooks = {0: {0: lambda: scores(0, h1), 3: lambda: scores(1, h1 + 1)},
                     1: {1: lambda: flip(0, h1), 3: lambda: flip(1, h1 + 1)},
                     2: {1: lambda: attend(0, h1), 3: lambda: attend(1, h1 + 1)}}
            for j in range(OUT_CHUNKS):
                project_final(j, Chunk(1, IT1, j), hooks.get(j, {}))

        @block.scalar
        def _(act):
            def split_hi(c):
                if not c.exists:
                    return
                act.wait_ge(landed[c.slot], c.landed)
                if c.waits:
                    act.wait_ge(mm_done, c.freed)
                act.activation(w_hi[:, c.slot, :], raw[:, c.slot, :], ACT.Copy).then_inc(hi_ready, 1)

            def gained_hi(k, at):
                act.activation(xg_hi[:, k, :], xT[:, k, :], ACT.Copy,
                               scale=par[:, at + k:at + k + 1]).then_inc(xghi_ready, 1)

            def root(norm):
                act.wait_ge(ms_done, norm + 1)
                act.activation(nv[:, 0, 0:cols(norm)], Y_PS[:, 0:cols(norm)], ACT.Sqrt,
                               bias=eps_t[:, (norm == 1):(norm == 1) + 1]).then_inc(sd_ready, 1)

            def norm_hi(dst, base, ks=range(KT)):
                for k in ks:
                    act.wait_ge(scaled, base + k + 1)
                    act.activation(dst[:, k, :], sq[:, k, :], ACT.Copy).then_inc(hnhi_ready, 1)

            def exps(h, count):
                act.wait_ge(s_free, count + 1)
                act.activation(s_m[:, h, 0:P], s_m[:, h, 0:P], ACT.Exp, bias=neg_max[:, h, 0:1], scale=-1.0,
                               accum_out=p_sum[:, h, 0:1])
                act.activation(s_m[:, h, P:BLK], s_m[:, h, P:BLK], ACT.Exp, bias=neg_max[:, h, 1:2], scale=-1.0,
                               accum_out=p_sum[:, h, 1:2]).then_inc(exp_done, 1)

            def take_t(h, count):
                act.wait_ge(t_done, count + 1)
                act.activation(pT[:, h, :], T_PS[:, 0:BLK], ACT.Copy).then_inc(t_ready, 1)

            def conv_start(c, pb, taps):
                if isinstance(c.n, int):
                    act.wait_ge(rescaled, c.n + 1)
                else:
                    act.wait_ge(mm_done, c.n + 1)
                for t in range(2):
                    o = (CONV + 1) * t
                    last = act.activation(conv[:, t, :], bank[pb][:, t * SEQ:(t + 1) * SEQ], ACT.Identity,
                                          bias=taps[:, o + CONV:o + CONV + 1], scale=taps[:, o + 3:o + 4])
                last.then_inc(tap_bias, 1)

            def conv_end(n, dst):
                act.wait_ge(dve_evac, n)
                act.activation(dst[:], conv[:], ACT.Tanh).then_inc(conv_tanh, 1)

            def dec(h, i):
                act.wait_ge(sub_done, i * HEADS_PER_IT + (h + 1))
                act.activation(decay[:, h % 2, :], decay[:, h % 2, :], ACT.Exp).then_inc(dec_ready, 1)

            def y_high(tile, count):
                act.wait_ge(yf_ready, count)
                act.activation(y_hi[:, tile, :], gate2[:].rearrange("p (a t) -> p a t", a=2),
                               ACT.Copy).then_inc(yhi_ready, 1)

            def take(dst, c, pb, scale=1.0):
                act.wait_ge(mm_done, c.n + 1)
                act.activation(dst, bank[pb][:], ACT.Copy, scale=scale).then_inc(act_evac, 1)

            def tanh_of(dst, c, pb, s):
                act.wait_ge(mm_done, c.n + 1)
                act.activation(dst, bank[pb][:], ACT.Tanh, scale=0.5).then_inc(s, 1)

            def flat(t):
                return t[:].rearrange("p a t -> p (a t)")

            def layer0(i, first):
                heads = (i - 1) * 2
                c = [Chunk(0, i, j) for j in range(PER0 + 2)]
                prev = Chunk(0, i, -1)
                if first:
                    act.wait_ge(xs_ready, 1)
                    conv_start(prev, 1, par[:, P_CONV + CPAR:P_CONV + 2 * CPAR])
                    split_hi(c[X + 2])
                    conv_end(2, c_s)
                    norm_hi(hn_hi, 0, range(KT // 2, KT))
                else:
                    act.wait_ge(u_ready, i)
                    tanh_of(gate2[:], prev, 1, tanh_g)
                    split_hi(c[X + 2])
                    exps(0, heads)
                if not first:
                    act.wait_ge(staged, i + 1)
                act.wait_ge(xs_ready, i + 2)
                conv_start(c[X], 0, par0 if first else it_par)
                if not first:
                    exps(1, heads + 1)
                    take_t(0, heads)
                conv_end(i * 3 + 3, xs)
                split_hi(c[Z + 2])
                dec(0, i)
                if first:
                    act.wait_ge(rescaled, c[Z].n + 1)
                tanh_of(z2[:], c[Z], 1, tanh_z)
                if not first:
                    take_t(1, heads + 1)
                dec(1, i)
                split_hi(c[Q0 + 2])
                dec(2, i)
                if not first:
                    act.wait_ge(s_done, heads + 2)
                take(flat(qT), c[Q0], 0, -SCALE)
                if not first:
                    y_high(bass.ds(i * 2 + (KT - 2), 2), i)
                split_hi(c[K0 + 2])
                dec(3, i)
                take(flat(kT), c[K0], 1)
                split_hi(c[V0 + 2])
                if not first:
                    act.wait_ge(o_done, heads + 2)
                take(flat(v_t), c[V0], 0)
                split_hi(c[G0 + 2])

            def layer1(i, first):
                heads = (i - 1) * 2 + MOBA_HEADS
                c = [Chunk(1, i, j) for j in range(PER1 + 2)]
                prev = Chunk(1, i, -1)
                if not first:
                    act.wait_ge(y_ready, i + (IT0 - 1))
                    tanh_of(gate2[:], prev, 1, tanh_g)
                split_hi(c[Q1 + 2])
                if first:
                    root(2)
                    act.preload_act_table(ACT.Exp)
                else:
                    exps(0, heads)
                    act.wait_ge(s_done, heads + 2)
                take(flat(qT), c[Q1], 0, -SCALE)
                if not first:
                    exps(1, heads + 1)
                split_hi(c[K1 + 2])
                if first:
                    norm_hi(hn_hi, 2 * KT)
                else:
                    take_t(0, heads)
                take(flat(kT), c[K1], 1)
                if not first:
                    take_t(1, heads + 1)
                split_hi(c[V1 + 2])
                if first:
                    act.wait_ge(mm_done, c[V1].n + 1)
                    for t in range(NT):
                        last = act.activation(v_t[:, t, :], bank[0][:, t * CW:(t + 1) * CW], ACT.Copy,
                                              scale=nv[:, 3, t:t + 1])
                    last.then_inc(act_evac, 1)
                else:
                    act.wait_ge(o_done, heads + 2)
                    take(flat(v_t), c[V1], 0)
                split_hi(c[G1 + 2])
                if not first:
                    y_high(bass.ds(i * 2 - 2, 2), i + IT0)

            act.preload_act_table(ACT.Sqrt)
            first, half = Chunk(0, 0, -2), KT // 2
            act.wait_ge(par_in_s, 16)
            act.wait_ge(x_in_a, 16)
            for k in range(half):
                gained_hi(k, P_EVEN)
            act.wait_ge(first_half, 16)
            act.activation(w_hi[:, first.slot, 0:CF // 2], raw[:, first.slot, 0:CF // 2],
                           ACT.Copy).then_inc(hi_half, 1)
            act.wait_ge(x_in_b, 16)
            for k in range(half, KT):
                gained_hi(k, P_EVEN)
            act.wait_ge(landed[first.slot], first.landed)
            act.activation(w_hi[:, first.slot, CF // 2:], raw[:, first.slot, CF // 2:],
                           ACT.Copy).then_inc(hi_ready, 1)
            act.wait_ge(id_in, 16)
            for t in range(2):
                last = act.activation(tri_r[:, t * P:(t + 1) * P], tri, ACT.Copy)
            act.wait_ge(wd_in, 16)
            act.activation(wd_hi[:], wd[:].rearrange("p (k h) -> p k h", k=KT), ACT.Copy).then_inc(wd_hi_s, 1)
            split_hi(Chunk(0, 0, -1))
            split_hi(Chunk(0, 0, X))
            act.wait_ge(eps_ready, 1)
            root(0)
            act.preload_act_table(ACT.Exp)
            act.activation(a_exp[:], par[:, P_ALOG:P_ALOG + NH], ACT.Exp).then_inc(a_ready, 1)
            act.wait_ge(dt_mm, 1)
            act.activation(dt_rows, D_PS[0:SSD_HEADS, 0:SEQ], ACT.Copy).then_inc(dt_copied, 1)
            act.wait_ge(taps_halved, 1)
            conv_start(Chunk(0, 0, -2), 0, par[:, P_CONV:P_CONV + CPAR])
            norm_hi(hn_hi, 0, range(KT // 2))
            split_hi(Chunk(0, 0, Z))
            act.wait_ge(dt_abs, 1)
            act.activation(sp[:, 2, :], sp[:, 1, :], ACT.Exp, scale=-1.0).then_inc(dt_exp, 1)
            conv_end(1, b_s)

            layer0(0, True)
            with act.Fori(1, IT0) as i:
                layer0(i, False)

            h0 = MOBA_HEADS - 2
            o = [Chunk(0, IT0, j) for j in range(-1, OUT_CHUNKS + 2)]
            act.wait_ge(u_ready, IT0)
            tanh_of(gate2[:], o[0], 1, tanh_g)
            split_hi(o[3])
            exps(0, h0)
            exps(1, h0 + 1)
            root(1)
            split_hi(o[4])
            take_t(0, h0)
            take_t(1, h0 + 1)
            for k in range(4):
                act.wait_ge(scaled, KT + k + 1)
                act.activation(y_hi[:, k, :], sq[:, k, :], ACT.Copy).then_inc(hnhi_ready, 1)
            split_hi(o[5])
            for k in range(4, KT):
                act.wait_ge(scaled, KT + k + 1)
                act.activation(y_hi[:, k, :], sq[:, k, :], ACT.Copy).then_inc(hnhi_ready, 1)
            y_high(slice(2 * KT - 2, 2 * KT), IT0)
            split_hi(o[6])
            split_hi(o[7])
            split_hi(o[8])
            split_hi(o[9])
            split_hi(o[10])
            act.preload_act_table(ACT.Sqrt)
            for k, b in enumerate(ACC_BANKS):
                act.wait_ge(x_ready, k + 1)
                for d in range(2):
                    gained_hi(2 * b + d, P_ODD)
                act.activation(sq[:, 2 * b:2 * b + 2, :], xT[:, 2 * b:2 * b + 2, :], ACT.Square).then_inc(bank_sq, 1)
            layer1(0, True)
            act.wait_ge(rescaled, 6)
            with act.Fori(1, IT1) as i:
                layer1(i, False)
            h1 = MOBA_HEADS + DIL_HEADS - 2
            o = [Chunk(1, IT1, j) for j in range(-1, OUT_CHUNKS + 2)]
            act.wait_ge(y_ready, IT0 + IT1 - 1)
            tanh_of(gate2[:], o[0], 1, tanh_g)
            split_hi(o[3])
            exps(0, h1)
            exps(1, h1 + 1)
            split_hi(o[4])
            take_t(0, h1)
            take_t(1, h1 + 1)
            split_hi(o[5])
            y_high(slice(2 * KT - 2, 2 * KT), IT0 + IT1)
            for k in range(6, 9):
                split_hi(o[k])
            act.preload_act_table(ACT.Sqrt)
            for q, b in enumerate(ACC_BANKS):
                act.wait_ge(*((acc_done, 3 + q + 1) if q < 3 else (mm_done, N_ALL)))
                act.activation(squared[:, q % 2 * 512:(q % 2 + 1) * 512], bank[b][:], ACT.Square, accum_out=row_ms[:, q:q + 1]).then_inc(row_sq, 1)
                if q % 2:
                    t = q // 2
                    act.wait_ge(ms_ready, t + 1)
                    act.activation(nv[:, 0, t:t + 1], nv[:, 1, t:t + 1], ACT.Sqrt).then_inc(sd_ready, 1)

        @block.vector
        def _(dve):
            ch = Chain(dve, dve_chain)

            def split_lo(c):
                if not c.exists:
                    return
                dve.wait_ge(hi_ready, c.n + 1)
                dve.tensor_tensor(w_lo[:, c.slot, :], raw[:, c.slot, :], w_hi[:, c.slot, :].bitcast(F32),
                                  ALU.subtract).then_inc(lo_ready, 1)

            def inverse_root(norm):
                n = slice(0, cols(norm))
                dve.wait_ge(sd_ready, norm + 1)
                ch.mark(dve.tensor_scalar(nv[:, 1, n], Y_PS[:, n], 4 * EPS if norm == 1 else EPS, None, ALU.add))
                newton(n)

            def newton(n):
                b = ch.mark(dve.reciprocal(nv[:, 2, n], nv[:, 0, n]))
                ch.wait(b)
                b = ch.mark(dve.tensor_tensor(nv[:, 4, n], nv[:, 2, n], nv[:, 2, n], ALU.mult))
                ch.wait(b)
                b = ch.mark(dve.tensor_tensor(nv[:, 4, n], nv[:, 4, n], nv[:, 1, n], ALU.mult))
                ch.wait(b)
                b = ch.mark(dve.tensor_scalar(nv[:, 4, n], nv[:, 4, n], -0.5, 1.5, ALU.mult, ALU.add))
                ch.wait(b)
                dve.tensor_tensor(nv[:, 3, n], nv[:, 2, n], nv[:, 4, n], ALU.mult).then_inc(r_ready, 1)

            def scale_tile(src, k, gains, norm):
                g = (k // 4) * SEQ if norm == 1 else 0
                dve.scalar_tensor_tensor(out=sq[:, k, :], in0=src[:, k, :], scalar=par[:, gains + k:gains + k + 1],
                                         in1=Y_PS[:, g:g + SEQ], op0=ALU.mult, op1=ALU.mult).then_inc(scaled, 1)

            def norm_lo(dst_hi, dst_lo, k, base):
                dve.wait_ge(hnhi_ready, base + k + 1)
                dve.tensor_tensor(dst_lo[:, k, :], sq[:, k, :], dst_hi[:, k, :].bitcast(F32),
                                  ALU.subtract).then_inc(hn_ready, 1)

            def gained_lo(k, at, n):
                dve.wait_ge(xghi_ready, n)
                dve.scalar_tensor_tensor(out=xg_lo[:, k, :], in0=xT[:, k, :], scalar=par[:, at + k:at + k + 1],
                                         in1=xg_hi[:, k, :].bitcast(F32), op0=ALU.mult,
                                         op1=ALU.subtract).then_inc(xg_ready, 1)

            def take_rb(norm):
                dve.wait_ge(rb_done, norm + 1)
                ch.wait(ch.mark(dve.tensor_copy(rb, Y_PS[:, 0:SEQ])))

            def rescale(ap):
                dve.tensor_tensor(ap, ap, rb.unsqueeze(1).to_broadcast([P, 2, SEQ]), ALU.mult).then_inc(rescaled, 1)

            def rescale_bank(c, pb):
                dve.wait_ge(mm_done, c.n + 1)
                rescale(bank[pb][:].rearrange("p (a t) -> p a t", a=2))

            def soft_scores(h, count, layer):
                dve.wait_ge(s_done, count + 1)
                dve.memset(pace[:, h:h + 1], 0.0)
                for t, cs in ((0, slice(0, P)), (1, slice(P, BLK))):
                    last = dve.tensor_tensor_reduce(s_m[:, h, cs], S_PS[:, cs], mask[layer][:, cs], 1.0, BIG,
                                                    ALU.add, ALU.min, neg_max[:, h, t:t + 1])
                last.then_inc(s_free, 1)

            def normalise(h, count):
                dve.wait_ge(exp_done, count + 1)
                ch.wait(ch.mark(dve.reciprocal(p_inv[:, h, :], p_sum[:, h, :])))
                for t, cs in ((0, slice(0, P)), (1, slice(P, BLK))):
                    last = dve.tensor_scalar(s_m[:, h, cs], s_m[:, h, cs], p_inv[:, h, t:t + 1], None, ALU.mult)
                last.then_inc(p_ready, 1)

            def gate_of(c, count):
                dve.wait_ge(tanh_g, count)
                dve.scalar_tensor_tensor(out=gate2[:], in0=gate2[:], scalar=1.0, in1=bank[1][:], op0=ALU.add,
                                         op1=ALU.mult).then_inc(dve_evac, 1)

            def gated(heads):
                dve.wait_ge(o_done, heads + 2)
                dve.scalar_tensor_tensor(out=gate2[:], in0=O_PS[:], scalar=0.5, in1=gate2[:], op0=ALU.mult,
                                         op1=ALU.mult).then_inc(yf_ready, 1)

            def y_low(tile, count):
                dve.wait_ge(yhi_ready, count)
                dve.tensor_tensor(y_lo[:, tile, :], gate2[:].rearrange("p (a t) -> p a t", a=2),
                                  y_hi[:, tile, :].bitcast(F32), ALU.subtract).then_inc(y_ready, 1)

            def conv_taps(n, pb, taps):
                dve.wait_ge(tap_bias, n)
                marks = [None, None]
                for k in range(CONV - 1):
                    shift = CONV - 1 - k
                    for t in range(2):
                        o = (CONV + 1) * t
                        if k:
                            ch.wait(marks[t])
                        last = dve.scalar_tensor_tensor(
                            out=conv[:, t, shift:], in0=bank[pb][:, t * SEQ:(t + 1) * SEQ - shift],
                            scalar=taps[:, o + k:o + k + 1], in1=conv[:, t, shift:], op0=ALU.mult, op1=ALU.add)
                        if k < CONV - 2:
                            marks[t] = ch.mark(last)
                last.then_inc(dve_evac, 1)

            def conv_silu(n, dst):
                dve.wait_ge(conv_tanh, n)
                dve.scalar_tensor_tensor(out=dst, in0=dst, scalar=1.0, in1=conv[:], op0=ALU.add,
                                         op1=ALU.mult).then_inc(xs_ready, 1)

            def sub(h, i):
                if not (isinstance(i, int) and i * HEADS_PER_IT + h < 2):
                    dve.wait_ge(m_ready, i * HEADS_PER_IT + (h - 1))
                dve.wait_ge(cum_done, i * HEADS_PER_IT + (h + 1))
                three = CUM[h % 2][:, 0:BLK].rearrange("p (b l) -> p b l", b=3)
                ch.wait(ch.mark(dve.tensor_tensor(decay[:, h % 2, :].rearrange("p (b l) -> p b l", b=3), three,
                                                  it_c[:, h, :].unsqueeze(2).to_broadcast([P, 3, P]),
                                                  ALU.subtract)))
                dve.tensor_scalar(decay[:, h % 2, :], decay[:, h % 2, :], 0.0, None,
                                  ALU.min).then_inc(sub_done, 1)

            def weigh(h, i):
                dve.wait_ge(dec_ready, i * HEADS_PER_IT + (h + 1))
                dve.tensor_tensor(m_t[:, h, :], decay[:, h % 2, :], g_flat[:, bass.ds(i * BLK, BLK)],
                                  ALU.mult).then_inc(m_ready, 1)

            def stage(i):
                if not (isinstance(i, int) and i == 0):
                    dve.wait_ge(cum_done, i * HEADS_PER_IT)
                hs = bass.ds(i * HEADS_PER_IT, HEADS_PER_IT)
                dve.tensor_copy(it_par[:], par[:, bass.ds(i * CPAR + (P_CONV + 2 * CPAR), CPAR)])
                dve.tensor_copy(it_c[:], cblk[:, hs, :])
                dve.tensor_copy(it_dt[:], dt[:, :, hs])
                dve.tensor_copy(it_ac[:], ac_hl[:].bitcast(F32).rearrange("p a (c h) -> p (a c) h", c=NT)
                                [:, :, hs]).then_inc(staged, 1)
                dve.wait_ge(staged, i + 1)

            def layer0(i, first):
                heads = (i - 1) * 2
                c = [Chunk(0, i, j) for j in range(PER0 + 2)]
                if first:
                    conv_taps(2, 1, par[:, P_CONV + CPAR:])
                    split_lo(c[X + 2])
                    conv_silu(2, c_s[:])
                    rescale_bank(c[X], 0)
                    for k in range(KT // 2, KT):
                        scale_tile(xT, k, P_EVEN, 0)
                    conv_taps(i + 3, 0, par0)
                    rescale_bank(c[Z], 1)
                    conv_silu(i + 3, xs[:])
                    prepare_cum()
                    stage(i)
                    prepare_gm()
                    split_lo(c[Z + 2])
                    sub(0, i)
                    sub(1, i)
                    dve.wait_ge(hn_ready, KT)
                else:
                    gate_of(None, i)
                    stage(i)
                    soft_scores(0, heads, 0)
                    split_lo(c[X + 2])
                    normalise(0, heads)
                    soft_scores(1, heads + 1, 0)
                    conv_taps(i + 3, 0, it_par)
                    normalise(1, heads + 1)
                    sub(0, i)
                    conv_silu(i + 3, xs[:])
                    split_lo(c[Z + 2])
                    sub(1, i)
                weigh(0, i)
                dve.wait_ge(tanh_z, i + 1)
                dve.scalar_tensor_tensor(out=z2[:], in0=z2[:], scalar=1.0, in1=bank[1][:], op0=ALU.add,
                                         op1=ALU.mult).then_inc(dve_evac, 1)
                dve.wait_ge(xt_done, i + 1)
                dve.tensor_tensor(xdt.rearrange("p t (h c) -> p (t h) c", h=HEADS_PER_IT),
                                  S_PS[:].rearrange("p (a c) -> p a c", c=64),
                                  it_dt[:].rearrange("p t h -> p (t h)").unsqueeze(2)
                                  .to_broadcast([P, NT * HEADS_PER_IT, 64]), ALU.mult).then_inc(xdt_ready, 1)
                weigh(1, i)
                sub(2, i)
                split_lo(c[Q0 + 2])
                if not first:
                    gated(heads)
                sub(3, i)
                weigh(2, i)
                split_lo(c[K0 + 2])
                weigh(3, i)
                if not first:
                    y_low(bass.ds(i * 2 + (KT - 2), 2), i)
                split_lo(c[V0 + 2])
                dve.wait_ge(yd_done, i + 1)
                for t in range(2):
                    m = ch.mark(dve.scalar_tensor_tensor(
                        out=xs[:, t, :], in0=xs[:, t, :], scalar=it_par[:, 2 * (CONV + 1) + t:2 * (CONV + 1) + t + 1],
                        in1=Y_PS[:, t * SEQ:(t + 1) * SEQ], op0=ALU.mult, op1=ALU.add))
                ch.wait(m)
                dve.tensor_tensor(ssd_u[:, bass.ds(i * 2, 2), :], xs[:], z2[:].rearrange("p (a t) -> p a t", a=2),
                                  ALU.mult).then_inc(u_ready, 1)
                split_lo(c[G0 + 2])

            def layer1(i, first):
                heads = (i - 1) * 2 + MOBA_HEADS
                c = [Chunk(1, i, j) for j in range(PER1 + 2)]
                if not first:
                    gate_of(None, i + IT0)
                    soft_scores(0, heads, 1)
                split_lo(c[Q1 + 2])
                if first:
                    inverse_root(2)
                    take_rb(2)
                    for k in range(KT):
                        scale_tile(xT, k, P_ODD, 2)
                else:
                    normalise(0, heads)
                    soft_scores(1, heads + 1, 1)
                    normalise(1, heads + 1)
                split_lo(c[K1 + 2])
                split_lo(c[V1 + 2])
                if first:
                    dve.wait_ge(act_evac, 3 * IT0 + 1)
                    rescale(qT[:])
                    dve.wait_ge(act_evac, 3 * IT0 + 2)
                    rescale(kT[:])
                else:
                    gated(heads)
                split_lo(c[G1 + 2])
                if not first:
                    y_low(bass.ds(i * 2 - 2, 2), i + IT0)

            def prepare_cum():
                dve.wait_ge(cs_done, 1)
                H = SSD_HEADS
                ch.wait(ch.mark(dve.tensor_copy(cum_s[:], D_PS[:, CS0:CS0 + NH])))
                dve.tensor_copy(cblk[:, :, 0:1], cum_s[:, 0:H].unsqueeze(2))
                dve.tensor_tensor(cblk[:, :, 1:2], cum_s[:, 0:H].unsqueeze(2),
                                  D_PS[:, CS0 + NH:CS0 + NH + H].unsqueeze(2), ALU.subtract)
                ch.wait(ch.mark(dve.tensor_copy(cblk[:, :, 2:3], cum_s[:, H:2 * H].unsqueeze(2))))

            def prepare_gm():
                dve.wait_ge(bc_done, 1)
                for g, ps in ((0, S_PS), (1, T_PS)):
                    last = dve.tensor_tensor(g_m[:, g * (IT0 // SSD_GROUPS), :], ps[:, 0:BLK], causal3, ALU.mult)
                last.then_inc(gm_ready, 1)
                dve.wait_ge(gm_ready, 1)

            def add_residual():
                def low(k):
                    for d in range(2):
                        gained_lo(2 * ACC_BANKS[k] + d, P_ODD, KT + 2 * k + d + 1)

                for k, b in enumerate(ACC_BANKS):
                    if k < 3:
                        dve.wait_ge(acc_done, k + 1)
                    else:
                        dve.wait_ge(mm_done, N_L1)
                    x2 = xT[:, 2 * b:2 * b + 2, :]
                    dve.tensor_tensor(x2, bank[b][:].rearrange("p (a t) -> p a t", a=2), x2,
                                      ALU.add).then_inc(x_ready, 1)
                    if k:
                        low(k - 1)
                dve.wait_ge(x_ready, 4)
                low(3)

            dve.memset(eps_t[:, 0:1], EPS)
            dve.memset(eps_t[:, 1:2], 4 * EPS).then_inc(eps_ready, 1)
            dve.wait_ge(eps_ready, 1)
            slot = Chunk(0, 0, -2).slot
            for half, hi_sem, lo_sem in ((0, hi_half, lo_half), (1, hi_ready, lo_ready)):
                for k in range(half * (KT // 2), (half + 1) * (KT // 2)):
                    gained_lo(k, P_EVEN, k + 1)
                cs = slice(half * (CF // 2), (half + 1) * (CF // 2))
                dve.wait_ge(hi_sem, 1)
                dve.tensor_tensor(w_lo[:, slot, cs], raw[:, slot, cs], w_hi[:, slot, cs].bitcast(F32),
                                  ALU.subtract).then_inc(lo_sem, 1)
            split_lo(Chunk(0, 0, -1))
            inverse_root(0)
            take_rb(0)
            rescale_bank(Chunk(0, 0, -2), 0)
            for k in range(KT // 2):
                scale_tile(xT, k, P_EVEN, 0)
            dve.wait_ge(taps_halved, 1)
            conv_taps(1, 0, par[:, P_CONV:])
            dve.wait_ge(dt_flipped, 1)
            v, mag, e, s = (sp[:, k, :] for k in range(4))
            for t in range(NT):
                hs = slice(t * SSD_HEADS, (t + 1) * SSD_HEADS)
                m = ch.mark(dve.scalar_tensor_tensor(out=v[:, hs], in0=D_PS[:, DT0 + hs.start:DT0 + hs.stop],
                                                     scalar=nv[:, 3, t:t + 1],
                                                     in1=par[:, P_DTB + hs.start:P_DTB + hs.stop],
                                                     op0=ALU.mult, op1=ALU.add))
            ch.wait(m)
            dve.scalar_tensor_tensor(out=mag, in0=v, scalar=-1.0, in1=v, op0=ALU.mult,
                                     op1=ALU.max).then_inc(dt_abs, 1)
            rescale_bank(Chunk(0, 0, -1), 1)
            dve.wait_ge(dt_exp, 1)
            ch.wait(ch.mark(dve.tensor_scalar(s, e, 2.0, None, ALU.add)))
            dve.reciprocal(s, s).then_inc(rec_ready, 1)
            conv_silu(1, b_s[:])
            dve.wait_ge(lo_ready, Chunk(0, 0, X).n + 1)
            split_lo(Chunk(0, 0, Z))

            layer0(0, True)
            dve.wait_ge(gm_copied, 1)
            dve.wait_ge(mask_in, 16)
            base = ch.base + ch.k
            with dve.Fori(1, IT0) as i:
                ch.restart(i * MARKS0 + (base - MARKS0))
                layer0(i, False)
                assert ch.k == MARKS0, ch.k
            ch.restart(base + (IT0 - 1) * MARKS0)

            h0 = MOBA_HEADS - 2
            o = [Chunk(0, IT0, j) for j in range(-1, OUT_CHUNKS + 2)]
            gate_of(None, IT0)
            soft_scores(0, h0, 0)
            soft_scores(1, h0 + 1, 0)
            split_lo(o[3])
            normalise(0, h0)
            normalise(1, h0 + 1)
            inverse_root(1)
            split_lo(o[4])
            dve.wait_ge(rb_done, 2)
            for k in range(5):
                if k < 4:
                    scale_tile(ssd_u, k, P_SSD, 1)
                if k:
                    norm_lo(y_hi, y_lo, k - 1, KT)
            for k in range(4, KT + 1):
                if k < KT:
                    scale_tile(ssd_u, k, P_SSD, 1)
                if k > 4:
                    norm_lo(y_hi, y_lo, k - 1, KT)
            split_lo(o[5])
            gated(h0)
            y_low(slice(2 * KT - 2, 2 * KT), IT0)
            for k in range(6, 11):
                split_lo(o[k])
            add_residual()
            layer1(0, True)
            base = ch.base + ch.k
            with dve.Fori(1, IT1) as i:
                ch.restart(i * MARKS1 + (base - MARKS1))
                layer1(i, False)
                assert ch.k == MARKS1, ch.k
            ch.restart(base + (IT1 - 1) * MARKS1)
            h1 = MOBA_HEADS + DIL_HEADS - 2
            o = [Chunk(1, IT1, j) for j in range(-1, OUT_CHUNKS + 2)]
            gate_of(None, IT0 + IT1)
            soft_scores(0, h1, 1)
            soft_scores(1, h1 + 1, 1)
            split_lo(o[3])
            normalise(0, h1)
            normalise(1, h1 + 1)
            split_lo(o[4])
            split_lo(o[5])
            gated(h1)
            y_low(slice(2 * KT - 2, 2 * KT), IT0 + IT1)
            for k in range(6, 9):
                split_lo(o[k])
            dve.wait_ge(gains_in, 16)
            for t in range(NT):
                n = slice(t, t + 1)
                dve.wait_ge(row_sq, 2 * t + 2)
                m = ch.mark(dve.tensor_tensor(nv[:, 4, n], row_ms[:, 2 * t:2 * t + 1],
                                              row_ms[:, 2 * t + 1:2 * t + 2], ALU.add))
                ch.wait(m)
                dve.tensor_scalar(nv[:, 1, n], nv[:, 4, n], 1.0 / D_MODEL, EPS, ALU.mult, ALU.add).then_inc(ms_ready, 1)
                dve.wait_ge(sd_ready, 3 + t + 1)
                newton(n)
                dve.wait_ge(r_ready, 3 + t + 1)
                for h in range(2):
                    q = 2 * t + h
                    dve.scalar_tensor_tensor(out=x_out[:, q * 512:(q + 1) * 512], in0=bank[ACC_BANKS[q]][:],
                                             scalar=nv[:, 3, n], in1=gains[:, h * 512:(h + 1) * 512],
                                             op0=ALU.mult, op1=ALU.mult).then_inc(out_ready, 1)

        @block.gpsimd
        def _(pool):
            ch = Chain(pool, pool_chain)

            def in_turn(ins):
                ch.wait(ch.mark(ins))

            def squares(dst, src):
                in_turn(pool.tensor_tensor(dst, src, src, ALU.mult))

            def add(dst, a, b):
                return pool.tensor_tensor(dst, a, b, ALU.add)

            def norm_lo(base, ks=range(KT)):
                for k in ks:
                    pool.wait_ge(hnhi_ready, base + k + 1)
                    pool.tensor_tensor(hn_lo[:, k, :], sq[:, k, :], hn_hi[:, k, :].bitcast(F32),
                                       ALU.subtract).then_inc(hn_ready, 1)

            half = KT // 2
            pool.wait_ge(x_in_a, 16)
            squares(sq[:, 0:half, :], xT[:, 0:half, :])
            pool.wait_ge(x_in_b, 16)
            squares(sq[:, half:KT, :], xT[:, half:KT, :])
            in_turn(add(sq[:, 0:4, :], sq[:, 0:4, :], sq[:, 4:8, :]))
            in_turn(add(sq[:, 0:2, :], sq[:, 0:2, :], sq[:, 2:4, :]))
            add(sq[:, 0, :], sq[:, 0, :], sq[:, 1, :]).then_inc(sums_ready, 1)
            pool.wait_ge(wd_hi_s, 1)
            pool.tensor_tensor(wd_lo[:], wd[:].rearrange("p (k h) -> p k h", k=KT), wd_hi[:].bitcast(F32),
                               ALU.subtract).then_inc(wd_ready, 1)
            cp = par[:, P_CONV:P_CONV + (IT0 + 2) * CPAR].rearrange("p (n c) -> p n c", c=CPAR)
            cp = cp[:, :, 0:2 * (CONV + 1)]
            pool.wait_ge(par_in_s, 16)
            pool.tensor_scalar(cp, cp, 0.5, None, ALU.mult).then_inc(taps_halved, 1)
            c = Chunk(0, 0, X)
            pool.wait_ge(hi_ready, c.n + 1)
            pool.wait_ge(lo_ready, c.n)
            pool.tensor_tensor(w_lo[:, c.slot, :], raw[:, c.slot, :], w_hi[:, c.slot, :].bitcast(F32),
                               ALU.subtract).then_inc(lo_ready, 1)
            norm_lo(0, range(KT // 2))

            v, e, s, z, zz, acc = (sp[:, k, :] for k in (0, 2, 3, 4, 5, 6))
            pool.wait_ge(rec_ready, 1)
            in_turn(pool.tensor_tensor(z, e, s, ALU.mult))
            in_turn(pool.tensor_tensor(zz, z, z, ALU.mult))
            in_turn(pool.tensor_scalar(acc, zz, 1.0 / 17, None, ALU.mult))
            for odd in (15, 13, 11, 9, 7, 5, 3):
                in_turn(pool.tensor_scalar(acc, acc, 1.0 / odd, None, ALU.add))
                in_turn(pool.tensor_tensor(acc, acc, zz, ALU.mult))
            in_turn(pool.tensor_scalar(acc, acc, 1.0, 2.0, ALU.add, ALU.mult))
            in_turn(pool.tensor_tensor(acc, acc, z, ALU.mult))
            in_turn(pool.tensor_scalar(v, v, 0.0, None, ALU.max))
            d = dt[:].rearrange("p t h -> p (t h)")
            in_turn(pool.tensor_tensor(d, acc, v, ALU.add))
            pool.wait_ge(a_ready, 1)
            in_turn(pool.tensor_tensor(ac[:], d, a_exp[:], ALU.mult))
            in_turn(pool.tensor_scalar(ac[:], ac[:], -1.0, None, ALU.mult))
            in_turn(pool.tensor_scalar(ac_hl[:, 0, :], ac[:], 1.0, None, ALU.mult))
            pool.tensor_tensor(ac_hl[:, 1, :], ac[:], ac_hl[:, 0, :].bitcast(F32),
                               ALU.subtract).then_inc(ac_ready, 1)
            norm_lo(0, range(KT // 2, KT))
            per = IT0 // SSD_GROUPS
            pool.wait_ge(gm_ready, 1)
            for i in range(IT0):
                if i % per:
                    last = pool.tensor_copy(g_m[:, i, :], g_m[:, i - i % per, :])
            last.then_inc(gm_copied, 1)

            for i in range(IT0):
                g, a = i // per, i % per
                acc = g_sum[:, g * SEQ:(g + 1) * SEQ]
                pool.wait_ge(u_ready, i + 1)
                squares(u_sq[:], ssd_u[:, 2 * i:2 * i + 2, :])
                both = u_sq[:, 0, :] if a else acc
                in_turn(add(both, u_sq[:, 0, :], u_sq[:, 1, :]))
                if i == IT0 - 1:
                    add(acc, acc, both).then_inc(sums_ready, 1)
                elif a:
                    in_turn(add(acc, acc, both))

            a2 = sq[:, 2 * ACC_BANKS[0]:2 * ACC_BANKS[0] + 2, :]
            for k in range(1, 4):
                b = ACC_BANKS[k]
                pool.wait_ge(bank_sq, k + 1)
                in_turn(add(a2, a2, sq[:, 2 * b:2 * b + 2, :]))
            add(a2[:, 0, :], a2[:, 0, :], a2[:, 1, :]).then_inc(sums_ready, 1)
            norm_lo(2 * KT)


def constants():
    import numpy as np
    con = np.zeros((P, N_CONST), np.float32)
    con[:, C_ID:C_ID + P] = np.eye(P)
    lower = np.triu(np.ones((P, P)))
    con[:, C_TRI:C_TRI + P] = con[:, C_TRI2:C_TRI2 + P] = lower
    con[:, C_ONE:C_ONE + P] = 1.0
    i, j = np.arange(SEQ)[:, None], np.arange(SEQ)[None, :]
    causal = (j <= i).astype(np.float64)
    count = sum(causal * ((i - j) % r == 0) * ((i - j) <= w) for w, r in ((128, 1), (512, 4), (2048, 16)))
    for at, times in ((C_M0, causal), (C_M1, count)):
        m = np.where(times > 0, -np.log(np.maximum(times, 1)), BIG)
        con[:, at:at + P] = m[0:P, 0:P]
        con[:, at + P:at + BLK] = m[P:SEQ, :]
    con[:, C_INV], con[:, C_INV + 1] = 1.0 / D_MODEL, SSD_GROUPS / SSD_INNER
    return con


def kernel(**inputs):
    import numpy as np
    import concourse.bacc as bacc
    from concourse.bass_utils import run_bass_kernel_spmd as run

    a = {k: np.asarray(v) for k, v in inputs.items()}
    w_in, w_out = a["even_w_in"][0], a["even_w_out"][0]
    v_in, v_out = a["odd_w_in"][0], a["odd_w_out"][0]

    def in_chunk(w, c0):
        return w[:, c0:c0 + CW].reshape(KT, P, CW).transpose(1, 0, 2).reshape(P, CF)

    def out_chunk(w, r0):
        return w[r0:r0 + CW].reshape(2, P, D_MODEL).transpose(1, 0, 2).reshape(P, CF)

    z0, x0 = 0, SSD_INNER
    b0 = x0 + SSD_INNER
    c0 = b0 + SSD_GROUPS * SSD_STATE
    dt0 = c0 + SSD_GROUPS * SSD_STATE
    q0 = dt0 + SSD_HEADS
    inner = MOBA_HEADS * HD
    w_all = np.empty((P, N_ALL, CF), np.float32)
    chunks = [in_chunk(w_in, b0), in_chunk(w_in, c0)]
    for i in range(IT0):
        chunks += [in_chunk(w_in, s + i * CW) for s in (x0, z0, q0, q0 + inner, q0 + 2 * inner, q0 + 3 * inner)]
    chunks += [out_chunk(w_out, t * P) for t in OUT_ORDER0]
    for i in range(IT1):
        chunks += [in_chunk(v_in, s * DIL_HEADS * HD + i * CW) for s in range(4)]
    chunks += [out_chunk(v_out, j * CW) for j in range(OUT_CHUNKS)]
    for n, chunk in enumerate(chunks):
        w_all[:, n] = chunk
    w_dt = np.ascontiguousarray(w_in[:, dt0:q0].reshape(KT, P, SSD_HEADS).transpose(1, 0, 2).reshape(P, -1))

    def by_tile(v):
        return v.reshape(-1, P).T

    par = np.zeros((P, N_PAR), np.float32)
    taps = np.concatenate([a["ssd_conv_w"][0], a["ssd_conv_b"][0][None]])
    skip = np.repeat(a["ssd_d"][0], SSD_INNER // SSD_HEADS)
    for n, ch0 in enumerate([SSD_INNER, SSD_INNER + CW] + [i * CW for i in range(IT0)]):
        at = P_CONV + n * CPAR
        par[:, at:at + 2 * (CONV + 1)] = taps[:, ch0:ch0 + CW].reshape(CONV + 1, 2, P).transpose(2, 1, 0).reshape(P, -1)
        if n >= 2:
            par[:, at + 2 * (CONV + 1):at + CPAR] = by_tile(skip[ch0:ch0 + CW])
    for at, v in ((P_EVEN, a["even_norm"][0]), (P_ODD, a["odd_norm"][0]), (P_SSD, a["ssd_norm"][0])):
        par[:, at:at + KT] = by_tile(v)
    par[:, P_DTB:P_DTB + NT * SSD_HEADS] = np.tile(a["ssd_dt_bias"][0], NT)
    par[:, P_ALOG:P_ALOG + NT * SSD_HEADS] = np.tile(a["ssd_a_log"][0], NT)
    x_in = np.ascontiguousarray(a["x"][0].T.reshape(KT, P, SEQ).transpose(1, 0, 2))

    nc = bacc.Bacc("TRN2", target_bir_lowering=False, num_devices=1)
    arrays = {"w_all": w_all, "w_dt": w_dt, "x_in": x_in, "par_in": par, "con_in": constants(),
              "gains_in": np.ascontiguousarray(np.broadcast_to(a["final_norm"], (P, D_MODEL)))}
    aps = [nc.dram_tensor(n, v.shape, F32, kind="ExternalInput").ap() for n, v in arrays.items()]
    out = nc.dram_tensor("out", (SEQ, D_MODEL), F32, kind="ExternalOutput").ap()
    build(nc, *aps, out)
    r = run(nc, [arrays], core_ids=[0])
    return r.results[0]["out"][None]
```

```python
from contextlib import ExitStack

import concourse.bass as bass
from concourse import mybir

P = 128
D_MODEL, SEQ = 1024, 256
KT = D_MODEL // P
NT = SEQ // P
SSD_HEADS, SSD_INNER, SSD_STATE, SSD_GROUPS, CONV = 16, 1024, 128, 2, 4
MOBA_HEADS, DIL_HEADS, HD = 8, 16, 128
IT0, IT1 = MOBA_HEADS // 2, DIL_HEADS // 2
CW = 256
CF = KT * CW
OUT_CHUNKS = 2048 // CW
X, Z, Q0, K0, V0, G0, PER0 = 0, 1, 2, 3, 4, 5, 6
Q1, K1, V1, G1, PER1 = 0, 1, 2, 3, 4
FIRST_B, FIRST_Q, FIRST_C, FIRST_K, FIRST_X, FIRST_V, FIRST_Z, FIRST_G = range(-2, PER0)
N_PRE = 2
N_OUT0 = N_PRE + PER0 * IT0
N_L1 = N_OUT0 + OUT_CHUNKS
N_OUT1 = N_L1 + PER1 * IT1
N_ALL = N_OUT1 + OUT_CHUNKS
RING0, RING1 = 3, 4
SLOTS1 = [3] + [(N_L1 - RING0 + j) % RING0 for j in range(RING0)]
USED1 = {s: len(range(s, N_L1, RING0)) if s < RING0 else 0 for s in range(RING1)}
OUT_ORDER0 = [8, 10, 12, 0, 2, 4, 6, 14]
ACC_BANKS = [2, 3, 0, 1]
WARM = 8
PART = KT // 4
HEADS_PER_IT = SSD_HEADS // IT0
CPAR = 2 * (CONV + 1) + 2
BLK = 3 * P
SCALE = float(HD) ** -0.5
EPS = 1e-5
BIG = 1e30

F32, F32R = mybir.dt.float32, mybir.dt.float32r
ALU, ACT = mybir.AluOpType, mybir.ActivationFunctionType

C_ID, C_INV, C_TRI = 0, P, P + 2
C_ONE, C_TRI2, C_M0 = C_TRI + P, C_TRI + 2 * P, C_TRI + 3 * P
C_M1 = C_M0 + BLK
N_CONST = C_M1 + BLK
DT0 = 0
CS0 = DT0 + NT * SSD_HEADS
MARKS0, MARKS1 = 12, 2
P_CONV, P_EVEN = 0, (IT0 + 2) * CPAR
P_ODD, P_SSD = P_EVEN + KT, P_EVEN + 2 * KT
P_DTB, P_ALOG = P_EVEN + 3 * KT, P_EVEN + 3 * KT + NT * SSD_HEADS
N_PAR = P_ALOG + NT * SSD_HEADS


class Chunk:

    def __init__(self, layer, i, j):
        if layer == 0 and isinstance(i, int) and N_PRE + PER0 * i + j >= N_L1:
            layer, j, i = 1, N_PRE + PER0 * i + j - N_L1, 0
        self.layer = layer
        if layer == 0:
            self.n = i * PER0 + (N_PRE + j)
            self.slot = (N_PRE + j) % RING0
            self.use = i * (PER0 // RING0) + (N_PRE + j) // RING0
            self.ring = RING0
        else:
            self.n = i * PER1 + (N_L1 + j)
            self.slot = SLOTS1[j % RING1]
            self.use = i + (USED1[self.slot] + j // RING1)
            self.ring = RING1
        self.landed = self.use * 16 + 16
        self.freed = self.n - (self.ring - 1)
        self.waits = not isinstance(self.n, int) or self.freed > 0
        self.exists = not isinstance(self.n, int) or self.n < N_ALL


class Chain:

    def __init__(self, eng, sem):
        self.eng, self.sem, self.base, self.k = eng, sem, 0, 0

    def restart(self, base):
        self.base, self.k = base, 0

    def mark(self, ins):
        ins.then_inc(self.sem, 1)
        self.k += 1
        return self.base + self.k

    def wait(self, mark):
        self.eng.wait_ge(self.sem, mark)


def build(nc, w_all, w_dt, x_in, par_in, con_in, gains_dram, out):
    with ExitStack() as ctx:
        def sb(name, shape, dt=F32):
            return ctx.enter_context(nc.sbuf_tensor(name, shape, dt))

        def sem(name):
            return ctx.enter_context(nc.semaphore(name))

        raw = sb("raw", [P, RING1, CF])
        w_hi = sb("w_hi", [P, RING1, CF], F32R)
        w_lo = sb("w_lo", [P, RING1, CF], F32R)
        xT = sb("xT", [P, KT, SEQ])
        work = sb("work", [P, KT * SEQ])
        sq = work[:].rearrange("p (k t) -> p k t", k=KT)
        m_t = work[:, 0:HEADS_PER_IT * BLK].rearrange("p (h c) -> p h c", h=HEADS_PER_IT)
        xdt = work[:, HEADS_PER_IT * BLK:KT * SEQ].rearrange("p (t c) -> p t c", t=NT)
        hn_hi = sb("hn_hi", [P, KT, SEQ], F32R)
        hn_lo = sb("hn_lo", [P, KT, SEQ], F32R)
        y_hi = sb("y_hi", [P, 2 * KT, SEQ], F32R)
        y_lo = sb("y_lo", [P, 2 * KT, SEQ], F32R)
        xg_hi, xg_lo = y_hi, y_lo
        ssd_u = raw[:, RING1 - 1, :].rearrange("p (k t) -> p k t", k=KT)
        con = sb("con", [P, N_CONST])
        par = sb("par", [P, N_PAR])
        tri_r = sb("tri_r", [P, 2 * P], F32R)
        q0, k0 = sb("q0", [P, 2, P]), sb("k0", [P, 2, P])
        q1_hi, q1_lo = sb("q1_hi", [P, 2, P], F32R), y_hi[:, 2 * KT - 2:2 * KT, 0:P]
        k_hi, k_lo = sb("k_hi", [P, 2, SEQ], F32R), y_lo[:, 2 * KT - 2:2 * KT, :]
        v0_hi, v0_lo = sb("v0_hi", [P, 2 * HD], F32R), sb("v0_lo", [P, 2 * HD], F32R)
        v1 = sb("v1", [P, 2 * HD])
        gate2 = sb("gate2", [P, 2 * SEQ])
        rb = gate2[:, 0:SEQ]
        s_m = sb("s_m", [P, 2, BLK])
        neg_max = sb("neg_max", [P, 2, NT])
        pace = sb("pace", [P, 2])
        p_sum = sb("p_sum", [P, 2, NT])
        p_inv = sb("p_inv", [P, 2, NT])
        pT0_hi, pT0_lo = sb("pT0_hi", [P, 2, SEQ], F32R), sb("pT0_lo", [P, 2, SEQ], F32R)
        pT1 = sb("pT1", [P, 2, P])
        conv = sb("conv", [P, 2, SEQ])
        xs = sb("xs", [P, 2, SEQ])
        b_s = sb("b_s", [P, SSD_GROUPS, SEQ])
        c_s = sb("c_s", [P, SSD_GROUPS, SEQ])
        z2 = sb("z2", [P, 2 * SEQ])
        decay = sb("decay", [P, 2, BLK])
        g_m = sb("g_m", [P, IT0, BLK])
        wd = sb("wd", [P, KT * SSD_HEADS])
        wd_hi = sb("wd_hi", [P, KT, SSD_HEADS], F32R)
        wd_lo = sb("wd_lo", [P, KT, SSD_HEADS], F32R)
        NH = NT * SSD_HEADS
        sp = sb("sp", [P, 7, NH])
        dt_rows = decay[0:SSD_HEADS, 0, 0:SEQ]
        dt = sb("dt", [P, NT, SSD_HEADS])
        a_exp = sb("a_exp", [P, NH])
        ac = sb("ac", [P, NH])
        ac_hl = sb("ac_hl", [P, 2, NH], F32R)
        cum_s = sb("cum_s", [P, NH])
        cblk = sb("cblk", [P, SSD_HEADS, 3])
        it_par = sb("it_par", [P, CPAR])
        it_c = sb("it_c", [P, HEADS_PER_IT, 3])
        it_dt = sb("it_dt", [P, NT, HEADS_PER_IT])
        it_ac = sb("it_ac", [P, 2 * NT, HEADS_PER_IT], F32R)
        eps_t = sb("eps_t", [P, 2])
        nv = sb("nv", [P, 5, 4])
        row_ms = sb("row_ms", [P, 4])

        bank = [ctx.enter_context(nc.psum_tensor(f"bank{b}", [P, 512], F32)) for b in range(8)]
        CUM, O_PS, Y_PS, S_PS, T_PS = [bank[2], bank[3]], bank[4], bank[5], bank[6], bank[7]

        D_PS = bank[3]
        ident, tri, ones = con[:, C_ID:C_ID + P], con[:, C_TRI:C_TRI + P], con[:, C_ONE:C_ONE + P]
        causal3 = con[:, C_TRI:C_TRI + BLK]
        mask = [con[:, C_M0:C_M0 + BLK], con[:, C_M1:C_M1 + BLK]]

        g_flat = g_m[:].rearrange("p i c -> p (i c)")
        u_sq, g_sum = b_s, c_s
        sums = {0: sq[:, 0:1, :], 1: g_sum, 2: sq[:, 2 * ACC_BANKS[0]:2 * ACC_BANKS[0] + 1, :]}
        gains = work[:, 0:D_MODEL]
        out_sq = work[:, D_MODEL:2 * D_MODEL]
        x_out = xT[:].rearrange("p k t -> p (k t)")

        def w3(t, slot):
            return t[:, slot, :].rearrange("p (k c) -> p k c", k=KT)

        def w_out(t, slot):
            return t[:, slot, :].rearrange("p (r c) -> p r c", r=2)

        landed = [sem(f"landed{s}") for s in range(RING1)]
        x_in_a, x_in_b, par_in_s, wd_in = (
            sem("x_in_a"), sem("x_in_b"), sem("par_landed"), sem("wd_landed"))
        hi_ready, lo_ready = sem("hi_ready"), sem("lo_ready")
        mm_done = sem("mm_done")
        qkv_hi, dve_evac = sem("qkv_hi"), sem("dve_evac")
        s_done, s_free = sem("s_done"), sem("s_free")
        exp_done, p_ready = sem("exp_done"), sem("p_ready")
        t_done, t_ready = sem("t_done"), sem("t_ready")
        o_done, yf_ready = sem("o_done"), sem("yf_ready")
        yhi_ready, y_ready = sem("yhi_ready"), sem("y_ready")
        tap_bias, conv_tanh, taps_halved = sem("tap_bias"), sem("conv_tanh"), sem("taps_halved")
        xs_ready, xt_done, xdt_ready = sem("xs_ready"), sem("xt_done"), sem("xdt_ready")
        tanh_z, tanh_g = sem("tanh_z"), sem("tanh_g")
        staged, cum_done, sub_done = sem("staged"), sem("cum_done"), sem("sub_done")
        dec_ready, m_ready, yd_done = sem("dec_ready"), sem("m_ready"), sem("yd_done")
        u_ready = sem("u_ready")
        bc_done = sem("bc_done")
        dt_mm, dt_abs, dt_exp, ac_ready, cs_done, a_ready, wd_hi_s, wd_ready = (
            sem("dt_mm"), sem("dt_abs"), sem("dt_exp"), sem("ac_ready"), sem("cs_done"),
            sem("a_ready"), sem("wd_hi_ready"), sem("wd_ready"))
        eps_ready = sem("eps_ready")
        squared, bank_sq, sums_ready = sem("squared"), sem("bank_sq"), sem("sums_ready")
        ms_done, sd_ready, r_ready = sem("ms_done"), sem("sd_ready"), sem("r_ready")
        rb_done, scaled, hnhi_ready, hn_ready = sem("rb_done"), sem("scaled"), sem("hnhi_ready"), sem("hn_ready")
        xghi_ready, xg_ready = sem("xghi_ready"), sem("xg_ready")
        rescaled = sem("rescaled")
        row_sq, ms_ready, with_gains = sem("row_sq"), sem("ms_ready"), sem("with_gains")
        dve_out, pool_out, act_out = sem("dve_out"), sem("pool_out"), sem("act_out")
        first_half = sem("first_half_landed")
        part_hi, part_lo = sem("part_hi"), sem("part_lo")
        id_in, tri_in, gains_in = sem("id_landed"), sem("tri_landed"), sem("gains_landed")
        zeroed = sem("zeroed")
        qk_ready = sem("qk_ready")
        v_ready, pt_ready = sem("v_ready"), sem("pt_ready")
        dt_copied, dt_flipped, rec_ready = sem("dt_copied"), sem("dt_flipped"), sem("rec_ready")
        gm_copied = sem("gm_copied")
        acc_done, x_ready = sem("acc_done"), sem("x_ready")
        dve_chain, pool_chain = sem("dve_chain"), sem("pool_chain")
        out_landed = sem("out_landed")

        block = ctx.enter_context(nc.Block())

        def send(eng, t, h):
            q = 2 * t + h
            eng.dma_start(out[t * P:(t + 1) * P, h * 512:(h + 1) * 512],
                          x_out[:, q * 512:(q + 1) * 512]).then_inc(out_landed, 16)

        def cols(norm):
            return NT * SSD_GROUPS if norm == 1 else NT

        @block.sync
        def _(sync):
            def load(c):
                if c.waits:
                    sync.wait_ge(lo_ready, c.freed)
                sync.dma_start(raw[:, c.slot, :], w_all[:, bass.ds(c.n, 1), :]).then_inc(landed[c.slot], 16)

            half, first = KT // 2, Chunk(0, 0, FIRST_B)
            sync.dma_start(xT[:, 0:half, :], x_in[:, 0:half, :]).then_inc(x_in_a, 16)
            sync.dma_start(raw[:, first.slot, 0:CF // 2], w_all[:, first.n, 0:CF // 2]).then_inc(first_half, 16)
            sync.dma_start(xT[:, half:KT, :], x_in[:, half:KT, :]).then_inc(x_in_b, 16)
            sync.dma_start(raw[:, first.slot, CF // 2:], w_all[:, first.n, CF // 2:]).then_inc(
                landed[first.slot], 16)
            sync.dma_start(wd[:], w_dt).then_inc(wd_in, 16)
            load(Chunk(0, 0, -1))
            load(Chunk(0, 0, 0))
            sync.dma_start(con[:, C_TRI:], con_in[:, C_TRI:]).then_inc(tri_in, 16)
            for j in range(1, PER0):
                load(Chunk(0, 0, j))
            with sync.Fori(1, IT0) as i:
                for j in range(PER0):
                    load(Chunk(0, i, j))
            for j in range(OUT_CHUNKS):
                load(Chunk(0, IT0, j))
            with sync.Fori(0, IT1) as i:
                for j in range(PER1):
                    load(Chunk(1, i, j))
            sync.wait_ge(hn_ready, 3 * KT)
            sync.dma_start(gains, gains_dram).then_inc(gains_in, 16)
            for j in range(OUT_CHUNKS):
                load(Chunk(1, IT1, j))
            for t, h, ready in ((0, 1, dve_out), (0, 0, pool_out), (1, 1, dve_out)):
                sync.wait_ge(ready, t + 1)
                send(sync, t, h)
            sync.wait_ge(out_landed, 64)

        @block.tensor
        def _(pe):
            def three(ps, a_hi, a_lo, m_hi, m_lo, start, stop, **kw):
                pe.matmul(ps, a_hi, m_hi, start=start, stop=False, **kw)
                pe.matmul(ps, a_hi, m_lo, start=False, stop=False, **kw)
                return pe.matmul(ps, a_lo, m_hi, start=False, stop=stop, **kw)

            def project(c, tile, pb, raw_x=False, order=range(KT), before=lambda n: None):
                cs = slice(tile * P, tile * P + P)
                hi, lo = w3(w_hi, c.slot), w3(w_lo, c.slot)
                m_hi, m_lo = (xg_hi, xg_lo) if raw_x else (hn_hi, hn_lo)
                for n, k in enumerate(order):
                    before(n)
                    last = three(bank[pb][:, tile * SEQ:(tile + 1) * SEQ], hi[:, k, cs], lo[:, k, cs],
                                 m_hi[:, k, :], m_lo[:, k, :], n == 0, n == KT - 1)
                return last

            def project_v(c, t, pb, raw_x=False):
                ts = slice(t * P, t * P + P)
                hi, lo = w3(w_hi, c.slot), w3(w_lo, c.slot)
                m_hi, m_lo = (xg_hi, xg_lo) if raw_x else (hn_hi, hn_lo)
                for k in range(KT):
                    last = three(bank[pb][:, t * CW:(t + 1) * CW], m_hi[:, k, ts], m_lo[:, k, ts],
                                 hi[:, k, :], lo[:, k, :], k == 0, k == KT - 1)
                return last

            def scores(h, count):
                pe.wait_ge(s_free, count + 1)
                pe.matmul(S_PS[:, 0:P], q0[:, h, :], k0[:, h, :], start=True, stop=True)
                three(S_PS[:, P:BLK], q1_hi[:, h, :], q1_lo[:, h, :], k_hi[:, h, :], k_lo[:, h, :],
                      True, True).then_inc(s_done, 1)

            def flip(h, count):
                pe.wait_ge(p_ready, count + 1)
                pe.wait_ge(pt_ready, count + 1)
                for b in range(3):
                    last = pe.transpose(T_PS[:, b * P:(b + 1) * P], s_m[:, h, b * P:(b + 1) * P], ident)
                last.then_inc(t_done, 1)

            def attend(h, count):
                pe.wait_ge(pt_ready, count + 2)
                hs = slice(h * HD, (h + 1) * HD)
                three(O_PS[:, h * SEQ:(h + 1) * SEQ], v0_hi[:, hs], v0_lo[:, hs],
                      pT0_hi[:, h, :], pT0_lo[:, h, :], True, False)
                pe.matmul(O_PS[:, h * SEQ + P:(h + 1) * SEQ], v1[:, hs], pT1[:, h, :],
                          start=False, stop=True).then_inc(o_done, 1)

            def mean_squares(norm):
                pe.wait_ge(sums_ready, norm + 1)
                for col in range(cols(norm)):
                    g, t = col // NT, col % NT
                    last = pe.matmul(Y_PS[:, col:col + 1], sums[norm][:, g, t * P:(t + 1) * P],
                                     con[:, C_INV + (norm == 1):C_INV + (norm == 1) + 1], start=True, stop=True)
                last.then_inc(ms_done, 1)

            def spread(norm):
                pe.wait_ge(r_ready, norm + 1)
                for c in range(cols(norm)):
                    last = pe.matmul(Y_PS[:, c * P:(c + 1) * P], nv[:, 3, c:c + 1].to_broadcast([P, P]), ident,
                                     start=True, stop=True)
                last.then_inc(rb_done, 1)

            def cum(h, i):
                n = i * HEADS_PER_IT + h
                if h == 0:
                    pe.wait_ge(staged, i + 1)
                if not (isinstance(n, int) and n < 2):
                    pe.wait_ge(sub_done, n - 1)
                ps = CUM[h % 2]
                for c, cs in ((0, slice(0, P)), (1, slice(P, BLK))):
                    for part in range(2):
                        last = pe.matmul(ps[:, cs], it_ac[:, part * NT + c, h:h + 1].to_broadcast([P, P]),
                                         tri_r[:, 0:cs.stop - cs.start], start=part == 0, stop=part == 1)
                last.then_inc(cum_done, 1)

            def x_to_tokens(i):
                pe.wait_ge(xs_ready, i + 3)
                for t in range(NT):
                    for c in range(2):
                        last = pe.transpose(S_PS[:, t * CW + c * P:t * CW + (c + 1) * P],
                                            xs[:, c, t * P:(t + 1) * P], ident)
                last.then_inc(xt_done, 1)

            def ssd_out(h, i):
                pe.wait_ge(m_ready, i * HEADS_PER_IT + (h + 1))
                if h == 0:
                    pe.wait_ge(xdt_ready, i + 1)
                    if not (isinstance(i, int) and i == 0):
                        pe.wait_ge(u_ready, i)
                rows, c0 = slice(64 * (h % 2), 64 * (h % 2) + 64), (h // 2) * SEQ
                pe.matmul(Y_PS[rows, c0:c0 + SEQ], xdt[:, 0, h * 64:(h + 1) * 64], m_t[:, h, 0:SEQ],
                          start=True, stop=False)
                last = pe.matmul(Y_PS[rows, c0 + P:c0 + SEQ], xdt[:, 1, h * 64:(h + 1) * 64],
                                 m_t[:, h, SEQ:BLK], start=False, stop=True)
                if h == HEADS_PER_IT - 1:
                    last.then_inc(yd_done, 1)

            def bc_scores():
                pe.wait_ge(xs_ready, 2)
                for g, ps in ((0, S_PS), (1, T_PS)):
                    pe.matmul(ps[:, 0:SEQ], b_s[:, g, 0:P], c_s[:, g, :], start=True, stop=True)
                    last = pe.matmul(ps[:, SEQ:BLK], b_s[:, g, P:SEQ], c_s[:, g, P:SEQ], start=True, stop=True)
                last.then_inc(bc_done, 1)

            def first_iteration():
                b, q, cc, k, x, v, z, g = (Chunk(0, 0, j) for j in range(-2, PER0))

                hi, lo = w3(w_hi, b.slot), w3(w_lo, b.slot)
                for half in range(2):
                    for tile in range(2):
                        for n in range(half * (KT // 2), (half + 1) * (KT // 2)):
                            if tile == 0:
                                pe.wait_ge(xg_ready, n + 1)
                                if n % PART == 0:
                                    pe.wait_ge(*((part_lo, n // PART + 1) if n + PART < KT else (lo_ready, 1)))
                            cs = slice(tile * P, (tile + 1) * P)
                            last = three(bank[0][:, tile * SEQ:(tile + 1) * SEQ], hi[:, n, cs], lo[:, n, cs],
                                         xg_hi[:, n, :], xg_lo[:, n, :], n == 0 and tile == 0, n == KT - 1,
                                         skip_group_check=True)
                last.then_inc(mm_done, 1)
                pe.wait_ge(id_in, 16)
                mean_squares(0)
                pe.wait_ge(wd_ready, 1)
                for n in range(KT):
                    last = three(D_PS[0:SSD_HEADS, 0:SEQ], wd_hi[:, n, :], wd_lo[:, n, :],
                                 xg_hi[:, n, :], xg_lo[:, n, :], n == 0, n == KT - 1)
                last.then_inc(dt_mm, 1)
                spread(0)
                pe.wait_ge(lo_ready, q.n + 1)
                project(q, 0, 1, True)
                pe.wait_ge(dt_copied, 1)
                for t in range(NT):
                    last = pe.transpose(D_PS[:, DT0 + t * SSD_HEADS:DT0 + (t + 1) * SSD_HEADS],
                                        dt_rows[:, t * P:(t + 1) * P], ident[0:SSD_HEADS, 0:SSD_HEADS])
                last.then_inc(dt_flipped, 1)
                project(q, 1, 1, True).then_inc(mm_done, 1)
                pe.wait_ge(lo_ready, cc.n + 1)
                pe.wait_ge(dve_evac, 1)
                project(cc, 0, 0, True)
                project(cc, 1, 0, True).then_inc(mm_done, 1)
                pe.wait_ge(lo_ready, k.n + 1)
                pe.wait_ge(qk_ready, 1)
                project(k, 0, 1, True)
                project(k, 1, 1, True).then_inc(mm_done, 1)
                cum_sums()
                pe.wait_ge(lo_ready, x.n + 1)
                pe.wait_ge(dve_evac, 2)
                project(x, 0, 0, before=lambda n: pe.wait_ge(hn_ready, n + 1))
                bc_scores()
                project(x, 1, 0).then_inc(mm_done, 1)
                cum(0, 0)
                cum(1, 0)
                pe.wait_ge(lo_ready, v.n + 1)
                pe.wait_ge(qk_ready, 2)
                project_v(v, 0, 1)
                cum(2, 0)
                project_v(v, 1, 1).then_inc(mm_done, 1)
                cum(3, 0)
                pe.wait_ge(lo_ready, z.n + 1)
                pe.wait_ge(dve_evac, 3)
                project(z, 0, 0)
                pe.wait_ge(s_free, 1)
                x_to_tokens(0)
                project(z, 1, 0).then_inc(mm_done, 1)
                pe.wait_ge(lo_ready, g.n + 1)
                pe.wait_ge(v_ready, 1)
                project(g, 0, 1)
                ssd_out(0, 0)
                ssd_out(1, 0)
                project(g, 1, 1).then_inc(mm_done, 1)
                ssd_out(2, 0)
                ssd_out(3, 0)
                pe.wait_ge(dve_evac, 4)

            def layer0(i):
                heads = (i - 1) * 2
                c = [Chunk(0, i, j) for j in range(PER0)]
                pe.wait_ge(lo_ready, c[X].n + 1)
                pe.wait_ge(v_ready, i)
                project(c[X], 0, 0)
                scores(0, heads)
                project(c[X], 1, 0).then_inc(mm_done, 1)
                scores(1, heads + 1)
                pe.wait_ge(lo_ready, c[Z].n + 1)
                pe.wait_ge(dve_evac, i * 3 + 2)
                project(c[Z], 0, 1)
                flip(0, heads)
                cum(0, i)
                project(c[Z], 1, 1).then_inc(mm_done, 1)
                flip(1, heads + 1)
                cum(1, i)
                pe.wait_ge(lo_ready, c[Q0].n + 1)
                pe.wait_ge(dve_evac, i * 3 + 3)
                project(c[Q0], 0, 0)
                attend(0, heads)
                x_to_tokens(i)
                project(c[Q0], 1, 0).then_inc(mm_done, 1)
                attend(1, heads + 1)
                cum(2, i)
                pe.wait_ge(lo_ready, c[K0].n + 1)
                pe.wait_ge(dve_evac, i * 3 + 4)
                project(c[K0], 0, 1)
                cum(3, i)
                project(c[K0], 1, 1).then_inc(mm_done, 1)
                pe.wait_ge(lo_ready, c[V0].n + 1)
                pe.wait_ge(qk_ready, i * 2 + 1)
                project_v(c[V0], 0, 0)
                ssd_out(0, i)
                ssd_out(1, i)
                project_v(c[V0], 1, 0).then_inc(mm_done, 1)
                ssd_out(2, i)
                ssd_out(3, i)
                pe.wait_ge(lo_ready, c[G0].n + 1)
                pe.wait_ge(qk_ready, i * 2 + 2)
                project(c[G0], 0, 1)
                project(c[G0], 1, 1).then_inc(mm_done, 1)

            def layer1(i, first):
                heads = (i - 1) * 2 + MOBA_HEADS
                c = [Chunk(1, i, j) for j in range(PER1)]
                taken = i * 2 + 2 * IT0
                pe.wait_ge(lo_ready, c[Q1].n + 1)
                if first:
                    order = [2 * b + d for b in ACC_BANKS for d in range(2)]
                    pe.wait_ge(x_ready, 3)
                    project(c[Q1], 0, 0, True, order, lambda n: pe.wait_ge(xg_ready, KT + n + 1))
                    project(c[Q1], 1, 0, True).then_inc(mm_done, 1)
                    mean_squares(2)
                else:
                    pe.wait_ge(v_ready, i + IT0)
                    project(c[Q1], 0, 0)
                    scores(0, heads)
                    project(c[Q1], 1, 0).then_inc(mm_done, 1)
                if not first:
                    scores(1, heads + 1)
                pe.wait_ge(lo_ready, c[K1].n + 1)
                if first:
                    pe.wait_ge(x_ready, 4)
                else:
                    pe.wait_ge(dve_evac, i + (2 + 3 * IT0))
                project(c[K1], 0, 1, first)
                if first:
                    spread(2)
                else:
                    flip(0, heads)
                project(c[K1], 1, 1, first).then_inc(mm_done, 1)
                if not first:
                    flip(1, heads + 1)
                pe.wait_ge(lo_ready, c[V1].n + 1)
                pe.wait_ge(qk_ready, taken + 1)
                project_v(c[V1], 0, 0, first)
                if not first:
                    attend(0, heads)
                project_v(c[V1], 1, 0, first).then_inc(mm_done, 1)
                if not first:
                    attend(1, heads + 1)
                pe.wait_ge(lo_ready, c[G1].n + 1)
                pe.wait_ge(qk_ready, taken + 2)
                project(c[G1], 0, 1, before=lambda k: pe.wait_ge(hn_ready, 2 * KT + k + 1) if first else None)
                project(c[G1], 1, 1).then_inc(mm_done, 1)

            def project_out(j, tiles, c, hooks, y_need):
                pe.wait_ge(lo_ready, c.n + 1)
                pe.wait_ge(y_ready, y_need)
                hi, lo = w_out(w_hi, c.slot), w_out(w_lo, c.slot)
                for nb, b in enumerate(ACC_BANKS):
                    if j == 0 and b == 0:
                        pe.wait_ge(v_ready, IT0)
                    if j == 0 and b == 1:
                        pe.wait_ge(dve_evac, 2 + 3 * IT0)
                    for d in range(2):
                        ds = slice((2 * b + d) * P, (2 * b + d + 1) * P)
                        for r in range(2):
                            last = three(bank[b][:, d * SEQ:(d + 1) * SEQ], hi[:, r, ds], lo[:, r, ds],
                                         y_hi[:, tiles + r, :], y_lo[:, tiles + r, :],
                                         j == 0 and d == 0 and r == 0, j == OUT_CHUNKS - 1 and r == 1,
                                         skip_group_check=True)
                    if nb == 3:
                        last.then_inc(mm_done, 1)
                    elif j == OUT_CHUNKS - 1:
                        last.then_inc(acc_done, 1)
                    if nb in hooks:
                        hooks[nb]()

            def project_final(j, c, hooks):
                if j == 0:
                    for q, b in enumerate(ACC_BANKS):
                        if b == 0:
                            pe.wait_ge(v_ready, IT0 + IT1)
                        if b == 1:
                            pe.wait_ge(dve_evac, 2 + 3 * IT0 + IT1)
                        t, k0 = q // 2, (q % 2) * (KT // 2)
                        for k in range(KT // 2):
                            last = pe.matmul(bank[b][:, k * P:(k + 1) * P], xT[:, k0 + k, t * P:(t + 1) * P],
                                             ident, start=k == 0, stop=False, skip_group_check=True)
                        if q in hooks:
                            hooks[q]()
                pe.wait_ge(lo_ready, c.n + 1)
                pe.wait_ge(y_ready, IT0 + j + 1)
                hi, lo = w_out(w_hi, c.slot), w_out(w_lo, c.slot)
                for q, b in enumerate(ACC_BANKS):
                    ts, ds = slice(q // 2 * P, (q // 2 + 1) * P), slice(q % 2 * 512, (q % 2 + 1) * 512)
                    for r in range(2):
                        last = three(bank[b][:], y_hi[:, 2 * j + r, ts], y_lo[:, 2 * j + r, ts],
                                     hi[:, r, ds], lo[:, r, ds], False, j == OUT_CHUNKS - 1 and r == 1,
                                     skip_group_check=True)
                    if q == 3:
                        last.then_inc(mm_done, 1)
                    elif j == OUT_CHUNKS - 1:
                        last.then_inc(acc_done, 1)
                    if j and q in hooks:
                        hooks[q]()

            def cum_sums():
                pe.wait_ge(tri_in, 16)
                pe.wait_ge(ac_ready, 1)
                pe.matmul(D_PS[:, CS0:CS0 + NH], tri, ac[:], start=True, stop=True)
                pe.matmul(D_PS[:, CS0 + NH:CS0 + NH + SSD_HEADS], ones, ac[:, 0:SSD_HEADS],
                          start=True, stop=True).then_inc(cs_done, 1)

            pe.wait_ge(zeroed, 1)
            for _ in range(WARM):
                pe.matmul(T_PS[:, 0:SEQ], xs[:, 0, 0:P], xs[:, 0, :], start=True, stop=True)
            first_iteration()
            with pe.Fori(1, IT0) as i:
                layer0(i)

            h0 = MOBA_HEADS - 2
            pe.wait_ge(qk_ready, 2 * IT0)
            pe.wait_ge(sub_done, SSD_HEADS)
            hooks = {0: {0: lambda: scores(0, h0), 1: lambda: mean_squares(1), 2: lambda: scores(1, h0 + 1)},
                     1: {1: lambda: flip(0, h0), 3: lambda: (flip(1, h0 + 1), spread(1))},
                     2: {1: lambda: attend(0, h0), 3: lambda: attend(1, h0 + 1)}}
            order = OUT_ORDER0
            for j in range(OUT_CHUNKS):
                if order[j] < KT:
                    pe.wait_ge(hn_ready, KT + order[j] + 2)
                    need = 3
                else:
                    need = order[j] // 2 - 3
                project_out(j, order[j], Chunk(0, IT0, j), hooks.get(j, {}), need)

            layer1(0, True)
            with pe.Fori(1, IT1) as i:
                layer1(i, False)
            h1 = MOBA_HEADS + DIL_HEADS - 2
            pe.wait_ge(qk_ready, 2 * IT0 + 2 * IT1)
            hooks = {0: {0: lambda: scores(0, h1), 3: lambda: scores(1, h1 + 1)},
                     1: {1: lambda: flip(0, h1), 3: lambda: flip(1, h1 + 1)},
                     2: {1: lambda: attend(0, h1), 3: lambda: attend(1, h1 + 1)}}
            for j in range(OUT_CHUNKS):
                project_final(j, Chunk(1, IT1, j), hooks.get(j, {}))

        @block.scalar
        def _(act):
            def split_hi(c):
                if not c.exists:
                    return
                act.wait_ge(landed[c.slot], c.landed)
                if c.waits:
                    act.wait_ge(mm_done, c.freed)
                act.activation(w_hi[:, c.slot, :], raw[:, c.slot, :], ACT.Copy).then_inc(hi_ready, 1)

            def split_hi_part(c, part, parts):
                cs = slice(part * CF // parts, (part + 1) * CF // parts)
                act.activation(w_hi[:, c.slot, cs], raw[:, c.slot, cs], ACT.Copy).then_inc(
                    hi_ready if part == parts - 1 else part_hi, 1)

            def gained_hi(k, at):
                act.activation(xg_hi[:, k, :], xT[:, k, :], ACT.Copy,
                               scale=par[:, at + k:at + k + 1]).then_inc(xghi_ready, 1)

            def root(norm):
                act.wait_ge(ms_done, norm + 1)
                act.activation(nv[:, 0, 0:cols(norm)], Y_PS[:, 0:cols(norm)], ACT.Sqrt,
                               bias=eps_t[:, (norm == 1):(norm == 1) + 1]).then_inc(sd_ready, 1)

            def norm_hi(dst, base, ks=range(KT)):
                for k in ks:
                    act.wait_ge(scaled, base + k + 1)
                    act.activation(dst[:, k, :], sq[:, k, :], ACT.Copy).then_inc(hnhi_ready, 1)

            def exps(h, count):
                act.wait_ge(s_free, count + 2)
                act.activation(s_m[:, h, 0:P], s_m[:, h, 0:P], ACT.Exp, bias=neg_max[:, h, 0:1], scale=-1.0,
                               accum_out=p_sum[:, h, 0:1])
                act.activation(s_m[:, h, P:BLK], s_m[:, h, P:BLK], ACT.Exp, bias=neg_max[:, h, 1:2], scale=-1.0,
                               accum_out=p_sum[:, h, 1:2]).then_inc(exp_done, 1)

            def take_t(h, count):
                act.wait_ge(t_done, count + 1)
                act.activation(pT0_hi[:, h, :], T_PS[:, 0:SEQ], ACT.Copy)
                act.activation(pT1[:, h, :], T_PS[:, SEQ:BLK], ACT.Copy).then_inc(t_ready, 1)

            def conv_start(c, pb, taps):
                act.wait_ge(mm_done, c.n + 1)
                for t in range(2):
                    o = (CONV + 1) * t
                    last = act.activation(conv[:, t, :], bank[pb][:, t * SEQ:(t + 1) * SEQ], ACT.Identity,
                                          bias=taps[:, o + CONV:o + CONV + 1], scale=taps[:, o + 3:o + 4])
                last.then_inc(tap_bias, 1)

            def conv_end(n, dst):
                act.wait_ge(dve_evac, n)
                act.activation(dst[:], conv[:], ACT.Tanh).then_inc(conv_tanh, 1)

            def dec(h, i):
                act.wait_ge(sub_done, i * HEADS_PER_IT + (h + 1))
                act.activation(decay[:, h % 2, :], decay[:, h % 2, :], ACT.Exp).then_inc(dec_ready, 1)

            def y_high(tile, count):
                act.wait_ge(yf_ready, count)
                act.activation(y_hi[:, tile, :], gate2[:].rearrange("p (a t) -> p a t", a=2),
                               ACT.Copy).then_inc(yhi_ready, 1)

            def product_of(c):
                if isinstance(c.n, int):
                    act.wait_ge(rescaled, (c.n - N_L1 + 5) if c.layer else c.n + 1)
                else:
                    act.wait_ge(mm_done, c.n + 1)

            def take_q(c, pb):
                product_of(c)
                q = bank[pb][:].rearrange("p (a t) -> p a t", a=2)
                act.activation(q0[:], q[:, :, 0:P], ACT.Copy, scale=-SCALE)
                act.activation(q1_hi[:], q[:, :, P:SEQ], ACT.Copy, scale=-SCALE).then_inc(qkv_hi, 1)

            def take_k(c, pb):
                product_of(c)
                k = bank[pb][:].rearrange("p (a t) -> p a t", a=2)
                act.activation(k_hi[:], k, ACT.Copy)
                act.activation(k0[:], k[:, :, 0:P], ACT.Copy).then_inc(qkv_hi, 1)

            def take_v(c, pb):
                if c.layer:
                    product_of(c)
                else:
                    act.wait_ge(mm_done, c.n + 1)
                act.activation(v0_hi[:], bank[pb][:, 0:CW], ACT.Copy)
                act.activation(v1[:], bank[pb][:, CW:2 * CW], ACT.Copy).then_inc(qkv_hi, 1)

            def tanh_of(dst, c, pb, s):
                act.wait_ge(mm_done, c.n + 1)
                act.activation(dst, bank[pb][:], ACT.Tanh, scale=0.5).then_inc(s, 1)

            def first_iteration():
                b, q, cc, k, x, v, z, g, x1, z1 = (Chunk(0, 0, j) for j in range(-2, PER0 + 2))
                act.wait_ge(landed[q.slot], q.landed)
                split_hi_part(q, 0, 2)
                split_hi_part(q, 1, 2)
                act.wait_ge(eps_ready, 1)
                root(0)
                split_hi(cc)
                act.preload_act_table(ACT.Exp)
                act.activation(a_exp[:], par[:, P_ALOG:P_ALOG + NH], ACT.Exp).then_inc(a_ready, 1)
                act.wait_ge(dt_mm, 1)
                act.activation(dt_rows, D_PS[0:SSD_HEADS, 0:SEQ], ACT.Copy).then_inc(dt_copied, 1)
                act.wait_ge(taps_halved, 1)
                act.wait_ge(rescaled, 1)
                conv_start(b, 0, par[:, P_CONV:])
                norm_hi(hn_hi, 0, range(KT // 2))
                split_hi(k)
                act.wait_ge(dt_abs, 1)
                act.activation(sp[:, 2, :], sp[:, 1, :], ACT.Exp, scale=-1.0).then_inc(dt_exp, 1)
                conv_end(1, b_s)
                take_q(q, 1)
                act.wait_ge(tri_in, 16)
                for t in range(2):
                    act.activation(tri_r[:, t * P:(t + 1) * P], tri, ACT.Copy)
                split_hi(x)
                act.wait_ge(xs_ready, 1)
                act.wait_ge(rescaled, 3)
                conv_start(cc, 0, par[:, P_CONV + CPAR:])
                norm_hi(hn_hi, 0, range(KT // 2, KT - 1))
                split_hi(v)
                norm_hi(hn_hi, 0, range(KT - 1, KT))
                conv_end(2, c_s)
                take_k(k, 1)
                split_hi(z)
                dec(0, 0)
                dec(1, 0)
                act.wait_ge(xs_ready, 2)
                conv_start(x, 0, it_par)
                split_hi(g)
                conv_end(3, xs)
                dec(2, 0)
                take_v(v, 1)
                dec(3, 0)
                split_hi(x1)
                tanh_of(z2[:], z, 0, tanh_z)
                split_hi(z1)

            def layer0(i):
                heads = (i - 1) * 2
                c = [Chunk(0, i, j) for j in range(PER0 + 2)]
                act.wait_ge(u_ready, i)
                tanh_of(gate2[:], Chunk(0, i, -1), 1, tanh_g)
                split_hi(c[X + 2])
                exps(0, heads)
                act.wait_ge(staged, i + 1)
                act.wait_ge(xs_ready, i + 2)
                conv_start(c[X], 0, it_par)
                exps(1, heads + 1)
                take_t(0, heads)
                conv_end(i * 3 + 3, xs)
                split_hi(c[Z + 2])
                dec(0, i)
                tanh_of(z2[:], c[Z], 1, tanh_z)
                take_t(1, heads + 1)
                dec(1, i)
                split_hi(c[Q0 + 2])
                dec(2, i)
                act.wait_ge(s_done, heads + 2)
                take_q(c[Q0], 0)
                y_high(bass.ds(i * 2 + (KT - 2), 2), i)
                split_hi(c[K0 + 2])
                dec(3, i)
                take_k(c[K0], 1)
                split_hi(c[V0 + 2])
                act.wait_ge(o_done, heads + 2)
                take_v(c[V0], 0)
                split_hi(c[G0 + 2])

            def layer1(i, first):
                heads = (i - 1) * 2 + MOBA_HEADS
                c = [Chunk(1, i, j) for j in range(PER1 + 2)]
                prev = Chunk(1, i, -1)
                if not first:
                    act.wait_ge(y_ready, i + (IT0 - 1))
                    tanh_of(gate2[:], prev, 1, tanh_g)
                split_hi(c[Q1 + 2])
                if first:
                    root(2)
                    act.preload_act_table(ACT.Exp)
                else:
                    exps(0, heads)
                    act.wait_ge(s_done, heads + 2)
                take_q(c[Q1], 0)
                if not first:
                    exps(1, heads + 1)
                split_hi(c[K1 + 2])
                if first:
                    norm_hi(hn_hi, 2 * KT, range(KT - 2))
                else:
                    take_t(0, heads)
                take_k(c[K1], 1)
                if first:
                    norm_hi(hn_hi, 2 * KT, range(KT - 2, KT))
                else:
                    take_t(1, heads + 1)
                split_hi(c[V1 + 2])
                if not first:
                    act.wait_ge(o_done, heads + 2)
                take_v(c[V1], 0)
                split_hi(c[G1 + 2])
                if not first:
                    y_high(bass.ds(i * 2 - 2, 2), i + IT0)

            act.dma_start(par[:], par_in).then_inc(par_in_s, 16)
            act.dma_start(con[:, 0:C_TRI], con_in[:, 0:C_TRI]).then_inc(id_in, 16)
            act.preload_act_table(ACT.Sqrt)
            first, half = Chunk(0, 0, FIRST_B), KT // 2
            act.wait_ge(par_in_s, 16)
            act.wait_ge(x_in_a, 16)
            for k in range(half):
                gained_hi(k, P_EVEN)
            act.wait_ge(first_half, 16)
            split_hi_part(first, 0, 4)
            split_hi_part(first, 1, 4)
            act.wait_ge(x_in_b, 16)
            for k in range(half, KT):
                gained_hi(k, P_EVEN)
            act.wait_ge(landed[first.slot], first.landed)
            split_hi_part(first, 2, 4)
            split_hi_part(first, 3, 4)
            act.wait_ge(wd_in, 16)
            act.activation(wd_hi[:], wd[:].rearrange("p (k h) -> p k h", k=KT), ACT.Copy).then_inc(wd_hi_s, 1)
            first_iteration()
            with act.Fori(1, IT0) as i:
                layer0(i)

            h0 = MOBA_HEADS - 2
            o = [Chunk(0, IT0, j) for j in range(-1, OUT_CHUNKS + 2)]
            act.wait_ge(u_ready, IT0)
            tanh_of(gate2[:], o[0], 1, tanh_g)
            split_hi(o[3])
            exps(0, h0)
            exps(1, h0 + 1)
            root(1)
            split_hi(o[4])
            take_t(0, h0)
            take_t(1, h0 + 1)
            for k in range(4):
                act.wait_ge(scaled, KT + k + 1)
                act.activation(y_hi[:, k, :], sq[:, k, :], ACT.Copy).then_inc(hnhi_ready, 1)
            split_hi(o[5])
            for k in range(4, KT):
                act.wait_ge(scaled, KT + k + 1)
                act.activation(y_hi[:, k, :], sq[:, k, :], ACT.Copy).then_inc(hnhi_ready, 1)
            y_high(slice(2 * KT - 2, 2 * KT), IT0)
            split_hi(o[6])
            split_hi(o[7])
            split_hi(o[8])
            split_hi(o[9])
            split_hi(o[10])
            act.preload_act_table(ACT.Sqrt)
            for k, b in enumerate(ACC_BANKS):
                act.wait_ge(x_ready, k + 1)
                for d in range(2):
                    gained_hi(2 * b + d, P_ODD)
                act.activation(sq[:, 2 * b:2 * b + 2, :], xT[:, 2 * b:2 * b + 2, :], ACT.Square).then_inc(bank_sq, 1)
            layer1(0, True)
            with act.Fori(1, IT1) as i:
                layer1(i, False)
            h1 = MOBA_HEADS + DIL_HEADS - 2
            o = [Chunk(1, IT1, j) for j in range(-1, OUT_CHUNKS + 2)]
            act.wait_ge(y_ready, IT0 + IT1 - 1)
            tanh_of(gate2[:], o[0], 1, tanh_g)
            split_hi(o[3])
            exps(0, h1)
            exps(1, h1 + 1)
            split_hi(o[4])
            take_t(0, h1)
            take_t(1, h1 + 1)
            split_hi(o[5])
            y_high(slice(2 * KT - 2, 2 * KT), IT0 + IT1)
            for k in range(6, 9):
                split_hi(o[k])
            act.preload_act_table(ACT.Sqrt)
            for q, b in enumerate(ACC_BANKS):
                act.wait_ge(*((acc_done, 3 + q + 1) if q < 3 else (mm_done, N_ALL)))
                act.activation(out_sq[:, q % 2 * 512:(q % 2 + 1) * 512], bank[b][:], ACT.Square,
                               accum_out=row_ms[:, q:q + 1]).then_inc(row_sq, 1)
                if q % 2:
                    t = q // 2
                    act.wait_ge(ms_ready, t + 1)
                    act.activation(nv[:, 0, t:t + 1], nv[:, 4, t:t + 1], ACT.Sqrt,
                                   bias=eps_t[:, 0:1]).then_inc(sd_ready, 1)
            t = NT - 1
            act.wait_ge(with_gains, 2 * t + 1)
            act.wait_ge(r_ready, 3 + t + 1)
            half = x_out[:, t * D_MODEL:t * D_MODEL + 512]
            act.activation(half, half, ACT.Copy, scale=nv[:, 3, t:t + 1]).then_inc(act_out, 1)
            act.wait_ge(act_out, 1)
            send(act, t, 0)

        @block.vector
        def _(dve):
            ch = Chain(dve, dve_chain)

            def split_lo(c):
                if not c.exists:
                    return
                dve.wait_ge(hi_ready, c.n + 1)
                dve.tensor_tensor(w_lo[:, c.slot, :], raw[:, c.slot, :], w_hi[:, c.slot, :].bitcast(F32),
                                  ALU.subtract).then_inc(lo_ready, 1)

            def inverse_root(norm):
                n = slice(0, cols(norm))
                dve.wait_ge(sd_ready, norm + 1)
                ch.mark(dve.tensor_scalar(nv[:, 1, n], Y_PS[:, n], 4 * EPS if norm == 1 else EPS, None, ALU.add))
                newton(n)

            def newton(n):
                b = ch.mark(dve.reciprocal(nv[:, 2, n], nv[:, 0, n]))
                ch.wait(b)
                b = ch.mark(dve.tensor_tensor(nv[:, 4, n], nv[:, 2, n], nv[:, 2, n], ALU.mult))
                ch.wait(b)
                b = ch.mark(dve.tensor_tensor(nv[:, 4, n], nv[:, 4, n], nv[:, 1, n], ALU.mult))
                ch.wait(b)
                b = ch.mark(dve.tensor_scalar(nv[:, 4, n], nv[:, 4, n], -0.5, 1.5, ALU.mult, ALU.add))
                ch.wait(b)
                dve.tensor_tensor(nv[:, 3, n], nv[:, 2, n], nv[:, 4, n], ALU.mult).then_inc(r_ready, 1)

            def scale_tile(src, k, gains, norm):
                g = (k // 4) * SEQ if norm == 1 else 0
                dve.scalar_tensor_tensor(out=sq[:, k, :], in0=src[:, k, :], scalar=par[:, gains + k:gains + k + 1],
                                         in1=Y_PS[:, g:g + SEQ], op0=ALU.mult, op1=ALU.mult).then_inc(scaled, 1)

            def norm_lo(dst_hi, dst_lo, k, base):
                dve.wait_ge(hnhi_ready, base + k + 1)
                dve.tensor_tensor(dst_lo[:, k, :], sq[:, k, :], dst_hi[:, k, :].bitcast(F32),
                                  ALU.subtract).then_inc(hn_ready, 1)

            def split_lo_part(c, part, parts, before):
                cs = slice(part * CF // parts, (part + 1) * CF // parts)
                final = part == parts - 1
                dve.wait_ge(*((hi_ready, c.n + 1) if final else (part_hi, before + part + 1)))
                dve.tensor_tensor(w_lo[:, c.slot, cs], raw[:, c.slot, cs], w_hi[:, c.slot, cs].bitcast(F32),
                                  ALU.subtract).then_inc(lo_ready if final else part_lo, 1)

            def gained_lo(k, at, n):
                dve.wait_ge(xghi_ready, n)
                dve.scalar_tensor_tensor(out=xg_lo[:, k, :], in0=xT[:, k, :], scalar=par[:, at + k:at + k + 1],
                                         in1=xg_hi[:, k, :].bitcast(F32), op0=ALU.mult,
                                         op1=ALU.subtract).then_inc(xg_ready, 1)

            def take_rb(norm):
                dve.wait_ge(rb_done, norm + 1)
                ch.wait(ch.mark(dve.tensor_copy(rb, Y_PS[:, 0:SEQ])))

            def rescale_bank(c, pb):
                dve.wait_ge(mm_done, c.n + 1)
                b = bank[pb][:].rearrange("p (a t) -> p a t", a=2)
                dve.tensor_tensor(b, b, rb.unsqueeze(1).to_broadcast([P, 2, SEQ]), ALU.mult).then_inc(rescaled, 1)

            def soft_scores(h, count, layer):
                dve.wait_ge(s_done, count + 1)
                dve.memset(pace[:, h:h + 1], 0.0)
                for t, cs in ((0, slice(0, P)), (1, slice(P, BLK))):
                    last = dve.tensor_tensor_reduce(s_m[:, h, cs], S_PS[:, cs], mask[layer][:, cs], 1.0, BIG,
                                                    ALU.add, ALU.min, neg_max[:, h, t:t + 1])
                last.then_inc(s_free, 1)

            def normalise(h, count):
                dve.wait_ge(exp_done, count + 1)
                ch.wait(ch.mark(dve.reciprocal(p_inv[:, h, :], p_sum[:, h, :])))
                for t, cs in ((0, slice(0, P)), (1, slice(P, BLK))):
                    last = dve.tensor_scalar(s_m[:, h, cs], s_m[:, h, cs], p_inv[:, h, t:t + 1], None, ALU.mult)
                last.then_inc(p_ready, 1)

            def take_q_lo(pb, count):
                dve.wait_ge(qkv_hi, count)
                dve.scalar_tensor_tensor(out=q1_lo, in0=bank[pb][:].rearrange("p (a t) -> p a t", a=2)[:, :, P:SEQ],
                                         scalar=-SCALE, in1=q1_hi[:].bitcast(F32), op0=ALU.mult,
                                         op1=ALU.subtract).then_inc(qk_ready, 1)

            def take_k_lo(pb, count):
                dve.wait_ge(qkv_hi, count)
                dve.tensor_tensor(k_lo, bank[pb][:].rearrange("p (a t) -> p a t", a=2), k_hi[:].bitcast(F32),
                                  ALU.subtract).then_inc(qk_ready, 1)

            def take_v_lo(pb, count):
                dve.wait_ge(qkv_hi, 3 * count)
                dve.tensor_tensor(v0_lo[:], bank[pb][:, 0:CW], v0_hi[:].bitcast(F32),
                                  ALU.subtract).then_inc(v_ready, 1)

            def take_t_lo(h, count):
                dve.wait_ge(t_ready, count + 1)
                dve.tensor_tensor(pT0_lo[:, h, :], T_PS[:, 0:SEQ], pT0_hi[:, h, :].bitcast(F32),
                                  ALU.subtract).then_inc(pt_ready, 1)

            def gate_z(i, pb):
                dve.wait_ge(tanh_z, i + 1)
                dve.scalar_tensor_tensor(out=z2[:], in0=z2[:], scalar=1.0, in1=bank[pb][:], op0=ALU.add,
                                         op1=ALU.mult).then_inc(dve_evac, 1)

            def tokens_by_dt(i):
                dve.wait_ge(xt_done, i + 1)
                dve.tensor_tensor(xdt.rearrange("p t (h c) -> p (t h) c", h=HEADS_PER_IT),
                                  S_PS[:].rearrange("p (a c) -> p a c", c=64),
                                  it_dt[:].rearrange("p t h -> p (t h)").unsqueeze(2)
                                  .to_broadcast([P, NT * HEADS_PER_IT, 64]), ALU.mult).then_inc(xdt_ready, 1)

            def skip_and_gate(i):
                dve.wait_ge(yd_done, i + 1)
                for t in range(2):
                    m = ch.mark(dve.scalar_tensor_tensor(
                        out=xs[:, t, :], in0=xs[:, t, :], scalar=it_par[:, 2 * (CONV + 1) + t:2 * (CONV + 1) + t + 1],
                        in1=Y_PS[:, t * SEQ:(t + 1) * SEQ], op0=ALU.mult, op1=ALU.add))
                ch.wait(m)
                dve.tensor_tensor(ssd_u[:, bass.ds(i * 2, 2), :], xs[:], z2[:].rearrange("p (a t) -> p a t", a=2),
                                  ALU.mult).then_inc(u_ready, 1)

            def gate_of(count):
                dve.wait_ge(tanh_g, count)
                dve.scalar_tensor_tensor(out=gate2[:], in0=gate2[:], scalar=1.0, in1=bank[1][:], op0=ALU.add,
                                         op1=ALU.mult).then_inc(dve_evac, 1)

            def gated(heads):
                dve.wait_ge(o_done, heads + 2)
                dve.scalar_tensor_tensor(out=gate2[:], in0=O_PS[:], scalar=0.5, in1=gate2[:], op0=ALU.mult,
                                         op1=ALU.mult).then_inc(yf_ready, 1)

            def y_low(tile, count):
                dve.wait_ge(yhi_ready, count)
                dve.tensor_tensor(y_lo[:, tile, :], gate2[:].rearrange("p (a t) -> p a t", a=2),
                                  y_hi[:, tile, :].bitcast(F32), ALU.subtract).then_inc(y_ready, 1)

            def conv_taps(n, pb, taps):
                dve.wait_ge(tap_bias, n)
                marks = [None, None]
                for k in range(CONV - 1):
                    shift = CONV - 1 - k
                    for t in range(2):
                        o = (CONV + 1) * t
                        if k:
                            ch.wait(marks[t])
                        last = dve.scalar_tensor_tensor(
                            out=conv[:, t, shift:], in0=bank[pb][:, t * SEQ:(t + 1) * SEQ - shift],
                            scalar=taps[:, o + k:o + k + 1], in1=conv[:, t, shift:], op0=ALU.mult, op1=ALU.add)
                        if k < CONV - 2:
                            marks[t] = ch.mark(last)
                last.then_inc(dve_evac, 1)

            def conv_silu(n, dst):
                dve.wait_ge(conv_tanh, n)
                dve.scalar_tensor_tensor(out=dst, in0=dst, scalar=1.0, in1=conv[:], op0=ALU.add,
                                         op1=ALU.mult).then_inc(xs_ready, 1)

            def sub(h, i):
                if not (isinstance(i, int) and i * HEADS_PER_IT + h < 2):
                    dve.wait_ge(m_ready, i * HEADS_PER_IT + (h - 1))
                dve.wait_ge(cum_done, i * HEADS_PER_IT + (h + 1))
                three = CUM[h % 2][:, 0:BLK].rearrange("p (b l) -> p b l", b=3)
                ch.wait(ch.mark(dve.tensor_tensor(decay[:, h % 2, :].rearrange("p (b l) -> p b l", b=3), three,
                                                  it_c[:, h, :].unsqueeze(2).to_broadcast([P, 3, P]),
                                                  ALU.subtract)))
                dve.tensor_scalar(decay[:, h % 2, :], decay[:, h % 2, :], 0.0, None,
                                  ALU.min).then_inc(sub_done, 1)

            def weigh(h, i):
                dve.wait_ge(dec_ready, i * HEADS_PER_IT + (h + 1))
                dve.tensor_tensor(m_t[:, h, :], decay[:, h % 2, :], g_flat[:, bass.ds(i * BLK, BLK)],
                                  ALU.mult).then_inc(m_ready, 1)

            def stage(i):
                if not (isinstance(i, int) and i == 0):
                    dve.wait_ge(cum_done, i * HEADS_PER_IT)
                hs = bass.ds(i * HEADS_PER_IT, HEADS_PER_IT)
                dve.tensor_copy(it_par[:], par[:, bass.ds(i * CPAR + (P_CONV + 2 * CPAR), CPAR)])
                dve.tensor_copy(it_c[:], cblk[:, hs, :])
                dve.tensor_copy(it_dt[:], dt[:, :, hs])
                dve.tensor_copy(it_ac[:], ac_hl[:].bitcast(F32).rearrange("p a (c h) -> p (a c) h", c=NT)
                                [:, :, hs]).then_inc(staged, 1)
                dve.wait_ge(staged, i + 1)

            def first_iteration():
                q, cc, k, x, v, z, g, x1, z1 = (Chunk(0, 0, j) for j in range(-1, PER0 + 2))
                split_lo_part(q, 0, 2, 3)
                split_lo_part(q, 1, 2, 3)
                inverse_root(0)
                take_rb(0)
                rescale_bank(Chunk(0, 0, FIRST_B), 0)
                for n in range(KT // 2):
                    scale_tile(xT, n, P_EVEN, 0)
                dve.wait_ge(taps_halved, 1)
                conv_taps(1, 0, par[:, P_CONV:])
                dve.wait_ge(dt_flipped, 1)
                arg, mag, e, s = (sp[:, n, :] for n in range(4))
                for t in range(NT):
                    hs = slice(t * SSD_HEADS, (t + 1) * SSD_HEADS)
                    m = ch.mark(dve.scalar_tensor_tensor(out=arg[:, hs], in0=D_PS[:, DT0 + hs.start:DT0 + hs.stop],
                                                         scalar=nv[:, 3, t:t + 1],
                                                         in1=par[:, P_DTB + hs.start:P_DTB + hs.stop],
                                                         op0=ALU.mult, op1=ALU.add))
                ch.wait(m)
                dve.scalar_tensor_tensor(out=mag, in0=arg, scalar=-1.0, in1=arg, op0=ALU.mult,
                                         op1=ALU.max).then_inc(dt_abs, 1)
                scale_tile(xT, KT // 2, P_EVEN, 0)
                dve.wait_ge(dt_exp, 1)
                ch.wait(ch.mark(dve.tensor_scalar(s, e, 2.0, None, ALU.add)))
                dve.reciprocal(s, s).then_inc(rec_ready, 1)
                rescale_bank(q, 1)
                conv_silu(1, b_s[:])
                dve.wait_ge(lo_ready, cc.n + 1)
                split_lo(k)
                take_q_lo(1, 1)
                scale_tile(xT, KT // 2 + 1, P_EVEN, 0)
                rescale_bank(cc, 0)
                scale_tile(xT, KT - 2, P_EVEN, 0)
                split_lo(x)
                conv_taps(2, 0, par[:, P_CONV + CPAR:])
                scale_tile(xT, KT - 1, P_EVEN, 0)
                conv_silu(2, c_s[:])
                rescale_bank(k, 1)
                prepare_cum()
                stage(0)
                take_k_lo(1, 2)
                split_lo(v)
                prepare_gm()
                sub(0, 0)
                sub(1, 0)
                dve.wait_ge(hn_ready, KT)
                split_lo(z)
                conv_taps(3, 0, it_par)
                weigh(0, 0)
                weigh(1, 0)
                sub(2, 0)
                conv_silu(3, xs[:])
                split_lo(g)
                take_v_lo(1, 1)
                sub(3, 0)
                weigh(2, 0)
                tokens_by_dt(0)
                weigh(3, 0)
                split_lo(x1)
                gate_z(0, 0)
                skip_and_gate(0)
                split_lo(z1)

            def layer0(i):
                heads = (i - 1) * 2
                c = [Chunk(0, i, j) for j in range(PER0 + 2)]
                gate_of(i)
                stage(i)
                soft_scores(0, heads, 0)
                split_lo(c[X + 2])
                normalise(0, heads)
                soft_scores(1, heads + 1, 0)
                conv_taps(i + 3, 0, it_par)
                take_t_lo(0, heads)
                normalise(1, heads + 1)
                sub(0, i)
                conv_silu(i + 3, xs[:])
                split_lo(c[Z + 2])
                sub(1, i)
                weigh(0, i)
                gate_z(i, 1)
                take_t_lo(1, heads + 1)
                tokens_by_dt(i)
                weigh(1, i)
                sub(2, i)
                split_lo(c[Q0 + 2])
                gated(heads)
                sub(3, i)
                weigh(2, i)
                take_q_lo(0, i * 3 + 1)
                split_lo(c[K0 + 2])
                weigh(3, i)
                y_low(bass.ds(i * 2 + (KT - 2), 2), i)
                take_k_lo(1, i * 3 + 2)
                split_lo(c[V0 + 2])
                skip_and_gate(i)
                take_v_lo(0, i + 1)
                split_lo(c[G0 + 2])

            def layer1(i, first):
                heads = (i - 1) * 2 + MOBA_HEADS
                c = [Chunk(1, i, j) for j in range(PER1 + 2)]
                if not first:
                    gate_of(i + IT0)
                    soft_scores(0, heads, 1)
                split_lo(c[Q1 + 2])
                if first:
                    inverse_root(2)
                    take_rb(2)
                    rescale_bank(c[Q1], 0)
                    for k in range(KT - 2):
                        scale_tile(xT, k, P_ODD, 2)
                        if k == 1:
                            take_q_lo(0, 3 * IT0 + 1)
                else:
                    normalise(0, heads)
                    soft_scores(1, heads + 1, 1)
                    normalise(1, heads + 1)
                if not first:
                    take_q_lo(0, i * 3 + (3 * IT0 + 1))
                    take_t_lo(0, heads)
                if first:
                    rescale_bank(c[K1], 1)
                split_lo(c[K1 + 2])
                take_k_lo(1, i * 3 + (3 * IT0 + 2))
                if first:
                    for k in range(KT - 2, KT):
                        scale_tile(xT, k, P_ODD, 2)
                else:
                    take_t_lo(1, heads + 1)
                if first:
                    dve.wait_ge(mm_done, c[V1].n + 1)
                    for t in range(NT):
                        b = bank[0][:, t * CW:(t + 1) * CW]
                        last = dve.tensor_scalar(b, b, nv[:, 3, t:t + 1], None, ALU.mult)
                    last.then_inc(rescaled, 1)
                split_lo(c[V1 + 2])
                if not first:
                    gated(heads)
                take_v_lo(0, i + (IT0 + 1))
                split_lo(c[G1 + 2])
                if not first:
                    y_low(bass.ds(i * 2 - 2, 2), i + IT0)

            def prepare_cum():
                dve.wait_ge(cs_done, 1)
                H = SSD_HEADS
                ch.wait(ch.mark(dve.tensor_copy(cum_s[:], D_PS[:, CS0:CS0 + NH])))
                dve.tensor_copy(cblk[:, :, 0:1], cum_s[:, 0:H].unsqueeze(2))
                dve.tensor_tensor(cblk[:, :, 1:2], cum_s[:, 0:H].unsqueeze(2),
                                  D_PS[:, CS0 + NH:CS0 + NH + H].unsqueeze(2), ALU.subtract)
                ch.wait(ch.mark(dve.tensor_copy(cblk[:, :, 2:3], cum_s[:, H:2 * H].unsqueeze(2))))

            def prepare_gm():
                dve.wait_ge(tri_in, 16)
                dve.wait_ge(bc_done, 1)
                for g, ps, emptied in ((0, S_PS, s_free), (1, T_PS, pt_ready)):
                    dve.tensor_tensor(g_m[:, g * (IT0 // SSD_GROUPS), :], ps[:, 0:BLK], causal3,
                                      ALU.mult).then_inc(emptied, 1)
                dve.wait_ge(pt_ready, 1)

            def add_residual():
                def low(k):
                    for d in range(2):
                        gained_lo(2 * ACC_BANKS[k] + d, P_ODD, KT + 2 * k + d + 1)

                for k, b in enumerate(ACC_BANKS):
                    if k < 3:
                        dve.wait_ge(acc_done, k + 1)
                    else:
                        dve.wait_ge(mm_done, N_L1)
                    x2 = xT[:, 2 * b:2 * b + 2, :]
                    dve.tensor_tensor(x2, bank[b][:].rearrange("p (a t) -> p a t", a=2), x2,
                                      ALU.add).then_inc(x_ready, 1)
                    if k:
                        low(k - 1)
                dve.wait_ge(x_ready, 4)
                low(3)

            dve.memset(eps_t[:, 0:1], EPS)
            dve.memset(eps_t[:, 1:2], 4 * EPS).then_inc(eps_ready, 1)
            dve.wait_ge(eps_ready, 1)
            for half in range(2):
                for k in range(half * (KT // 2), (half + 1) * (KT // 2)):
                    gained_lo(k, P_EVEN, k + 1)
                for part in (2 * half, 2 * half + 1):
                    split_lo_part(Chunk(0, 0, FIRST_B), part, 4, 0)
            dve.wait_ge(squared, 2)
            for n in (4, 2):
                ch.wait(ch.mark(dve.tensor_tensor(sq[:, 0:n, :], sq[:, 0:n, :], sq[:, n:2 * n, :], ALU.add)))
            dve.tensor_tensor(sq[:, 0, :], sq[:, 0, :], sq[:, 1, :], ALU.add).then_inc(sums_ready, 1)
            first_iteration()
            dve.wait_ge(gm_copied, 1)
            base = ch.base + ch.k
            with dve.Fori(1, IT0) as i:
                ch.restart(i * MARKS0 + (base - MARKS0))
                layer0(i)
                assert ch.k == MARKS0, ch.k
            ch.restart(base + (IT0 - 1) * MARKS0)

            h0 = MOBA_HEADS - 2
            o = [Chunk(0, IT0, j) for j in range(-1, OUT_CHUNKS + 2)]
            gate_of(IT0)
            soft_scores(0, h0, 0)
            soft_scores(1, h0 + 1, 0)
            split_lo(o[3])
            normalise(0, h0)
            normalise(1, h0 + 1)
            inverse_root(1)
            take_t_lo(0, h0)
            split_lo(o[4])
            dve.wait_ge(rb_done, 2)
            for k in range(5):
                if k < 4:
                    scale_tile(ssd_u, k, P_SSD, 1)
                if k:
                    norm_lo(y_hi, y_lo, k - 1, KT)
            take_t_lo(1, h0 + 1)
            for k in range(4, KT + 1):
                if k < KT:
                    scale_tile(ssd_u, k, P_SSD, 1)
                if k > 4:
                    norm_lo(y_hi, y_lo, k - 1, KT)
            split_lo(o[5])
            gated(h0)
            y_low(slice(2 * KT - 2, 2 * KT), IT0)
            for k in range(6, 11):
                split_lo(o[k])
            add_residual()
            layer1(0, True)
            base = ch.base + ch.k
            with dve.Fori(1, IT1) as i:
                ch.restart(i * MARKS1 + (base - MARKS1))
                layer1(i, False)
                assert ch.k == MARKS1, ch.k
            ch.restart(base + (IT1 - 1) * MARKS1)
            h1 = MOBA_HEADS + DIL_HEADS - 2
            o = [Chunk(1, IT1, j) for j in range(-1, OUT_CHUNKS + 2)]
            gate_of(IT0 + IT1)
            soft_scores(0, h1, 1)
            soft_scores(1, h1 + 1, 1)
            split_lo(o[3])
            normalise(0, h1)
            normalise(1, h1 + 1)
            take_t_lo(0, h1)
            split_lo(o[4])
            take_t_lo(1, h1 + 1)
            split_lo(o[5])
            gated(h1)
            y_low(slice(2 * KT - 2, 2 * KT), IT0 + IT1)
            for k in range(6, 9):
                split_lo(o[k])
            dve.wait_ge(gains_in, 16)
            def by_gains(q):
                h = q % 2
                dve.tensor_tensor(x_out[:, q * 512:(q + 1) * 512], bank[ACC_BANKS[q]][:],
                                  gains[:, h * 512:(h + 1) * 512], ALU.mult).then_inc(with_gains, 1)

            for t in range(NT):
                n, q = slice(t, t + 1), 2 * t
                dve.wait_ge(row_sq, q + 1)
                by_gains(q)
                dve.wait_ge(row_sq, q + 2)
                dve.tensor_scalar(nv[:, 4, n], row_ms[:, q:q + 1], row_ms[:, q + 1:q + 2], 1.0 / D_MODEL,
                                  ALU.add, ALU.mult).then_inc(ms_ready, 1)
                by_gains(q + 1)
                dve.wait_ge(sd_ready, 3 + t + 1)
                ch.mark(dve.tensor_scalar(nv[:, 1, n], nv[:, 4, n], EPS, None, ALU.add))
                newton(n)
                dve.wait_ge(r_ready, 3 + t + 1)
                half = x_out[:, (q + 1) * 512:(q + 2) * 512]
                dve.tensor_scalar(half, half, nv[:, 3, n], None, ALU.mult).then_inc(dve_out, 1)

        @block.gpsimd
        def _(pool):
            ch = Chain(pool, pool_chain)

            def in_turn(ins):
                ch.wait(ch.mark(ins))

            def squares(dst, src):
                in_turn(pool.tensor_tensor(dst, src, src, ALU.mult))

            def add(dst, a, b):
                return pool.tensor_tensor(dst, a, b, ALU.add)

            def norm_lo(base, ks=range(KT)):
                for k in ks:
                    pool.wait_ge(hnhi_ready, base + k + 1)
                    pool.tensor_tensor(hn_lo[:, k, :], sq[:, k, :], hn_hi[:, k, :].bitcast(F32),
                                       ALU.subtract).then_inc(hn_ready, 1)

            pool.memset(xs[:, 0, :], 0.0).then_inc(zeroed, 1)
            half = KT // 2
            pool.wait_ge(x_in_a, 16)
            for ks, s in ((slice(0, half), x_in_a), (slice(half, KT), x_in_b)):
                pool.wait_ge(s, 16)
                pool.tensor_tensor(sq[:, ks, :], xT[:, ks, :], xT[:, ks, :], ALU.mult).then_inc(squared, 1)
            pool.wait_ge(wd_hi_s, 1)
            pool.tensor_tensor(wd_lo[:], wd[:].rearrange("p (k h) -> p k h", k=KT), wd_hi[:].bitcast(F32),
                               ALU.subtract).then_inc(wd_ready, 1)
            cp = par[:, P_CONV:P_CONV + (IT0 + 2) * CPAR].rearrange("p (n c) -> p n c", c=CPAR)
            cp = cp[:, :, 0:2 * (CONV + 1)]
            pool.wait_ge(par_in_s, 16)
            pool.tensor_scalar(cp, cp, 0.5, None, ALU.mult).then_inc(taps_halved, 1)
            def split_lo(c):
                pool.wait_ge(hi_ready, c.n + 1)
                pool.wait_ge(lo_ready, c.n)
                pool.tensor_tensor(w_lo[:, c.slot, :], raw[:, c.slot, :], w_hi[:, c.slot, :].bitcast(F32),
                                   ALU.subtract).then_inc(lo_ready, 1)

            split_lo(Chunk(0, 0, FIRST_C))
            norm_lo(0, range(KT // 2))

            v, e, s, z, zz, acc = (sp[:, k, :] for k in (0, 2, 3, 4, 5, 6))
            pool.wait_ge(rec_ready, 1)
            in_turn(pool.tensor_tensor(z, e, s, ALU.mult))
            in_turn(pool.tensor_tensor(zz, z, z, ALU.mult))
            in_turn(pool.tensor_scalar(acc, zz, 1.0 / 17, None, ALU.mult))
            for odd in (15, 13, 11, 9, 7, 5, 3):
                in_turn(pool.tensor_scalar(acc, acc, 1.0 / odd, None, ALU.add))
                in_turn(pool.tensor_tensor(acc, acc, zz, ALU.mult))
            in_turn(pool.tensor_scalar(acc, acc, 1.0, 2.0, ALU.add, ALU.mult))
            in_turn(pool.tensor_tensor(acc, acc, z, ALU.mult))
            in_turn(pool.tensor_scalar(v, v, 0.0, None, ALU.max))
            d = dt[:].rearrange("p t h -> p (t h)")
            in_turn(pool.tensor_tensor(d, acc, v, ALU.add))
            pool.wait_ge(a_ready, 1)
            in_turn(pool.tensor_tensor(ac[:], d, a_exp[:], ALU.mult))
            in_turn(pool.tensor_scalar(ac[:], ac[:], -1.0, None, ALU.mult))
            in_turn(pool.tensor_scalar(ac_hl[:, 0, :], ac[:], 1.0, None, ALU.mult))
            pool.tensor_tensor(ac_hl[:, 1, :], ac[:], ac_hl[:, 0, :].bitcast(F32),
                               ALU.subtract).then_inc(ac_ready, 1)
            norm_lo(0, range(KT // 2, KT))
            per = IT0 // SSD_GROUPS
            pool.wait_ge(s_free, 1)
            pool.wait_ge(pt_ready, 1)
            for i in range(IT0):
                if i % per:
                    last = pool.tensor_copy(g_m[:, i, :], g_m[:, i - i % per, :])
            last.then_inc(gm_copied, 1)

            for i in range(IT0):
                g, a = i // per, i % per
                acc = g_sum[:, g, :]
                pool.wait_ge(u_ready, i + 1)
                squares(u_sq[:], ssd_u[:, 2 * i:2 * i + 2, :])
                both = u_sq[:, 0, :] if a else acc
                in_turn(add(both, u_sq[:, 0, :], u_sq[:, 1, :]))
                if i == IT0 - 1:
                    add(acc, acc, both).then_inc(sums_ready, 1)
                elif a:
                    in_turn(add(acc, acc, both))

            a2 = sq[:, 2 * ACC_BANKS[0]:2 * ACC_BANKS[0] + 2, :]
            for k in range(1, 4):
                b = ACC_BANKS[k]
                pool.wait_ge(bank_sq, k + 1)
                in_turn(add(a2, a2, sq[:, 2 * b:2 * b + 2, :]))
            add(a2[:, 0, :], a2[:, 0, :], a2[:, 1, :]).then_inc(sums_ready, 1)
            norm_lo(2 * KT)

            pool.wait_ge(r_ready, 3 + 1)
            half = x_out[:, 0:512]
            pool.tensor_scalar(half, half, nv[:, 3, 0:1], None, ALU.mult).then_inc(pool_out, 1)


def constants():
    import numpy as np
    con = np.zeros((P, N_CONST), np.float32)
    con[:, C_ID:C_ID + P] = np.eye(P)
    lower = np.triu(np.ones((P, P)))
    con[:, C_TRI:C_TRI + P] = con[:, C_TRI2:C_TRI2 + P] = lower
    con[:, C_ONE:C_ONE + P] = 1.0
    i, j = np.arange(SEQ)[:, None], np.arange(SEQ)[None, :]
    causal = (j <= i).astype(np.float64)
    count = sum(causal * ((i - j) % r == 0) * ((i - j) <= w) for w, r in ((128, 1), (512, 4), (2048, 16)))
    for at, times in ((C_M0, causal), (C_M1, count)):
        m = np.where(times > 0, -np.log(np.maximum(times, 1)), BIG)
        con[:, at:at + P] = m[0:P, 0:P]
        con[:, at + P:at + BLK] = m[P:SEQ, :]
    con[:, C_INV], con[:, C_INV + 1] = 1.0 / D_MODEL, SSD_GROUPS / SSD_INNER
    return con


def kernel(**inputs):
    import numpy as np
    import concourse.bacc as bacc
    from concourse.bass_utils import run_bass_kernel_spmd as run

    a = {k: np.asarray(v) for k, v in inputs.items()}
    w_in, w_out = a["even_w_in"][0], a["even_w_out"][0]
    v_in, v_out = a["odd_w_in"][0], a["odd_w_out"][0]

    def in_chunk(w, c0):
        return w[:, c0:c0 + CW].reshape(KT, P, CW).transpose(1, 0, 2).reshape(P, CF)

    def out_chunk(w, r0):
        return w[r0:r0 + CW].reshape(2, P, D_MODEL).transpose(1, 0, 2).reshape(P, CF)

    z0, x0 = 0, SSD_INNER
    b0 = x0 + SSD_INNER
    c0 = b0 + SSD_GROUPS * SSD_STATE
    dt0 = c0 + SSD_GROUPS * SSD_STATE
    q0 = dt0 + SSD_HEADS
    inner = MOBA_HEADS * HD
    w_all = np.empty((P, N_ALL, CF), np.float32)
    chunks = [in_chunk(w_in, s) for s in (b0, q0, c0, q0 + inner, x0, q0 + 2 * inner, z0, q0 + 3 * inner)]
    for i in range(1, IT0):
        chunks += [in_chunk(w_in, s + i * CW) for s in (x0, z0, q0, q0 + inner, q0 + 2 * inner, q0 + 3 * inner)]
    chunks += [out_chunk(w_out, t * P) for t in OUT_ORDER0]
    for i in range(IT1):
        chunks += [in_chunk(v_in, s * DIL_HEADS * HD + i * CW) for s in range(4)]
    chunks += [out_chunk(v_out, j * CW) for j in range(OUT_CHUNKS)]
    for n, chunk in enumerate(chunks):
        w_all[:, n] = chunk
    w_dt = np.ascontiguousarray(w_in[:, dt0:q0].reshape(KT, P, SSD_HEADS).transpose(1, 0, 2).reshape(P, -1))

    def by_tile(v):
        return v.reshape(-1, P).T

    par = np.zeros((P, N_PAR), np.float32)
    taps = np.concatenate([a["ssd_conv_w"][0], a["ssd_conv_b"][0][None]])
    skip = np.repeat(a["ssd_d"][0], SSD_INNER // SSD_HEADS)
    for n, ch0 in enumerate([SSD_INNER, SSD_INNER + CW] + [i * CW for i in range(IT0)]):
        at = P_CONV + n * CPAR
        par[:, at:at + 2 * (CONV + 1)] = taps[:, ch0:ch0 + CW].reshape(CONV + 1, 2, P).transpose(2, 1, 0).reshape(P, -1)
        if n >= 2:
            par[:, at + 2 * (CONV + 1):at + CPAR] = by_tile(skip[ch0:ch0 + CW])
    for at, v in ((P_EVEN, a["even_norm"][0]), (P_ODD, a["odd_norm"][0]), (P_SSD, a["ssd_norm"][0])):
        par[:, at:at + KT] = by_tile(v)
    par[:, P_DTB:P_DTB + NT * SSD_HEADS] = np.tile(a["ssd_dt_bias"][0], NT)
    par[:, P_ALOG:P_ALOG + NT * SSD_HEADS] = np.tile(a["ssd_a_log"][0], NT)
    x_in = np.ascontiguousarray(a["x"][0].T.reshape(KT, P, SEQ).transpose(1, 0, 2))

    nc = bacc.Bacc("TRN2", target_bir_lowering=False, num_devices=1)
    arrays = {"w_all": w_all, "w_dt": w_dt, "x_in": x_in, "par_in": par, "con_in": constants(),
              "gains_in": np.ascontiguousarray(np.broadcast_to(a["final_norm"], (P, D_MODEL)))}
    aps = [nc.dram_tensor(n, v.shape, F32, kind="ExternalInput").ap() for n, v in arrays.items()]
    out = nc.dram_tensor("out", (SEQ, D_MODEL), F32, kind="ExternalOutput").ap()
    build(nc, *aps, out)
    r = run(nc, [arrays], core_ids=[0])
    return r.results[0]["out"][None]
```
